# Optimizing a Trainium2 kernel written in Bass

```python
import math
import jax, jax.numpy as jnp
from jax import lax
import numpy as np

D_MODEL = 1024
BATCH = 1
SEQ = 1024
DEPTH = 2

GRID_W = 64
CTX_LEN = 256
N_MIXERS = 3
HEAD_DIM = 64
ROT_FREQS = HEAD_DIM // 4
ROPE_THETA = 10000.0
Q_BLOCK = 128
DIFF_HEADS = D_MODEL // (2 * HEAD_DIM)
DIFF_V_DIM = 2 * HEAD_DIM
SWA_Q_HEADS = D_MODEL // HEAD_DIM
SWA_KV_HEADS = 4
SWA_GROUP = SWA_Q_HEADS // SWA_KV_HEADS
WINDOW = 128
FOURIER_GROUPS = 4
FOURIER_GROUP_DIM = D_MODEL // FOURIER_GROUPS
N_GROUPS = 4
EXPERTS_PER_GROUP = 8
N_EXPERTS = N_GROUPS * EXPERTS_PER_GROUP
TOP_K = 2
D_EXPERT = 512
MOE_BLOCK = 128
EPS = 1e-6
NEG_INF = -1e30

kernel_name = 'hybrid_diffusion_trunk_diffattn_swa_fnet_hmoe'

def _rmsnorm(x, g):
    x32 = x.astype(jnp.float32)
    y = x32 * lax.rsqrt(jnp.mean(x32 * x32, axis=-1, keepdims=True) + EPS)
    return (y * g.astype(jnp.float32)).astype(x.dtype)

def _modulate(h, shift, scale):
    return h * (1 + scale) + shift

def _rope_tables(rows):
    row = jnp.repeat(jnp.arange(rows, dtype=jnp.float32), GRID_W)
    col = jnp.tile(jnp.arange(GRID_W, dtype=jnp.float32), rows)
    inv = ROPE_THETA ** (-jnp.arange(ROT_FREQS, dtype=jnp.float32) / ROT_FREQS)
    ang = jnp.stack([row[:, None] * inv, col[:, None] * inv], axis=1)
    return jnp.cos(ang), jnp.sin(ang)

def _apply_rope(x, cs, sn):
    shp = x.shape
    xr = x.reshape(shp[0], shp[1], -1, 2, 2, ROT_FREQS).astype(jnp.float32)
    x1, x2 = xr[..., 0, :], xr[..., 1, :]
    c, s = cs[None, :, None], sn[None, :, None]
    out = jnp.stack([x1 * c - x2 * s, x2 * c + x1 * s], axis=-2)
    return out.reshape(shp).astype(x.dtype)

def _diff_attention(h, hc, wqkv, wo, q_g, k_g, lq1, lk1, lq2, lk2, sub_g, lam_init, cs, sn, need_ctx):
    def project(u):
        b, n, _ = u.shape
        q, k, v = jnp.split(u @ wqkv, 3, axis=-1)
        q = _rmsnorm(q.reshape(b, n, DIFF_HEADS, 2, HEAD_DIM), q_g)
        k = _rmsnorm(k.reshape(b, n, DIFF_HEADS, 2, HEAD_DIM), k_g)
        return q, k, v.reshape(b, n, DIFF_HEADS, DIFF_V_DIM)

    q, k, v = project(h)
    q, k = _apply_rope(q, cs, sn), _apply_rope(k, cs, sn)
    qc, kc, vc = project(hc)
    f32 = jnp.float32
    lam = (jnp.exp(jnp.sum(lq1.astype(f32) * lk1.astype(f32)))
           - jnp.exp(jnp.sum(lq2.astype(f32) * lk2.astype(f32))) + lam_init)
    scale = HEAD_DIM ** -0.5

    def attend(qb, kk, vv):
        s = jnp.einsum('bqhmd,bkhmd->bhmqk', qb, kk).astype(f32) * scale
        p = jax.nn.softmax(s, axis=-1)
        a = p[:, :, 0] - lam * p[:, :, 1]
        return jnp.einsum('bhqk,bkhe->bqhe', a.astype(vv.dtype), vv)

    def finish(o):
        o = _rmsnorm(o, sub_g) * (1 - lam_init)
        return o.reshape(o.shape[0], o.shape[1], -1) @ wo

    b, n = h.shape[:2]
    nblk = n // Q_BLOCK
    k_all = jnp.concatenate([k, kc], axis=1)
    v_all = jnp.concatenate([v, vc], axis=1)
    qb = q.reshape(b, nblk, Q_BLOCK, DIFF_HEADS, 2, HEAD_DIM).swapaxes(0, 1)
    o = lax.map(lambda blk: attend(blk, k_all, v_all), qb)
    o = o.swapaxes(0, 1).reshape(b, n, DIFF_HEADS, DIFF_V_DIM)
    y = finish(o)
    yc = finish(attend(qc, kc, vc)) if need_ctx else None
    return y, yc

def _swa_sink_attention(h, hc, wqkv, wo, q_g, k_g, sink, cs, sn, need_ctx):
    nq, nk = SWA_Q_HEADS * HEAD_DIM, SWA_KV_HEADS * HEAD_DIM

    def project(u):
        b, n, _ = u.shape
        qkv = u @ wqkv
        q = qkv[..., :nq].reshape(b, n, SWA_KV_HEADS, SWA_GROUP, HEAD_DIM)
        k = qkv[..., nq:nq + nk].reshape(b, n, SWA_KV_HEADS, HEAD_DIM)
        v = qkv[..., nq + nk:].reshape(b, n, SWA_KV_HEADS, HEAD_DIM)
        return _rmsnorm(q, q_g), _rmsnorm(k, k_g), v

    q, k, v = project(h)
    q, k = _apply_rope(q, cs, sn), _apply_rope(k, cs, sn)
    qc, kc, vc = project(hc)
    f32 = jnp.float32
    scale = HEAD_DIM ** -0.5
    sink_l = sink.astype(f32).reshape(SWA_KV_HEADS, SWA_GROUP)[None, :, :, None, None]

    def sink_softmax(s):
        sk = jnp.broadcast_to(sink_l, s.shape[:-1] + (1,))
        return jax.nn.softmax(jnp.concatenate([s, sk], axis=-1), axis=-1)[..., :-1]

    b, n = h.shape[:2]
    nblk = n // Q_BLOCK
    span = Q_BLOCK + 2 * WINDOW
    pad = ((0, 0), (WINDOW, WINDOW), (0, 0), (0, 0))
    kp, vp = jnp.pad(k, pad), jnp.pad(v, pad)
    rel = jnp.arange(span)[None, :] - WINDOW - jnp.arange(Q_BLOCK)[:, None]
    band = jnp.abs(rel) <= WINDOW

    def block(bi):
        start = bi * Q_BLOCK
        qb = lax.dynamic_slice_in_dim(q, start, Q_BLOCK, axis=1)
        kb = lax.dynamic_slice_in_dim(kp, start, span, axis=1)
        vb = lax.dynamic_slice_in_dim(vp, start, span, axis=1)
        kpos = start - WINDOW + jnp.arange(span)
        valid = band & ((kpos >= 0) & (kpos < n))[None, :]
        s_loc = jnp.einsum('bqhgd,bkhd->bhgqk', qb, kb).astype(f32) * scale
        s_loc = jnp.where(valid, s_loc, NEG_INF)
        s_ctx = jnp.einsum('bqhgd,bkhd->bhgqk', qb, kc).astype(f32) * scale
        p = sink_softmax(jnp.concatenate([s_loc, s_ctx], axis=-1)).astype(v.dtype)
        return (jnp.einsum('bhgqk,bkhd->bqhgd', p[..., :span], vb)
                + jnp.einsum('bhgqk,bkhd->bqhgd', p[..., span:], vc))

    o = lax.map(block, jnp.arange(nblk))
    y = o.swapaxes(0, 1).reshape(b, n, nq) @ wo
    yc = None
    if need_ctx:
        s = jnp.einsum('bqhgd,bkhd->bhgqk', qc, kc).astype(f32) * scale
        p = sink_softmax(s).astype(vc.dtype)
        oc = jnp.einsum('bhgqk,bkhd->bqhgd', p, vc)
        yc = oc.reshape(oc.shape[0], oc.shape[1], nq) @ wo
    return y, yc

def _fourier_mix(h, hc, wo, need_ctx):
    def mix(u):
        b, n, _ = u.shape
        ug = u.astype(jnp.float32).reshape(b, n, FOURIER_GROUPS, FOURIER_GROUP_DIM)
        f = jnp.fft.fft2(ug, axes=(1, 3), norm='ortho').real
        return f.reshape(b, n, D_MODEL).astype(u.dtype) @ wo
    y = mix(h)
    yc = mix(hc) if need_ctx else None
    return y, yc

def _hier_moe(h, w_r1, b_r1, w_r2, b_r2, w13, w2):
    n_tok, d = h.shape
    f32 = jnp.float32
    rows = jnp.arange(n_tok)
    p_grp = jax.nn.softmax((h @ w_r1).astype(f32) + b_r1.astype(f32), axis=-1)
    grp = jnp.argmax(p_grp, axis=-1)
    pg = p_grp[rows, grp]
    logits2 = jnp.einsum('nd,gde->nge', h, w_r2).astype(f32) + b_r2.astype(f32)
    p_in = jax.nn.softmax(logits2[rows, grp], axis=-1)
    top_p, top_j = lax.top_k(p_in, TOP_K)
    top_p = top_p / jnp.sum(top_p, axis=-1, keepdims=True)
    expert = grp[:, None] * EXPERTS_PER_GROUP + top_j
    wts = pg[:, None] * top_p

    n_asg = n_tok * TOP_K
    e_flat = expert.reshape(-1)
    t_flat = jnp.repeat(rows, TOP_K)
    w_flat = wts.reshape(-1)
    order = jnp.argsort(e_flat)
    e_s, t_s, w_s = e_flat[order], t_flat[order], w_flat[order]
    counts = jnp.bincount(e_flat, length=N_EXPERTS)
    starts = jnp.cumsum(counts) - counts
    padded = ((counts + MOE_BLOCK - 1) // MOE_BLOCK) * MOE_BLOCK
    pend = jnp.cumsum(padded)
    pstarts = pend - padded
    dest = pstarts[e_s] + jnp.arange(n_asg) - starts[e_s]
    n_blocks = (n_asg + MOE_BLOCK - 1) // MOE_BLOCK + N_EXPERTS
    n_rows = n_blocks * MOE_BLOCK
    tok_buf = jnp.zeros((n_rows,), jnp.int32).at[dest].set(t_s.astype(jnp.int32))
    wt_buf = jnp.zeros((n_rows,), f32).at[dest].set(w_s)
    blk_exp = jnp.clip(jnp.searchsorted(pend, jnp.arange(n_blocks) * MOE_BLOCK, side='right'), 0, N_EXPERTS - 1)

    def expert_block(args):
        tok, e = args
        gu = h[tok] @ w13[e]
        g, u = jnp.split(gu, 2, axis=-1)
        return (jax.nn.silu(g) * u) @ w2[e]

    ys = lax.map(expert_block, (tok_buf.reshape(n_blocks, MOE_BLOCK), blk_exp))
    y = ys.reshape(n_rows, d) * wt_buf[:, None].astype(ys.dtype)
    return jnp.zeros_like(h).at[tok_buf].add(y)

def setup_inputs(seed: int = 0) -> dict:
    key = jax.random.key(seed)
    ks = iter(jax.random.split(key, 40))

    def nrm(shape, scale):
        return scale * jax.random.normal(next(ks), shape, jnp.float32)

    d = D_MODEL
    n_a = len(range(0, DEPTH, N_MIXERS))
    n_b = len(range(1, DEPTH, N_MIXERS))
    n_f = len(range(2, DEPTH, N_MIXERS))
    return {
        'x': nrm((BATCH, SEQ, d), 1.0),
        'c': nrm((BATCH, d), 1.0),
        'ctx': nrm((BATCH, CTX_LEN, d), 1.0),
        'c_ctx': nrm((d,), 1.0),
        'ada_w': nrm((DEPTH, d, 6 * d), 0.5 * d ** -0.5),
        'ada_b': nrm((DEPTH, 6 * d), 0.02),
        'norm1_g': 1.0 + nrm((DEPTH, d), 0.05),
        'norm2_g': 1.0 + nrm((DEPTH, d), 0.05),
        'a_wqkv': nrm((n_a, d, 3 * DIFF_HEADS * 2 * HEAD_DIM), d ** -0.5),
        'a_wo': nrm((n_a, DIFF_HEADS * DIFF_V_DIM, d), (DIFF_HEADS * DIFF_V_DIM) ** -0.5),
        'a_q_norm': 1.0 + nrm((n_a, HEAD_DIM), 0.05),
        'a_k_norm': 1.0 + nrm((n_a, HEAD_DIM), 0.05),
        'a_lambda_q1': nrm((n_a, HEAD_DIM), 0.1),
        'a_lambda_k1': nrm((n_a, HEAD_DIM), 0.1),
        'a_lambda_q2': nrm((n_a, HEAD_DIM), 0.1),
        'a_lambda_k2': nrm((n_a, HEAD_DIM), 0.1),
        'a_subln_g': 1.0 + nrm((n_a, DIFF_V_DIM), 0.05),
        'b_wqkv': nrm((n_b, d, (SWA_Q_HEADS + 2 * SWA_KV_HEADS) * HEAD_DIM), d ** -0.5),
        'b_wo': nrm((n_b, SWA_Q_HEADS * HEAD_DIM, d), (SWA_Q_HEADS * HEAD_DIM) ** -0.5),
        'b_q_norm': 1.0 + nrm((n_b, HEAD_DIM), 0.05),
        'b_k_norm': 1.0 + nrm((n_b, HEAD_DIM), 0.05),
        'b_sink': nrm((n_b, SWA_Q_HEADS), 0.5),
        'f_wo': nrm((n_f, d, d), d ** -0.5),
        'r_w1': nrm((DEPTH, d, N_GROUPS), d ** -0.5),
        'r_b1': nrm((DEPTH, N_GROUPS), 0.01),
        'r_w2': nrm((DEPTH, N_GROUPS, d, EXPERTS_PER_GROUP), d ** -0.5),
        'r_b2': nrm((DEPTH, N_GROUPS, EXPERTS_PER_GROUP), 0.01),
        'e_w13': nrm((DEPTH, N_EXPERTS, d, 2 * D_EXPERT), d ** -0.5),
        'e_w2': nrm((DEPTH, N_EXPERTS, D_EXPERT, d), D_EXPERT ** -0.5),
    }

def reference(x, c, ctx, c_ctx, ada_w, ada_b, norm1_g, norm2_g,
              a_wqkv, a_wo, a_q_norm, a_k_norm, a_lambda_q1, a_lambda_k1, a_lambda_q2, a_lambda_k2, a_subln_g,
              b_wqkv, b_wo, b_q_norm, b_k_norm, b_sink,
              f_wo,
              r_w1, r_b1, r_w2, r_b2, e_w13, e_w2):
    b, n, d = x.shape
    rows = n // GRID_W
    cs, sn = _rope_tables(rows)
    silu_c = jax.nn.silu(c)
    silu_cc = jax.nn.silu(c_ctx)
    for i in range(DEPTH):
        kind, j = i % N_MIXERS, i // N_MIXERS
        need_ctx = i < DEPTH - 1
        sh1, sc1, g1, sh2, sc2, g2 = [m[:, None, :] for m in jnp.split(silu_c @ ada_w[i] + ada_b[i], 6, axis=-1)]
        sh1c, sc1c, g1c, sh2c, sc2c, g2c = jnp.split(silu_cc @ ada_w[i] + ada_b[i], 6, axis=-1)
        h = _modulate(_rmsnorm(x, norm1_g[i]), sh1, sc1)
        hc = _modulate(_rmsnorm(ctx, norm1_g[i]), sh1c, sc1c)
        if kind == 0:
            lam_init = 0.8 - 0.6 * math.exp(-0.3 * i)
            y, yc = _diff_attention(h, hc, a_wqkv[j], a_wo[j], a_q_norm[j], a_k_norm[j],
                                    a_lambda_q1[j], a_lambda_k1[j], a_lambda_q2[j], a_lambda_k2[j],
                                    a_subln_g[j], lam_init, cs, sn, need_ctx)
        elif kind == 1:
            y, yc = _swa_sink_attention(h, hc, b_wqkv[j], b_wo[j], b_q_norm[j], b_k_norm[j], b_sink[j],
                                        cs, sn, need_ctx)
        else:
            y, yc = _fourier_mix(h, hc, f_wo[j], need_ctx)
        x = x + g1 * y
        h2 = _modulate(_rmsnorm(x, norm2_g[i]), sh2, sc2)
        if need_ctx:
            ctx = ctx + g1c * yc
            h2c = _modulate(_rmsnorm(ctx, norm2_g[i]), sh2c, sc2c)
            tokens = jnp.concatenate([h2.reshape(-1, d), h2c.reshape(-1, d)], axis=0)
        else:
            tokens = h2.reshape(-1, d)
        out = _hier_moe(tokens, r_w1[i], r_b1[i], r_w2[i], r_b2[i], e_w13[i], e_w2[i])
        x = x + g2 * out[:b * n].reshape(b, n, d)
        if need_ctx:
            ctx = ctx + g2c * out[b * n:].reshape(ctx.shape)
    return x


_drawn_inputs = setup_inputs


def setup_inputs(seed=0):
    import zlib

    import numpy as np

    out = dict(_drawn_inputs(seed))
    spreads = {}
    factors = {'norm1_g': 4.963,
     'a_q_norm': 8.0,
     'a_k_norm': 8.0,
     'a_lambda_q1': 4.972,
     'a_lambda_q2': 8.0,
     'a_lambda_k2': 4.891,
     'a_subln_g': 3.336,
     'b_q_norm': 8.0,
     'b_k_norm': 8.0,
     'b_sink': 8.0,
     'r_b1': 8.0,
     'r_b2': 8.0}
    for name, (base, spread) in spreads.items():
        noise = np.random.default_rng([zlib.crc32(name.encode()), seed]).standard_normal(out[name].shape)
        drawn = base * np.exp(spread * noise) if base else spread * noise
        out[name] = __import__('jax').numpy.asarray(drawn.astype(out[name].dtype))
    for name, factor in factors.items():
        out[name] = (out[name] * factor).astype(out[name].dtype)
    return out
```

```python
import math

import concourse.bass as bass
from concourse import mybir

F32 = mybir.dt.float32
BF16 = mybir.dt.bfloat16
I32 = mybir.dt.int32
ALU = mybir.AluOpType
ACT = mybir.ActivationFunctionType
AX = mybir.AxisListType.X

P = 128
D = 1024
KD = D // P
SEQ, CTX = 1024, 256
TX, TC = SEQ // P, CTX // P
TA = TX + TC
NTOK = SEQ + CTX
HALF = 512
HD = 64
EPS = 1e-6
SCALE = HD ** -0.5
LAM_INIT = 0.8 - 0.6 * math.exp(-0.3 * 0)
NG, EPG = 4, 8
NE = NG * EPG
DE = 512
BIG = 1e30
NB_MAX = [2 * NTOK // P + NE, 2 * SEQ // P + NE]
NB_MIN = [2 * NTOK // P, 2 * SEQ // P]
NBT = NB_MAX[0] + 1
EMPTY = 1 << 20
TILES = [TA, TX]

C_ID, C_TRI, C_IOTA, C_PREV, C_NEXT = 0, 128, 256, 384, 512
C_COS, C_SIN = 640, 640 + TA * HD
C_TOK = C_SIN + TA * HD
C_END = C_TOK + TA


def build(nc, x, c, ctx, c_ctx, ada_w, ada_b, norm1_g, norm2_g, a_wqkv, a_wo, a_q_norm, a_k_norm,
          a_lambda_q1, a_lambda_k1, a_lambda_q2, a_lambda_k2, a_subln_g, b_wqkv, b_wo, b_q_norm,
          b_k_norm, b_sink, r_w1, r_b1, r_w2, r_b2, e_w13, e_w2, consts, out):
    ds = bass.ds
    nc.disable_value_cache = True

    def dram(name, shape):
        return nc.dram_tensor(name, shape, F32, kind="Internal").ap()

    mod_d = dram("mod_d", [2, 2, 6 * D])
    qk_d = dram("qk_d", [16, P, NTOK])
    v_d = dram("v_d", [NTOK, 256])
    o_d = dram("o_d", [TA, P, D])
    xs_d = dram("xs_d", [NTOK, D])
    h2_d = dram("h2_d", [NTOK, D])
    y_d = dram("y_d", [2 * NTOK, D])

    def sb(name, shape, dt=F32):
        return nc.alloc_sbuf_tensor(name, shape, dt)

    cst = sb("cst", [P, C_END])
    ident = cst[:, C_ID:C_ID + P]
    tri = cst[:, C_TRI:C_TRI + P]
    iota = cst[:, C_IOTA:C_IOTA + P]
    tokrow = cst[:, C_TOK:C_TOK + TA]
    ones = sb("ones", [P, P])
    ident_h = sb("ident_h", [P, P], BF16)
    mask_h = sb("mask_h", [P, 2, P], BF16)
    neghalf = sb("neghalf", [P, TA * 2])
    gains = sb("gains", [P, 4, HD])
    subg = sb("subg", [P, 1])
    lamv = sb("lamv", [P, 4, HD])
    lamw = sb("lamw", [P, 2, HD])
    lams = sb("lams", [P, 4])
    neglam = sb("neglam", [P, 1])
    sinks = sb("sinks", [P, 16])
    negsink = sb("negsink", [P, 16])
    wrt = sb("wrt", [P, 2, KD, NG + NE])
    brt = sb("brt", [P, 2, NG + NE])
    colw = sb("colw", [P, 40])
    mod_a = sb("mod_a", [P, 2, KD])
    mod_b = sb("mod_b", [P, 2, KD])
    logits = sb("logits", [P, TA, NG + NE])
    wsel = sb("wsel", [P, 2, TA])
    rowtab = sb("rowtab", [P, NBT], I32)
    toktab = sb("toktab", [P, NBT], I32)
    exptab = sb("exptab", [P, NBT], I32)
    blkcount = sb("blkcount", [P, 2], I32)
    arena0 = nc.sbuf_base
    limit = nc.sbuf_usable_end

    class Arena:

        def __init__(self, tag, at=None):
            self.tag, self.at = tag, at or (arena0 + 63) // 64 * 64

        def __call__(self, name, shape, dt=F32):
            size = (4 if dt != BF16 else 2) * math.prod(shape[1:])
            t = nc.alloc_sbuf_tensor_at(f"{self.tag}_{name}", shape, dt, offset=self.at)
            self.at += (size + 63) // 64 * 64
            assert self.at <= limit, (self.tag, name, self.at, limit)
            return t

    psum = nc.alloc_psum_tensor("psum", [P, 8, HALF], F32)

    def sem(name):
        return nc.alloc_semaphore(name)

    s_phase = sem("s_phase")
    phases = {}

    def phase_end(eng):
        phases[eng] = phases.get(eng, 0) + 1
        eng.drain().then_inc(s_phase, 1)
        eng.wait_ge(s_phase, 5 * phases[eng])

    class Chain:

        def __init__(self, name):
            self.sem, self.base, self.n = sem(name), 0, 0

        def link(self, eng, ins):
            self.n += 1
            ins.then_inc(self.sem, 1)
            eng.wait_ge(self.sem, self.base + self.n)

        def trips(self, eng, n, body):
            if n == 1:
                return body(0)
            start, self.n = self.base + self.n, 0
            per = None
            with eng.Fori(0, n) as i:
                per = self.per_trip
                self.base, self.n = start + i * per, 0
                body(i)
                assert self.n == per, (self.n, per)
            self.base, self.n = start + n * per, 0

    dvec, actc, poolc = Chain("s_dve_chain"), Chain("s_act_chain"), Chain("s_pool_chain")

    def trips(eng, n, body, chain=None, links=0):
        if chain is None:
            if n == 1:
                return body(0)
            with eng.Fori(0, n) as i:
                body(i)
            return
        chain.per_trip = links
        chain.trips(eng, n, body)

    s_settled = sem("s_settled")

    def settled(eng, s, value):
        eng.wait_ge(s, value)
        if not isinstance(value, int):
            eng.sem_inc(s_settled, 1)

    s_const, s_small = sem("s_const"), sem("s_small")
    s_crow, s_ct, s_cs = sem("s_crow"), sem("s_ct"), sem("s_cs")
    s_adaw = [sem("s_adaw0"), sem("s_adaw1")]
    s_adaacc, s_adafree = sem("s_adaacc"), sem("s_adafree")
    s_adaput = [sem("s_adaput0"), sem("s_adaput1")]
    A = Arena("ada")
    crow = A("crow", [16, P])
    cs = A("cs", [P, 2, KD])
    adaw = A("w", [P, 2, KD, HALF])
    adab = A("b", [2, 2, HALF])
    adar = A("r", [2, 2, HALF])
    NCH = 6 * D // HALF
    SMALL = 0

    def sp_setup(sp):
        sp.dma_start(cst[:, :], consts).then_inc(s_const, 16)
        sp.dma_start(crow[0:8, :], c.rearrange("o (k p) -> (o k) p", p=P)).then_inc(s_crow, 16)
        sp.dma_start(crow[8:16, :], c_ctx.rearrange("(k p) -> k p", p=P)).then_inc(s_crow, 16)
        sp.sem_inc(s_adaw[0], 16)
        sp.sem_inc(s_adaw[1], 16)
        for l in range(2):
            wv = ada_w[l].rearrange("(k p) n -> p k n", p=P)

            def body(i):
                for par in range(2):
                    n = 2 * i + par
                    sp.wait_ge(s_adafree, l * NCH + n + 1)
                    sp.dma_start(adaw[:, par], wv[:, :, ds(n * HALF, HALF)]).then_inc(s_adaw[par], 16)
                    sp.dma_start(adab[:, par], ada_b[l:l + 1, ds(n * HALF, HALF)].broadcast_to([2, HALF])).then_inc(s_adaw[par], 16)

            trips(sp, NCH // 2, body)

    def act_small_loads(act):
        n = 0
        vecs = [(gains[:, 0], a_q_norm), (gains[:, 1], a_k_norm), (gains[:, 2], b_q_norm), (gains[:, 3], b_k_norm),
                (lamv[:, 0], a_lambda_q1), (lamv[:, 1], a_lambda_k1), (lamv[:, 2], a_lambda_q2),
                (lamv[:, 3], a_lambda_k2)]
        for dst, src in vecs:
            act.dma_start(dst, src.broadcast_to([P, HD])).then_inc(s_small, 16)
            n += 16
        act.dma_start(sinks[:, :], b_sink.broadcast_to([P, 16])).then_inc(s_small, 16)
        act.dma_start(subg[:, :], a_subln_g.rearrange("o e -> e o")).then_inc(s_small, 16)
        n += 32
        for l in range(2):
            act.dma_start(wrt[:, l, :, 0:NG], r_w1[l].rearrange("(k p) g -> p k g", p=P)).then_inc(s_small, 16)
            act.dma_start(brt[:, l, 0:NG], r_b1[l:l + 1, :].broadcast_to([P, NG])).then_inc(s_small, 16)
            act.dma_start(brt[:, l, NG:], r_b2[l:l + 1].rearrange("o g e -> o (g e)").broadcast_to([P, NE])).then_inc(s_small, 16)
            n += 48
            for g in range(NG):
                act.dma_start(wrt[:, l, :, NG + g * EPG:NG + (g + 1) * EPG],
                              r_w2[l, g].rearrange("(k p) e -> p k e", p=P)).then_inc(s_small, 16)
                n += 16
        return n

    n_small = 16 * (8 + 2 + 2 * (3 + NG))

    def act_setup(act):
        assert act_small_loads(act) == n_small
        act.wait_ge(s_ct, 1)
        nc.scalar.activation(cs[:, :, :], psum[:, 0, 0:16].rearrange("p (s k) -> p s k", s=2), ACT.Silu).then_inc(s_cs, 1)
        act.sem_inc(s_adaput[0], 16)
        act.sem_inc(s_adaput[1], 16)
        for l in range(2):
            def body(i):
                for par in range(2):
                    n = 2 * i + par
                    act.wait_ge(s_adafree, l * NCH + n + 3)
                    act.dma_start(mod_d[l, :, ds(n * HALF, HALF)], adar[:, par]).then_inc(s_adaput[par], 16)
            trips(act, NCH // 2, body)
        for par in range(2):
            act.wait_ge(s_adaput[par], 16 + 16 * NCH)
        act.wait_ge(s_lam, 1)
        nc.scalar.activation(lams[:, 2:4], lams[:, 0:2], ACT.Exp).then_inc(s_lam, 1)

    s_lam = sem("s_lam")

    def pe_setup(pe):
        pe.wait_ge(s_const, 16)
        pe.wait_ge(s_crow, 32)
        nc.tensor.transpose(psum[:, 0, 0:16], crow[:, :], ident[0:16, 0:16]).then_inc(s_ct, 1)
        pe.wait_ge(s_cs, 1)
        for l in range(2):
            def body(i):
                for par in range(2):
                    n = 2 * i + par
                    pe.wait_ge(s_adaw[par], 16 + 32 * (l * NCH // 2 + i + 1))
                    pe.wait_ge(s_adafree, l * NCH + n + 1)
                    for k in range(KD):
                        ins = nc.tensor.matmul(psum[0:2, 1 + par, :], cs[:, :, k], adaw[:, par, k], start=(k == 0), stop=(k == KD - 1))
                    ins.then_inc(s_adaacc, 1)
            trips(pe, NCH // 2, body)

    def dve_setup(dve):
        nc.vector.memset(ones[:, :], 1.0)
        dve.sem_inc(s_adafree, 2)
        nc.vector.memset(neghalf[:, :], -0.5)
        nc.vector.memset(blkcount[:, :], 0)
        for l in range(2):
            def body(i):
                for par in range(2):
                    n = 2 * i + par
                    dve.wait_ge(s_adaacc, l * NCH + n + 1)
                    dve.wait_ge(s_adaw[par], 16 + 32 * (l * NCH // 2 + i + 1))
                    dve.wait_ge(s_adaput[par], 16 + 16 * (l * NCH // 2 + i))
                    nc.vector.tensor_tensor(adar[:, par], psum[0:2, 1 + par, :], adab[:, par], ALU.add).then_inc(s_adafree, 1)
            trips(dve, NCH // 2, body)
        dve.wait_ge(s_const, 16)
        nc.vector.tensor_copy(ident_h[:, :], ident)
        nc.vector.tensor_copy(mask_h[:, 0], cst[:, C_PREV:C_PREV + P])
        nc.vector.tensor_copy(mask_h[:, 1], cst[:, C_NEXT:C_NEXT + P])
        dve.wait_ge(s_small, n_small)
        nc.vector.tensor_scalar(negsink[:, :], sinks[:, :], -1.0, None, ALU.mult)
        dvec.link(dve, nc.vector.tensor_scalar(subg[:, :], subg[:, :], 1.0 - LAM_INIT, None, ALU.mult))
        dvec.link(dve, nc.vector.tensor_tensor(lamw[:, :, :], lamv[:, 0:4:2], lamv[:, 1:4:2], ALU.mult))
        nc.vector.reduce_sum(lams[:, 0:2], lamw[:, :, :], AX).then_inc(s_lam, 1)
        dve.wait_ge(s_lam, 2)
        dvec.link(dve, nc.vector.tensor_tensor(neglam[:, :], lams[:, 3:4], lams[:, 2:3], ALU.subtract))
        dvec.link(dve, nc.vector.tensor_scalar(neglam[:, :], neglam[:, :], -LAM_INIT, None, ALU.add))

    s_cols, s_colt = sem("s_cols"), sem("s_colt")
    s_px = [sem("s_px0"), sem("s_px1")]
    s_pxfree, s_pss, s_prs = sem("s_pxfree"), sem("s_pss"), sem("s_prs")
    s_pxn, s_ptp, s_pta, s_ptd = sem("s_pxn"), sem("s_ptp"), sem("s_pta"), sem("s_ptd")
    s_pu = sem("s_pu")
    s_pst = [sem("s_pst0"), sem("s_pst1")]
    s_pg = sem("s_pg")
    Q = Arena("act")
    hT = Q("hT", [P, KD, NTOK])
    after_hT = Q.at
    A = Arena("prep", after_hT)
    prow = A("row", [40, P])
    pxt = A("x", [P, 2, D])
    psq = A("sq", [P, 2, D])
    pxn = A("xn", [P, 2, D])
    pss = A("ss", [P, 2])
    prs = A("rs", [P, 2])
    py2 = A("y2", [P, 2, 2, D])
    pu = A("u", [P, 2, D])
    pg2 = A("g2", [P, D])
    pw = A("w", [P, 2, 2])

    def sources(l):
        if l == 0:
            return [(0, x[0], TX, 0, 0), (TX, ctx[0], TC, 1, 0)]
        return [(TA, xs_d[0:SEQ, :], TX, 0, 0), (TA + TX, xs_d[SEQ:, :], TC, 1, SEQ)]

    def sp_cols(sp, l):
        for s in range(2):
            sp.dma_start(prow[s * 16:s * 16 + 16, :], mod_d[l, s, 0:2 * D].rearrange("(r p) -> r p", p=P)).then_inc(s_cols, 16)
        sp.dma_start(prow[32:40, :], norm1_g[l].rearrange("(r p) -> r p", p=P)).then_inc(s_cols, 16)

    def pe_cols(pe, l):
        pe.wait_ge(s_cols, 48 * (l + 1))
        nc.tensor.transpose(psum[:, 0, 0:40], prow[:, :], ident[0:40, 0:40]).then_inc(s_colt, 1)

    def dve_cols(dve, l):
        dve.wait_ge(s_colt, 1 + 2 * l)
        dvec.link(dve, nc.vector.tensor_copy(colw[:, :], psum[:, 0, 0:40]))
        for s in range(2):
            nc.vector.tensor_copy(mod_b[:, s], colw[:, s * 16:s * 16 + 8])
            ins = nc.vector.scalar_tensor_tensor(mod_a[:, s], colw[:, s * 16 + 8:s * 16 + 16], 1.0, colw[:, 32:40], ALU.add, ALU.mult)
        ins.then_inc(s_colt, 1)
        dve.wait_ge(s_colt, 2 + 2 * l)

    def combine_part(T):
        return T >= TA

    def sp_prep(sp, l):
        sp_cols(sp, l)
        for T0, src, nt, s, r0 in sources(l):
            if l:
                sp.wait_ge(s_pxn, T0 + 2)
                sp.dma_start(pg2[:, :], mod_d[0, s:s + 1, 5 * D:].broadcast_to([P, D])).then_inc(s_pg, 16)

            def body(i):
                for par in range(2):
                    t = 2 * i + par
                    sp.wait_ge(s_pxfree, T0 + t + 1)
                    sp.dma_start(pxt[:, par], src[ds(t * P, P), :]).then_inc(s_px[par], 16)
                    if l:
                        sp.dma_start(py2[:, par], y_d[ds(2 * r0 + t * 2 * P, 2 * P), :].rearrange("(p c) n -> p c n", c=2)).then_inc(s_px[par], 16)
            trips(sp, nt // 2, body)

    def px_count(l, T0, i):
        return 16 * (T0 // 2 + i + 1) if l == 0 else 16 * (TA // 2) + 32 * (T0 // 2 - TA // 2 + i + 1)

    def act_prep(act, l):
        for T0, src, nt, s, r0 in sources(l):
            def body(i):
                for par in range(2):
                    t = 2 * i + par
                    T = T0 + t
                    if l == 0:
                        act.wait_ge(s_px[par], px_count(l, T0, i))
                    else:
                        act.wait_ge(s_pu, T - TA + 1)
                        act.dma_start(xs_d[ds(r0 + t * P, P), :], pxt[:, par]).then_inc(s_pst[par], 16)
                    act.wait_ge(s_pxn, T + 1 - 2 + 2)
                    nc.scalar.activation(psq[:, par], pxt[:, par], ACT.Square, scale=1 / 32, accum_out=pss[:, par:par + 1]).then_inc(s_pss, 1)
                    act.wait_ge(s_ptp, T + 1)
                    for k in range(4):
                        ins = nc.scalar.activation(hT[:, k, ds(t * P + s * SEQ, P)], psum[:, 2 * par, k * P:(k + 1) * P], ACT.Identity,
                                                   bias=mod_b[:, s, k:k + 1], scale=mod_a[:, s, k:k + 1])
                    ins.then_inc(s_pta, 1)
            act.wait_ge(s_colt, 2 + 2 * l)
            trips(act, nt // 2, body)
        if l:
            for par in range(2):
                act.wait_ge(s_pst[par], 16 * (TA // 2))

    def pool_rstd(pool, i, dst, src, half, ready, request):
        settled(pool, *request)
        poolc.link(pool, nc.gpsimd.tensor_scalar(src, src, EPS, None, ALU.add))
        nc.gpsimd.tensor_tensor(dst, src, half, ALU.pow).then_inc(ready, 1)

    def pool_prep(pool, l):
        for T0, src, nt, s, r0 in sources(l):
            def body(i):
                for par in range(2):
                    T = T0 + 2 * i + par
                    pool_rstd(pool, i, prs[:, par:par + 1], pss[:, par:par + 1], neghalf[:, 0:1], s_prs, (s_pss, T + 1))
            trips(pool, nt // 2, body, poolc, 2)

    def dve_combine(dve, par, t, s, xt, yt, ut, wt, g2, done=None):
        dvec.link(dve, nc.vector.tensor_copy(wt, wsel[:, :, ds(t + s * TX, 1)].rearrange("p c o -> p (c o)")))
        dvec.link(dve, nc.vector.tensor_scalar(ut, yt[:, 0], wt[:, 0:1], None, ALU.mult))
        dvec.link(dve, nc.vector.scalar_tensor_tensor(ut, yt[:, 1], wt[:, 1:2], ut, ALU.mult, ALU.add))
        dvec.link(dve, nc.vector.tensor_tensor(ut, ut, g2, ALU.mult))
        return nc.vector.tensor_tensor(xt, xt, ut, ALU.add)

    def dve_prep(dve, l):
        if l == 0:
            dve.sem_inc(s_pxfree, 2)
            dve.sem_inc(s_ptd, 2)
        dve_cols(dve, l)
        for T0, src, nt, s, r0 in sources(l):
            if l:
                dve.wait_ge(s_pg, 16 * (s + 1))
            def body(i):
                for par in range(2):
                    t = 2 * i + par
                    T = T0 + t
                    dve.wait_ge(s_px[par], px_count(l, T0, i))
                    if l:
                        dve_combine(dve, par, t, s, pxt[:, par], py2[:, par], pu[:, par], pw[:, par], pg2[:, :]).then_inc(s_pu, 1)
                    dve.wait_ge(s_prs, T + 1)
                    if l:
                        dve.wait_ge(s_pst[par], 16 * (T0 // 2 - TA // 2 + i + 1))
                    nc.vector.tensor_scalar(pxn[:, par], pxt[:, par], prs[:, par:par + 1], None, ALU.mult).then_inc(s_pxn, 1)
                    dve.wait_ge(s_pxn, T + 3)
                    dve.sem_inc(s_pxfree, 1)
                    dve.wait_ge(s_ptp, T + 1)
                    for k in range(4, 8):
                        ins = nc.vector.tensor_scalar(hT[:, k, ds(t * P + s * SEQ, P)], psum[:, 2 * par + 1, (k - 4) * P:(k - 3) * P],
                                                      mod_a[:, s, k:k + 1], mod_b[:, s, k:k + 1], ALU.mult, ALU.add)
                    ins.then_inc(s_ptd, 1)
            if l == 0 and T0 == 0:
                dve.sem_inc(s_pxn, 2)
            trips(dve, nt // 2, body, dvec, 8 if l else 0)

    def pe_prep(pe, l):
        pe_cols(pe, l)
        pe.wait_ge(s_colt, 2 + 2 * l)
        if l == 0:
            pe.sem_inc(s_pta, 2)
        for T0, src, nt, s, r0 in sources(l):
            def body(i):
                for par in range(2):
                    T = T0 + 2 * i + par
                    pe.wait_ge(s_pxn, T + 3)
                    pe.wait_ge(s_pta, T + 1)
                    pe.wait_ge(s_ptd, T + 1)
                    for k in range(KD):
                        ins = nc.tensor.transpose(psum[:, 2 * par + k // 4, (k % 4) * P:(k % 4 + 1) * P], pxn[:, par, k * P:(k + 1) * P], ident)
                    ins.then_inc(s_ptp, 1)
            trips(pe, nt // 2, body)

    s_qw = [sem("s_qw0"), sem("s_qw1")]
    s_qwfree, s_qacc, s_qaccfree = sem("s_qwfree"), sem("s_qacc"), sem("s_qaccfree")
    s_qsq, s_qms, s_qrs, s_qxn, s_qt2 = sem("s_qsq"), sem("s_qms"), sem("s_qrs"), sem("s_qxn"), sem("s_qt2")
    s_qrot, s_qtr, s_qev = sem("s_qrot"), sem("s_qtr"), sem("s_qev")
    s_qst = [sem("s_qst0"), sem("s_qst1")]
    s_vev, s_vst = sem("s_vev"), sem("s_vst")
    s_rope = sem("s_rope")
    V = Q("V", [P, TA, D])
    A = Arena("qkv", Q.at)
    qw = A("w", [P, 2, KD, HALF])
    rope = A("rope", [P, 2, 2, TA, HD])
    qsq = A("sq", [P, 2, HALF])
    qms = A("ms", [P, 2, 8])
    qrs = A("rs", [P, 2, 8])
    qxn = A("xn", [P, 2, HALF])
    qt1 = A("t1", [P, 2, HALF])
    qt2 = A("t2", [P, 2, HALF])
    qrot = A("rot", [P, 2, HALF])
    qstg = A("stg", [P, 2, 4, P])
    vstg = A("vstg", [P, TA, 256])

    SECTIONS = [
        [(2, 2, TA, "qk", 8, 0, 0, 0), (1, 2, TA, "v", 0, 40, 40, 4)],
        [(1, 2, TX, "qk", 8, 60, 40, 6), (1, 1, TA, "kv", 4, 76, 56, 8)],
    ]
    WQKV = [a_wqkv[0], b_wqkv[0]]

    def sp_qkv(sp, l):
        wv = WQKV[l].rearrange("(k p) n -> p k n", p=P)

        def load(C, par, col):
            sp.wait_ge(s_qwfree, C + 1)
            sp.dma_start(qw[:, par], wv[:, :, ds(col, HALF)]).then_inc(s_qw[par], 16)

        def pair(i):
            load(2 * i, 0, 2 * i * HALF)
            load(2 * i + 1, 1, (2 * i + 1) * HALF)
        if l == 0:
            trips(sp, 3, pair)
        else:
            for n in range(3):
                load(6 + n, n % 2, n * HALF)
            for t in range(TA):
                sp.wait_ge(s_vev, t + 1)
                sp.dma_start(v_d[t * P:(t + 1) * P, :], vstg[:, t, :]).then_inc(s_vst, 16)
            sp.wait_ge(s_vst, 16 * TA)

    def pe_qkv(pe, l):
        if l == 0:
            pe.sem_inc(s_qwfree, 2)
        for ntrip, nch, nt, kind, heads, U0, R0, C0 in SECTIONS[l]:
            def body(i):
                def transposes(j):
                    R = R0 + nch * nt * i + j
                    pe.wait_ge(s_qrot, R + 1)
                    pe.wait_ge(s_qev, R + 1)
                    for b in range(4):
                        ins = nc.tensor.transpose(psum[:, 2 + j % 2, b * P:(b + 1) * P], qrot[:, j % 2, b * P:(b + 1) * P], ident)
                    ins.then_inc(s_qtr, 1)
                for ci in range(nch):
                    C = C0 + nch * i + ci
                    pe.wait_ge(s_qw[ci % 2], 16 * (C0 // 2 + i + 1))
                    for t in range(nt):
                        j = ci * nt + t
                        U = U0 + nch * nt * i + j
                        pe.wait_ge(s_qaccfree, U + 1)
                        for k in range(KD):
                            ins = nc.tensor.matmul(psum[:, j % 2, :], hT[:, k, t * P:(t + 1) * P], qw[:, ci % 2, k], start=(k == 0), stop=(k == KD - 1))
                        ins.then_inc(s_qacc, 1)
                        if t == nt - 1:
                            pe.wait_ge(s_qacc, U + 1)
                            pe.sem_inc(s_qwfree, 1)
                        if heads and j:
                            transposes(j - 1)
                if heads:
                    transposes(nch * nt - 1)
            trips(pe, ntrip, body)

    def act_qkv(act, l):
        if l == 0:
            act.sem_inc(s_qaccfree, 2)
            act.sem_inc(s_qev, 2)
            act.sem_inc(s_qst[0], 16)
            act.sem_inc(s_qst[1], 16)
        for ntrip, nch, nt, kind, heads, U0, R0, C0 in SECTIONS[l]:
            def body(i):
                def evac(j):
                    R = R0 + nch * nt * i + j
                    act.wait_ge(s_qtr, R + 3)
                    act.wait_ge(s_qst[j % 2], 16 * ((R0 + nch * nt * i) // 2 + j // 2 + 1))
                    nc.scalar.activation(qstg[:, j % 2], psum[:, 2 + j % 2, :].rearrange("p (b n) -> p b n", b=4), ACT.Copy).then_inc(s_qev, 1)
                    act.wait_ge(s_qev, R + 3)
                    q0 = (C0 - 6 * l + nch * i + j // nt) * 4
                    act.dma_start(qk_d[ds(q0, 4), :, (j % nt) * P:(j % nt + 1) * P].rearrange("h p n -> p h n"), qstg[:, j % 2]).then_inc(s_qst[j % 2], 16)
                for j in range(nch * nt):
                    U = U0 + nch * nt * i + j
                    act.wait_ge(s_qacc, U + 1)
                    if kind == "v":
                        nc.scalar.activation(V[:, j % nt, (j // nt) * HALF:(j // nt + 1) * HALF], psum[:, j % 2, :], ACT.Copy).then_inc(s_qaccfree, 1)
                    if kind == "kv":
                        nc.scalar.activation(vstg[:, j, :], psum[:, j % 2, 256:512], ACT.Copy).then_inc(s_vev, 1)
                    if heads:
                        nc.scalar.activation(qsq[:, j % 2, 0:heads * HD], psum[:, j % 2, 0:heads * HD], ACT.Square, scale=1 / 8).then_inc(s_qsq, 1)
                        if j:
                            evac(j - 1)
                if heads:
                    evac(nch * nt - 1)
            trips(act, ntrip, body)
        for par in range(2):
            act.wait_ge(s_qst[par], 16 + 16 * [40, 66][l] // 2)

    def pool_qkv(pool, l):
        settled(pool, s_rope, l + 1)
        for ntrip, nch, nt, kind, heads, U0, R0, C0 in SECTIONS[l]:
            if not heads:
                continue

            def body(i):
                which = i if l == 0 else int(kind == "kv")
                for j in range(nch * nt):
                    R = R0 + nch * nt * i + j
                    t, par = j % nt, j % 2
                    pool_rstd(pool, i, qrs[:, par, 0:heads], qms[:, par, 0:heads], neghalf[:, 0:heads], s_qrs, (s_qms, R + 1))
                    settled(pool, s_qxn, R + 1)
                    src = qxn[:, par, 0:heads * HD].rearrange("p (h a b f) -> p h a b f", a=2, b=2, f=16)
                    dst = qt2[:, par, 0:heads * HD].rearrange("p (h a b f) -> p h a b f", a=2, b=2, f=16)
                    for b in range(2):
                        for a in range(2):
                            o = a * 32 + b * 16
                            if isinstance(which, int):
                                sn = rope[:, which, 1, t, o:o + 16].unsqueeze(1).broadcast_to([P, heads, 16])
                            else:
                                sn = rope[:, ds(which, 1), 1, t, o:o + 16].broadcast_to([P, heads, 16])
                            ins = nc.gpsimd.tensor_tensor(dst[:, :, a, b, :], src[:, :, a, 1 - b, :], sn, ALU.mult)
                    ins.then_inc(s_qt2, 1)
            trips(pool, ntrip, body, poolc, nch * nt)

    def dve_qkv(dve, l):
        for w in range(2):
            g = gains[:, 2 * l + w]
            gs = g.rearrange("p (a b f) -> p a b f", a=2, b=2)
            nc.vector.tensor_tensor(rope[:, w, 0], cst[:, C_COS:C_COS + TA * HD].rearrange("p (t d) -> p t d", d=HD),
                                    g.unsqueeze(1).broadcast_to([P, TA, HD]), ALU.mult)
            sn = cst[:, C_SIN:C_SIN + TA * HD].rearrange("p (t a b f) -> p t a b f", a=2, b=2, f=16)
            dst = rope[:, w, 1].rearrange("p t (a b f) -> p t a b f", a=2, b=2)
            for a in range(2):
                for b in range(2):
                    ins = nc.vector.tensor_tensor(dst[:, :, a, b, :], sn[:, :, a, b, :],
                                                  gs[:, a, 1 - b, :].unsqueeze(1).broadcast_to([P, TA, 16]), ALU.mult)
        ins.then_inc(s_rope, 1)
        dve.wait_ge(s_rope, l + 1)
        for ntrip, nch, nt, kind, heads, U0, R0, C0 in SECTIONS[l]:
            if not heads:
                continue

            def body(i):
                which = i if l == 0 else int(kind == "kv")
                n = heads * HD
                for j in range(nch * nt):
                    R = R0 + nch * nt * i + j
                    t, par = j % nt, j % 2
                    dve.wait_ge(s_qsq, R + 1)
                    nc.vector.reduce_sum(qms[:, par, 0:heads], qsq[:, par, 0:n].rearrange("p (h d) -> p h d", d=HD), AX).then_inc(s_qms, 1)
                    dve.wait_ge(s_qrs, R + 1)
                    xn3 = qxn[:, par, 0:n].rearrange("p (h d) -> p h d", d=HD)
                    nc.vector.tensor_tensor(xn3, psum[:, par, 0:n].rearrange("p (h d) -> p h d", d=HD),
                                            qrs[:, par, 0:heads].unsqueeze(2).broadcast_to([P, heads, HD]), ALU.mult).then_inc(s_qxn, 1)
                    dve.wait_ge(s_qxn, R + 1)
                    dve.sem_inc(s_qaccfree, 1)
                    if isinstance(which, int):
                        cos = rope[:, which, 0, t].unsqueeze(1).broadcast_to([P, heads, HD])
                    else:
                        cos = rope[:, ds(which, 1), 0, t].broadcast_to([P, heads, HD])
                    t13 = qt1[:, par, 0:n].rearrange("p (h d) -> p h d", d=HD)
                    dvec.link(dve, nc.vector.tensor_tensor(t13, xn3, cos, ALU.mult))
                    dve.wait_ge(s_qt2, R + 1)
                    dve.wait_ge(s_qtr, R - 1 + 2)
                    if kind == "kv":
                        rot = qrot[:, par, :].rearrange("p (h c d) -> p h c d", c=2, d=HD)
                        dvec.link(dve, nc.vector.tensor_tensor(rot[:, :, 0], t13, qt2[:, par, 0:n].rearrange("p (h d) -> p h d", d=HD), ALU.add))
                        nc.vector.tensor_tensor(rot[:, :, 1], t13, qt2[:, par, 0:n].rearrange("p (h d) -> p h d", d=HD), ALU.add).then_inc(s_qrot, 1)
                    else:
                        nc.vector.tensor_tensor(qrot[:, par, :], qt1[:, par, :], qt2[:, par, :], ALU.add).then_inc(s_qrot, 1)
            if l == 0:
                dve.sem_inc(s_qtr, 2)
            trips(dve, ntrip, body, dvec, nch * nt * (2 if kind == "kv" else 1))


    s_kt = sem("s_kt")
    s_aq = [sem("s_aq0"), sem("s_aq1")]
    s_aqfree, s_score, s_nmax, s_exp = sem("s_aqfree"), sem("s_score"), sem("s_nmax"), sem("s_exp")
    s_mix, s_b6, s_b7, s_b6free, s_b7free = sem("s_mix"), sem("s_b6"), sem("s_b7"), sem("s_b6free"), sem("s_b7free")
    s_sumsq, s_fac, s_facdone, s_sinkexp = sem("s_sumsq"), sem("s_fac"), sem("s_facdone"), sem("s_sinkexp")
    s_ost = [sem("s_ost0"), sem("s_ost1")]
    A = Arena("att0", after_hT)
    assert A.at == after_hT
    A.at = Q.at
    kT = nc.alloc_sbuf_tensor_at("att0_kT", [P, KD, NTOK], F32, offset=(arena0 + 63) // 64 * 64)
    B = Arena("att1")
    kc = B("kc", [P, 4, CTX])
    vc = B("vc", [P, TC, 256])
    kw = B("kw", [P, 2, 4, 3 * P])
    vw = B("vw", [P, 2, 3, 256])
    es = B("es", [P, 2, 2])
    A = Arena("att", max(A.at, B.at))
    aq = A("q", [P, 2, KD, P])
    prob = A("prob", [P, 2, 2, NTOK])
    mix = A("mix", [P, 2, NTOK])
    aT = A("aT", [P, 2, 10, P])
    nmax = A("nmax", [P, 2, 2])
    mx = A("mx", [P, 2, 2])
    den = A("den", [P, 2, 2])
    rden = A("rden", [P, 2, 2])
    coef = A("coef", [P, 2, 1])
    osq = A("osq", [P, 2, P])
    ssq = A("ssq", [P, 2, 1])
    fac = A("fac", [P, 2, 1])
    on = A("on", [P, 2, P])
    oTs = A("oTs", [P, 2, KD, P])

    class Plan:

        def __init__(self, l, tiles, nblk, base):
            self.l, self.tiles, self.nblk, self.base = l, tiles, nblk, base
            self.use6, self.use7 = {}, {}
            n6 = n7 = 0
            for j in range(16):
                total = self.blocks(j)
                self.use6[j, "a"] = n6
                n6 += 1
                if total > 4:
                    self.use7[j, "b"] = n7
                    n7 += 1
                if total > 8 or j:
                    self.use6[j, "c"] = n6
                    n6 += 1
                self.use7[j, "o"] = n7
                n7 += 1
            self.use6["last"] = n6
            self.n6, self.n7 = n6 + 1, n7

        def blocks(self, j):
            return self.nblk[j // 8] * (1 if self.l == 0 else 2)

    PARTS = []
    u6 = u7 = units = 0
    for l, ntrip, t0, kinds, nblk in [(0, TX // 2, 0, ("all", "all"), (10, 10)), (0, 1, TX, ("ctx", "ctx"), (2, 2)),
                                      (1, 1, 0, ("first", "last"), (4, 4)), (1, TX // 2 - 1, 1, ("mid", "mid"), (5, 5))]:
        plan = Plan(l, kinds, nblk, (u6, u7, units))
        PARTS.append((l, ntrip, t0, kinds, nblk, plan))
        u6, u7, units = u6 + ntrip * plan.n6, u7 + ntrip * plan.n7, units + 16 * ntrip

    def tile_of(t0, kinds, i, par):
        return par * (TX - 1) if kinds[0] == "first" else t0 + 2 * i + par

    def at(plan, i):
        return plan.base[0] + i * plan.n6, plan.base[1] + i * plan.n7, plan.base[2] + i * 16

    def pair_no(plan, i):
        return plan.base[2] // 16 + i

    def q_loads(plan, i):
        n0 = PARTS[0][1] + PARTS[1][1]
        return 16 * (pair_no(plan, i) + 1) if plan.l == 0 else 16 * n0 + 48 * (pair_no(plan, i) - n0 + 1)

    def sp_att(sp, l):
        kv = qk_d.rearrange("h p n -> p h n")
        if l == 0:
            sp.dma_start(kT[:, :, :], kv[:, KD:2 * KD, :]).then_inc(s_kt, 16)
        else:
            sp.dma_start(kc[:, :, :], kv[:, 8:12, SEQ:]).then_inc(s_kt, 16)
            sp.dma_start(vc[:, :, :], v_d[SEQ:, :].rearrange("(t p) n -> p t n", p=P)).then_inc(s_kt, 16)
        for pl, ntrip, t0, kinds, nblk, plan in PARTS:
            if pl != l:
                continue

            def body(i):
                for par in range(2):
                    t = tile_of(t0, kinds, i, par)
                    sp.wait_ge(s_aqfree, 2 * pair_no(plan, i) + par + 1)
                    sp.dma_start(aq[:, par], kv[:, 0:KD, ds(t * P, P)]).then_inc(s_aq[par], 16)
                    if l:
                        lo = {"first": 0, "last": t - 1, "mid": t - 1}[kinds[par]]
                        w = {"first": 2, "last": 2, "mid": 3}[kinds[par]]
                        sp.dma_start(kw[:, par, :, 0:w * P], kv[:, 8:12, ds(lo * P, w * P)]).then_inc(s_aq[par], 16)
                        sp.dma_start(vw[:, par, 0:w, :], v_d[ds(lo * P, w * P), :].rearrange("(b p) n -> p b n", p=P)).then_inc(s_aq[par], 16)
            trips(sp, ntrip, body)

    def pool_att(pool, l):
        if l:
            return
        for pl, ntrip, t0, kinds, nblk, plan in PARTS:
            if pl != l:
                continue

            def body(i):
                u0 = at(plan, i)[2]
                for j in range(16):
                    settled(pool, s_fac, u0 + j + 1)
                    nc.gpsimd.tensor_tensor(fac[:, j % 2], ssq[:, j % 2], neghalf[:, 0:1], ALU.pow).then_inc(s_facdone, 1)
            trips(pool, ntrip, body)

    def pe_att(pe, l):
        if l == 0:
            pe.sem_inc(s_aqfree, 2)
        pe.wait_ge(s_kt, 16 if l == 0 else 48)
        for pl, ntrip, t0, kinds, nblk, plan in PARTS:
            if pl != l:
                continue

            def body(i):
                b6, b7, u0 = at(plan, i)

                def scores(j, m):
                    par, h, kind = j // 8, j % 8, kinds[j // 8]
                    if h == 0 and m == 0:
                        pe.wait_ge(s_aq[par], q_loads(plan, i))
                    n = 2 * (u0 + j) + m
                    pe.wait_ge(s_exp, n + 1)
                    q = aq[64 * m:64 * m + 64, par, h, :]
                    r = slice(64 * m, 64 * m + 64)
                    if l == 0:
                        if kind == "all":
                            for b, (lo, hi) in enumerate(((0, 512), (512, 1024), (1024, 1280))):
                                ins = nc.tensor.matmul(psum[:, 3 * m + b, 0:hi - lo], q, kT[r, h, lo:hi], start=True, stop=True)
                        else:
                            ins = nc.tensor.matmul(psum[:, 3 * m, 0:CTX], q, kT[r, h, SEQ:], start=True, stop=True)
                    else:
                        g = h // 2
                        nc.tensor.matmul(psum[:, 3 * m, 0:CTX], q, kc[r, g, :], start=True, stop=True)
                        window = {"mid": [(0, CTX, 0, 0), (0, CTX + P, 1, None), (1, 0, 2, 1)],
                                  "first": [(0, CTX, 0, None), (0, CTX + P, 1, 1)],
                                  "last": [(0, CTX, 0, 0), (0, CTX + P, 1, None)]}[kind]
                        for bank, col, blk, mask in window:
                            o = psum[:, 3 * m + bank, col:col + P]
                            ins = nc.tensor.matmul(o, q, kw[r, par, g, blk * P:(blk + 1) * P], start=True, stop=mask is None)
                            if mask is not None:
                                ins = nc.tensor.matmul(o, ident_h[:, :], mask_h[:, mask], start=False, stop=True)
                    ins.then_inc(s_score, 1)

                def block(j, b):
                    if l == 0:
                        return mix[:, j % 2, b * P:(b + 1) * P]
                    nb = nblk[j // 8]
                    return prob[:, j % 2, b // nb, (b % nb) * P:(b % nb + 1) * P]

                def values(j, b):
                    par, h = j // 8, j % 8
                    if l == 0:
                        return V[:, b if kinds[par] == "all" else TX + b, h * P:(h + 1) * P]
                    g = h // 2
                    b = b % nblk[par]
                    return vc[:, b, g * HD:(g + 1) * HD] if b < TC else vw[:, par, b - TC, g * HD:(g + 1) * HD]

                def turn(j, bank, lo, hi, extra=None):
                    for b in range(lo, hi):
                        ins = nc.tensor.transpose(psum[:, bank, (b - lo) * P:(b - lo + 1) * P], block(j, b), ident)
                    if extra is not None:
                        ins = nc.tensor.transpose(psum[:, bank, 3 * P:4 * P], on[:, extra % 2], ident)
                    ins.then_inc(s_b6 if bank == 6 else s_b7, 1)

                scores(0, 0)
                scores(0, 1)
                for j in range(16):
                    total = plan.blocks(j)
                    if j < 15:
                        scores(j + 1, 0)
                    if l == 0:
                        pe.wait_ge(s_mix, u0 + j + 1)
                    else:
                        pe.wait_ge(s_exp, 2 * (u0 + j) + 2 + 2)
                    pe.wait_ge(s_b6free, b6 + plan.use6[j, "a"] + 1)
                    turn(j, 6, 0, min(4, total))
                    if total > 4:
                        pe.wait_ge(s_b7free, b7 + plan.use7[j, "b"] + 1)
                        turn(j, 7, 4, min(8, total))
                    if j < 15:
                        scores(j + 1, 1)
                    if (j, "c") in plan.use6:
                        pe.wait_ge(s_b6free, b6 + plan.use6[j, "c"] + 1)
                        if j:
                            pe.wait_ge(s_b7free, b7 + plan.use7[j - 1, "o"] + 2)
                        turn(j, 6, 8, max(8, total), j - 1 if j else None)
                    pe.wait_ge(s_b6free, b6 + plan.use6[j, "c" if total > 8 else "a"] + 2)
                    pe.wait_ge(s_b7free, b7 + plan.use7[j, "o"] + 1)
                    nb = nblk[j // 8]
                    for b in range(total):
                        m = b // nb
                        o = psum[:, 7, 0:P] if l == 0 else psum[:, 7, m * HD:(m + 1) * HD]
                        ins = nc.tensor.matmul(o, aT[:, j % 2, b, :], values(j, b), start=(b % nb == 0), stop=(b % nb == nb - 1))
                    ins.then_inc(s_b7, 1)
                    if j % 8 == 7:
                        pe.wait_ge(s_b7, b7 + plan.use7[j, "o"] + 1)
                        pe.sem_inc(s_aqfree, 1)
                pe.wait_ge(s_b7free, b7 + plan.use7[15, "o"] + 2)
                pe.wait_ge(s_b6free, b6 + plan.use6["last"] + 1)
                turn(15, 6, 0, 0, 15)
            trips(pe, ntrip, body)

    def act_att(act, l):
        for pl, ntrip, t0, kinds, nblk, plan in PARTS:
            if pl != l:
                continue

            def body(i):
                b6, b7, u0 = at(plan, i)

                def expo(j, m):
                    width = nblk[j // 8] * P
                    n = 2 * (u0 + j) + m
                    act.wait_ge(s_nmax, n + 1)
                    if l:
                        act.wait_ge(s_b7, b7 + plan.use7[j - 2, "o"] + 1) if j >= 2 else None
                    q = 0 if l == 0 else j % 2
                    nc.scalar.activation(prob[:, q, m, 0:width], psum[:, 3 * m:3 * m + 3, :].rearrange("p b n -> p (b n)")[:, 0:width], ACT.Exp,
                                         bias=nmax[:, j % 2, m:m + 1], scale=SCALE, accum_out=den[:, j % 2, m:m + 1]).then_inc(s_exp, 1)
                    if l:
                        h = 2 * (j % 8) + m
                        nc.scalar.activation(es[:, j % 2, m:m + 1], nmax[:, j % 2, m:m + 1], ACT.Exp, bias=sinks[:, h:h + 1]).then_inc(s_sinkexp, 1)

                def evac6(j, key, lo, hi, extra=None):
                    use = plan.use6[key if key == "last" else (j, key)]
                    act.wait_ge(s_b6, b6 + use + 1)
                    if hi > lo:
                        ins = nc.scalar.activation(aT[:, j % 2, lo:hi, :], psum[:, 6, 0:(hi - lo) * P].rearrange("p (b n) -> p b n", n=P), ACT.Copy)
                    if extra is not None:
                        if extra % 8 == 0:
                            act.wait_ge(s_ost[extra // 8], 16 + 16 * pair_no(plan, i))
                        dst = oTs[:, extra // 8, extra % 8, :]
                        if l == 0:
                            ins = nc.scalar.activation(dst, psum[:, 6, 3 * P:4 * P], ACT.Copy, scale=subg[:, 0:1])
                        else:
                            ins = nc.scalar.activation(dst, psum[:, 6, 3 * P:4 * P], ACT.Copy)
                    ins.then_inc(s_b6free, 1)
                    if extra in (7, 15):
                        par = extra // 8
                        act.wait_ge(s_b6free, b6 + use + 2)
                        act.dma_start(o_d[ds(tile_of(t0, kinds, i, par), 1)].rearrange("o p n -> p (o n)"),
                                      oTs[:, par].rearrange("p k n -> p (k n)")).then_inc(s_ost[par], 16)

                expo(0, 0)
                expo(0, 1)
                for j in range(16):
                    total = plan.blocks(j)
                    if j < 15:
                        expo(j + 1, 0)
                    evac6(j, "a", 0, min(4, total))
                    if j < 15:
                        expo(j + 1, 1)
                    if (j, "c") in plan.use6:
                        evac6(j, "c", 8, max(8, total), j - 1 if j else None)
                    if l == 0:
                        act.wait_ge(s_b7, b7 + plan.use7[j, "o"] + 1)
                        nc.scalar.activation(osq[:, j % 2], psum[:, 7, 0:P], ACT.Square, accum_out=ssq[:, j % 2]).then_inc(s_sumsq, 1)
                evac6(15, "last", 0, 0, 15)
            if l == 0 and t0 == 0:
                act.sem_inc(s_ost[0], 16)
                act.sem_inc(s_ost[1], 16)
                act.sem_inc(s_b6free, 1)
                act.sem_inc(s_exp, 2)
            trips(act, ntrip, body)
        for par in range(2):
            act.wait_ge(s_ost[par], 16 + 16 * sum(p[1] for p in PARTS if p[0] <= l))

    def dve_att(dve, l):
        for pl, ntrip, t0, kinds, nblk, plan in PARTS:
            if pl != l:
                continue

            def body(i):
                b6, b7, u0 = at(plan, i)

                def peak(j, m):
                    width = nblk[j // 8] * P
                    dve.wait_ge(s_score, 2 * (u0 + j) + m + 1)
                    dvec.link(dve, nc.vector.reduce_max(mx[:, j % 2, m:m + 1], psum[:, 3 * m:3 * m + 3, :].rearrange("p b n -> p (b n)")[:, 0:width], AX))
                    if l == 0:
                        nc.vector.tensor_scalar(nmax[:, j % 2, m:m + 1], mx[:, j % 2, m:m + 1], -SCALE, None, ALU.mult).then_inc(s_nmax, 1)
                    else:
                        h = 2 * (j % 8) + m
                        nc.vector.scalar_tensor_tensor(nmax[:, j % 2, m:m + 1], mx[:, j % 2, m:m + 1], -SCALE, negsink[:, h:h + 1], ALU.mult, ALU.min).then_inc(s_nmax, 1)

                def weigh(j):
                    width = nblk[j // 8] * P
                    q = j % 2
                    dve.wait_ge(s_exp, 2 * (u0 + j) + 2 + 2)
                    dvec.link(dve, nc.vector.reciprocal(rden[:, q, 1:2], den[:, q, 1:2]))
                    dvec.link(dve, nc.vector.scalar_tensor_tensor(coef[:, q], den[:, q, 0:1], neglam[:, 0:1], rden[:, q, 1:2], ALU.mult, ALU.mult))
                    nc.vector.scalar_tensor_tensor(mix[:, q, 0:width], prob[:, 0, 1, 0:width], coef[:, q], prob[:, 0, 0, 0:width], ALU.mult, ALU.add).then_inc(s_mix, 1)

                def finish(j):
                    q = j % 2
                    dve.wait_ge(s_b7, b7 + plan.use7[j, "o"] + 1)
                    if l == 0:
                        dvec.link(dve, nc.vector.scalar_tensor_tensor(coef[:, q], den[:, q, 0:1], EPS, den[:, q, 0:1], ALU.mult, ALU.mult))
                        dve.wait_ge(s_sumsq, u0 + j + 1)
                        nc.vector.scalar_tensor_tensor(ssq[:, q], ssq[:, q], 1 / P, coef[:, q], ALU.mult, ALU.add).then_inc(s_fac, 1)
                        dve.wait_ge(s_facdone, u0 + j + 1)
                        nc.vector.tensor_scalar(on[:, q], psum[:, 7, 0:P], fac[:, q], None, ALU.mult).then_inc(s_b7free, 1)
                    else:
                        n1 = 2 * (u0 - 16 * (PARTS[0][1] + PARTS[1][1]) + j) + 2
                        dve.wait_ge(s_sinkexp, n1)
                        dvec.link(dve, nc.vector.tensor_tensor(rden[:, q], den[:, q], es[:, q], ALU.add))
                        dvec.link(dve, nc.vector.reciprocal(rden[:, q], rden[:, q]))
                        nc.vector.tensor_tensor(on[:, q].rearrange("p (m d) -> p m d", m=2), psum[:, 7, 0:P].rearrange("p (m d) -> p m d", m=2),
                                                rden[:, q].unsqueeze(2).broadcast_to([P, 2, HD]), ALU.mult).then_inc(s_b7free, 1)

                peak(0, 0)
                peak(0, 1)
                if l == 0:
                    weigh(0)
                for j in range(16):
                    total = plan.blocks(j)
                    if j < 15:
                        peak(j + 1, 0)
                    if total > 4:
                        dve.wait_ge(s_b7, b7 + plan.use7[j, "b"] + 1)
                        hi = min(8, total)
                        nc.vector.tensor_copy(aT[:, j % 2, 4:hi, :], psum[:, 7, 0:(hi - 4) * P].rearrange("p (b n) -> p b n", n=P)).then_inc(s_b7free, 1)
                    if j < 15:
                        peak(j + 1, 1)
                        if l == 0:
                            weigh(j + 1)
                    finish(j)
            if l == 0 and t0 == 0:
                dve.sem_inc(s_b7free, 1)
            trips(dve, ntrip, body, dvec, 16 * 2 + (16 * 3 if l == 0 else 16 * 2))

    s_pw = sem("s_pw")
    s_pin = [sem("s_pin0"), sem("s_pin1")]
    s_pinfree, s_y, s_x1, s_x1ss, s_x1rs, s_h, s_h2 = [sem(n) for n in ("s_pinfree", "s_y", "s_x1", "s_x1ss", "s_x1rs", "s_h", "s_h2")]
    s_h2t, s_h2ta, s_h2td, s_rl, s_rld = [sem(n) for n in ("s_h2t", "s_h2ta", "s_h2td", "s_rl", "s_rld")]
    s_x1st = [sem("s_x1st0"), sem("s_x1st1")]
    s_h2st = [sem("s_h2st0"), sem("s_h2st1")]
    s_bc, s_bcd = sem("s_bc"), sem("s_bcd")
    A = Arena("post")
    wo = A("wo", [P, KD, D])
    bc = A("bc", [P, 4, D])
    oT = A("oT", [P, 2, KD, P])
    xt = A("xt", [P, 2, D])
    x1 = A("x1", [P, 2, D])
    xsq = A("sq", [P, 2, D])
    xss = A("ss", [P, 2])
    xrs = A("rs", [P, 2])
    hm = A("hm", [P, 2, D])
    h2 = A("h2", [P, 2, D])
    h2T = A("h2T", [P, 2, KD, P])

    POST = [[(0, TX, 0), (TX, TC, 1)], [(TA, TX, 0)]]

    def sp_post(sp, l):
        sp.dma_start(wo[:, :, :], [a_wo, b_wo][l][0].rearrange("(k p) n -> p k n", p=P)).then_inc(s_pw, 16)
        for T0, nt, s in POST[l]:
            sp.wait_ge(s_h2, T0)
            for n, src in enumerate([mod_d[l, s:s + 1, 2 * D:3 * D], mod_d[l, s:s + 1, 3 * D:4 * D],
                                     mod_d[l, s:s + 1, 4 * D:5 * D], norm2_g[l:l + 1, :]]):
                sp.dma_start(bc[:, n], src.broadcast_to([P, D])).then_inc(s_bc, 16)

            def body(i):
                for par in range(2):
                    T = T0 + 2 * i + par
                    t = T - TA * l
                    src = x[0, ds(t * P, P), :] if l == 0 and s == 0 else (ctx[0, ds((t - TX) * P, P), :] if l == 0 else xs_d[ds(t * P, P), :])
                    sp.wait_ge(s_pinfree, T + 1)
                    sp.dma_start(oT[:, par].rearrange("p k n -> p (k n)"), o_d[ds(t, 1)].rearrange("o p n -> p (o n)")).then_inc(s_pin[par], 16)
                    sp.dma_start(xt[:, par], src).then_inc(s_pin[par], 16)
            trips(sp, nt // 2, body)

    def pe_post(pe, l):
        pe.wait_ge(s_pw, 16 * (l + 1))
        for T0, nt, s in POST[l]:
            def body(i):
                def turn(par):
                    T = T0 + 2 * i + par
                    pe.wait_ge(s_h2, T + 1)
                    pe.wait_ge(s_h2ta, T)
                    pe.wait_ge(s_h2td, T)
                    for k in range(KD):
                        ins = nc.tensor.transpose(psum[:, 4 + k // 4, (k % 4) * P:(k % 4 + 1) * P], h2[:, par, k * P:(k + 1) * P], ident)
                    ins.then_inc(s_h2t, 1)

                def route(par):
                    T = T0 + 2 * i + par
                    pe.wait_ge(s_h2ta, T + 1)
                    pe.wait_ge(s_h2td, T + 1)
                    pe.wait_ge(s_rld, T + 1)
                    for k in range(KD):
                        ins = nc.tensor.matmul(psum[:, 6 + par, 0:NG + NE], h2T[:, par, k, :], wrt[:, l, k, :], start=(k == 0), stop=(k == KD - 1))
                    ins.then_inc(s_rl, 1)

                for par in range(2):
                    T = T0 + 2 * i + par
                    pe.wait_ge(s_pin[par], 32 * (T0 // 2 + i + 1))
                    pe.wait_ge(s_x1, T + 1)
                    for n in range(2):
                        for k in range(KD):
                            ins = nc.tensor.matmul(psum[:, 2 * par + n, :], oT[:, par, k, :], wo[:, k, n * HALF:(n + 1) * HALF], start=(k == 0), stop=(k == KD - 1))
                        if n == 1:
                            ins.then_inc(s_y, 1)
                        elif par:
                            turn(0)
                route(0)
                turn(1)
                route(1)
            if l == 0 and T0 == 0:
                pe.sem_inc(s_pinfree, 2)
            trips(pe, nt // 2, body)

    def dve_post(dve, l):
        if l == 0:
            dve.sem_inc(s_x1, 2)
            dve.sem_inc(s_rld, 2)
        for n, (T0, nt, s) in enumerate(POST[l]):
            parts = n + len(POST[0]) * l
            dve.wait_ge(s_bc, 64 * (parts + 1))
            nc.vector.scalar_tensor_tensor(bc[:, 2], bc[:, 2], 1.0, bc[:, 3], ALU.add, ALU.mult).then_inc(s_bcd, 1)
            dve.wait_ge(s_bcd, parts + 1)

            def body(i):
                def first(par):
                    T = T0 + 2 * i + par
                    dve.wait_ge(s_pin[par], 32 * (T0 // 2 + i + 1))
                    dve.wait_ge(s_y, T + 1)
                    dve.wait_ge(s_x1st[par], 16 * (T0 // 2 + i + 1))
                    y = psum[:, 2 * par:2 * par + 2, :].rearrange("p b n -> p (b n)")
                    dvec.link(dve, nc.vector.tensor_tensor(x1[:, par], y, bc[:, 0], ALU.mult))
                    dvec.link(dve, nc.vector.tensor_tensor(x1[:, par], x1[:, par], xt[:, par], ALU.add))
                    dve.sem_inc(s_x1, 1)
                    dve.sem_inc(s_pinfree, 1)
                    dve.wait_ge(s_x1rs, T + 1)
                    nc.vector.scalar_tensor_tensor(hm[:, par], x1[:, par], xrs[:, par:par + 1], bc[:, 2], ALU.mult, ALU.mult).then_inc(s_h, 1)

                def second(par):
                    T = T0 + 2 * i + par
                    dve.wait_ge(s_h2t, T + 1)
                    nc.vector.tensor_copy(h2T[:, par, 4:8, :], psum[:, 5, :].rearrange("p (b n) -> p b n", b=4)).then_inc(s_h2td, 1)

                def third(par):
                    T = T0 + 2 * i + par
                    dve.wait_ge(s_rl, T + 1)
                    nc.vector.tensor_tensor(logits[:, ds(T - TA * l, 1), :].rearrange("p o n -> p (o n)"), psum[:, 6 + par, 0:NG + NE], brt[:, l, :], ALU.add).then_inc(s_rld, 1)
                first(0)
                second(0)
                first(1)
                third(0)
                second(1)
                third(1)
            trips(dve, nt // 2, body, dvec, 4)

    def act_post(act, l):
        if l == 0:
            for s in s_x1st + s_h2st:
                act.sem_inc(s, 16)
        for T0, nt, s in POST[l]:
            def body(i):
                def first(par):
                    T = T0 + 2 * i + par
                    t = T - TA * l
                    act.wait_ge(s_x1, T + 3)
                    act.dma_start(xs_d[ds(t * P, P), :], x1[:, par]).then_inc(s_x1st[par], 16)
                    nc.scalar.activation(xsq[:, par], x1[:, par], ACT.Square, scale=1 / 32, accum_out=xss[:, par:par + 1]).then_inc(s_x1ss, 1)
                    act.wait_ge(s_h2, T + 1)
                    act.dma_start(h2_d[ds(t * P, P), :], h2[:, par]).then_inc(s_h2st[par], 16)

                def second(par):
                    T = T0 + 2 * i + par
                    act.wait_ge(s_h2t, T + 1)
                    nc.scalar.activation(h2T[:, par, 0:4, :], psum[:, 4, :].rearrange("p (b n) -> p b n", b=4), ACT.Copy).then_inc(s_h2ta, 1)
                first(0)
                second(0)
                first(1)
                second(1)
            trips(act, nt // 2, body)
        for s in s_x1st + s_h2st:
            act.wait_ge(s, 16 + 16 * (TA // 2 if l == 0 else (TA + TX) // 2))

    def pool_post(pool, l):
        for n, (T0, nt, s) in enumerate(POST[l]):
            def body(i):
                for par in range(2):
                    T = T0 + 2 * i + par
                    pool_rstd(pool, i, xrs[:, par:par + 1], xss[:, par:par + 1], neghalf[:, 0:1], s_x1rs, (s_x1ss, T + 1))
                    settled(pool, s_h, T + 1)
                    settled(pool, s_h2st[par], 16 * (T0 // 2 + i + 1))
                    nc.gpsimd.tensor_tensor(h2[:, par], hm[:, par], bc[:, 1], ALU.add).then_inc(s_h2, 1)
            trips(pool, nt // 2, body, poolc, 2)

    s_rt, s_rta, s_rtp, s_rtm = sem("s_rt"), sem("s_rta"), sem("s_rtp"), sem("s_rtm")
    A = Arena("route")
    rg = A("rg", [P, TA, 8, NG])
    ru = A("ru", [P, TA, 16])
    re = A("re", [P, TA, 8, NE])
    pre = A("pre", [P, TA, NE])
    tot = A("tot", [P, NE])
    er = A("er", [P, 8, NE])
    eri = A("eri", [P, 2, NE], I32)
    sli = A("sli", [P, 2, TA], I32)
    slf = A("slf", [P, 6, TA])
    cmp_ = A("cmp", [P, NBT, NE])
    ebf = A("ebf", [P, NBT])
    lane1 = A("lane1", [P, 2, TA, P])
    blk1 = A("blk1", [P, 2, TA, NBT])
    tabf = A("tabf", [P, 2, NBT])

    def dve_route(dve, l):
        nt = TILES[l]
        V_ = nc.vector
        L = lambda ins: dvec.link(dve, ins)

        def pick(val, width, eq, code, top, code_top, one):
            L(V_.reduce_max(top, val, AX))
            L(V_.tensor_tensor(eq, val, top.unsqueeze(2).broadcast_to([P, nt, width]), ALU.is_equal))
            L(V_.tensor_tensor(code, eq, iota[:, P - width:P].unsqueeze(1).broadcast_to([P, nt, width]), ALU.mult))
            L(V_.tensor_scalar(eq, eq, float(P), None, ALU.mult))
            L(V_.tensor_tensor(code, eq, code, ALU.subtract))
            L(V_.reduce_max(code_top, code, AX))
            L(V_.tensor_tensor(one, code, code_top.unsqueeze(2).broadcast_to([P, nt, width]), ALU.is_equal))

        g = lambda n: rg[:, 0:nt, n, :]
        e = lambda n: re[:, 0:nt, n, :]
        u = lambda n: ru[:, 0:nt, n]
        G = logits[:, 0:nt, 0:NG]
        pick(G, NG, g(0), g(1), u(0), u(1), g(2))
        V_.tensor_tensor(g(3), G, u(0).unsqueeze(2).broadcast_to([P, nt, NG]), ALU.subtract).then_inc(s_rt, 1)
        L(V_.tensor_scalar(g(4), g(2), BIG, -BIG, ALU.mult, ALU.add))
        for n in range(NG):
            ins = V_.tensor_tensor(e(0)[:, :, n * EPG:(n + 1) * EPG], logits[:, 0:nt, NG + n * EPG:NG + (n + 1) * EPG],
                                   g(4)[:, :, n:n + 1].broadcast_to([P, nt, EPG]), ALU.add)
        L(ins)
        pick(e(0), NE, e(3), e(4), u(2), u(3), e(1))
        L(V_.scalar_tensor_tensor(e(5), e(1), -2 * BIG, e(0), ALU.mult, ALU.add))
        pick(e(5), NE, e(3), e(4), u(4), u(5), e(2))
        V_.tensor_tensor(u(6), u(4), u(2), ALU.subtract).then_inc(s_rt, 1)
        dve.wait_ge(s_rta, 2 * (l + 1))
        L(V_.reduce_sum(u(7), g(5), AX))
        L(V_.reciprocal(u(7), u(7)))
        L(V_.tensor_scalar(u(9), u(8), 1.0, None, ALU.add))
        L(V_.reciprocal(u(9), u(9)))
        L(V_.tensor_tensor(wsel[:, 0, 0:nt], u(7), u(9), ALU.mult))
        L(V_.tensor_tensor(wsel[:, 1, 0:nt], u(8), wsel[:, 0, 0:nt], ALU.mult))
        L(V_.tensor_tensor(e(6), e(1), e(2), ALU.add))
        L(V_.memset(pre[:, 0], 0.0))
        for t in range(1, nt):
            L(V_.tensor_tensor(pre[:, t], pre[:, t - 1], re[:, t - 1, 6], ALU.add))
        V_.tensor_tensor(tot[:, :], pre[:, nt - 1], re[:, nt - 1, 6], ALU.add).then_inc(s_rtp, 1)
        dve.wait_ge(s_rtm, 2 * l + 1)
        L(V_.tensor_scalar(er[:, 0], psum[:, 1, 0:NE], float(P - 1), None, ALU.add))
        L(V_.tensor_copy(eri[:, 0], er[:, 0]))
        L(V_.tensor_scalar(eri[:, 1], eri[:, 0], 7, None, ALU.arith_shift_right))
        L(V_.tensor_copy(er[:, 1], eri[:, 1]))
        L(V_.memset(er[:, 2], 1.0))
        L(V_.tensor_tensor_scan(er[:, 3], er[:, 2], er[:, 1], 0.0, ALU.mult, ALU.add))
        L(V_.tensor_copy(blkcount[:, l:l + 1], er[:, 3, NE - 1:NE]))
        L(V_.tensor_tensor(er[:, 4], er[:, 3], er[:, 1], ALU.subtract))
        L(V_.tensor_scalar(er[:, 4], er[:, 4], float(P), None, ALU.mult))
        L(V_.tensor_tensor(cmp_[:, :, :], er[:, 3].unsqueeze(1).broadcast_to([P, NBT, NE]),
                           iota[:, 0:NBT].unsqueeze(2).broadcast_to([P, NBT, NE]), ALU.is_le))
        L(V_.reduce_sum(ebf[:, :], cmp_[:, :, :], AX))
        L(V_.tensor_scalar(ebf[:, :], ebf[:, :], float(NE - 1), None, ALU.min))
        L(V_.tensor_copy(exptab[:, :], ebf[:, :]))
        L(V_.tensor_tensor(e(7), psum[:, 0, 0:nt * NE].rearrange("p (t e) -> p t e", e=NE),
                           er[:, 4].unsqueeze(1).broadcast_to([P, nt, NE]), ALU.add))
        for q in range(2):
            L(V_.tensor_tensor(e(3), e(7), e(1 + q), ALU.mult))
            L(V_.reduce_sum(slf[:, q, 0:nt], e(3), AX))
            L(V_.tensor_copy(sli[:, 0, 0:nt], slf[:, q, 0:nt]))
            L(V_.tensor_scalar(sli[:, 1, 0:nt], sli[:, 0, 0:nt], 7, None, ALU.arith_shift_right))
            L(V_.tensor_copy(slf[:, 2 + q, 0:nt], sli[:, 1, 0:nt]))
            L(V_.scalar_tensor_tensor(slf[:, 4 + q, 0:nt], slf[:, 2 + q, 0:nt], -float(P), slf[:, q, 0:nt], ALU.mult, ALU.add))
        for q in range(2):
            for t in range(nt):
                V_.tensor_scalar(lane1[:, q, t], iota, slf[:, 4 + q, t:t + 1], None, ALU.is_equal)
                ins = V_.tensor_scalar(blk1[:, q, t], iota[:, 0:NBT], slf[:, 2 + q, t:t + 1], tokrow[:, t:t + 1], ALU.is_equal, ALU.mult)
            L(ins)
            if q:
                for t in range(nt):
                    L(V_.tensor_scalar(cmp_[:, 0:NBT, 0], iota[:, 0:NBT], slf[:, 3, t:t + 1], None, ALU.is_equal))
                    ins = V_.tensor_tensor(blk1[:, 1, t], blk1[:, 1, t], cmp_[:, 0:NBT, 0], ALU.add)
                    L(ins)
        L(V_.memset(tabf[:, 1], 0.0))
        dve.sem_inc(s_rtp, 1)
        dve.wait_ge(s_rtm, 2 * l + 2)
        L(V_.tensor_scalar(tabf[:, 1], psum[:, 2, 0:NBT], 0.0, float(EMPTY), ALU.is_equal, ALU.mult))
        L(V_.scalar_tensor_tensor(tabf[:, 0], psum[:, 2, 0:NBT], -1.0, tabf[:, 1], ALU.add, ALU.add))
        L(V_.tensor_scalar(tabf[:, 0], tabf[:, 0], 0.0, None, ALU.max))
        L(V_.tensor_copy(rowtab[:, :], tabf[:, 0]))
        L(V_.tensor_scalar(toktab[:, :], rowtab[:, :], 1, None, ALU.arith_shift_right))

    def act_route(act, l):
        nt = TILES[l]
        act.wait_ge(s_rt, 2 * l + 1)
        nc.scalar.activation(rg[:, 0:nt, 5, :], rg[:, 0:nt, 3, :], ACT.Exp).then_inc(s_rta, 1)
        act.wait_ge(s_rt, 2 * l + 2)
        nc.scalar.activation(ru[:, 0:nt, 8], ru[:, 0:nt, 6], ACT.Exp).then_inc(s_rta, 1)

    def pe_route(pe, l):
        nt = TILES[l]
        pe.wait_ge(s_rtp, 2 * l + 1)
        nc.tensor.matmul(psum[:, 0, 0:nt * NE].rearrange("p (t e) -> p t e", e=NE), tri, re[:, 0:nt, 6, :], start=True, stop=False)
        nc.tensor.matmul(psum[:, 0, 0:nt * NE].rearrange("p (t e) -> p t e", e=NE), ones[:, :], pre[:, 0:nt, :], start=False, stop=True)
        nc.tensor.matmul(psum[:, 1, 0:NE], ones[:, :], tot[:, :], start=True, stop=True).then_inc(s_rtm, 1)
        pe.wait_ge(s_rtp, 2 * l + 2)
        for q in range(2):
            for t in range(nt):
                ins = nc.tensor.matmul(psum[:, 2, 0:NBT], lane1[:, q, t], blk1[:, q, t], start=(q + t == 0), stop=(q == 1 and t == nt - 1))
        ins.then_inc(s_rtm, 1)

    s_g, s_u, s_w2 = sem("s_g"), sem("s_u"), sem("s_w2")
    s_gup, s_upp = sem("s_gup"), sem("s_upp")
    s_xg, s_xtp, s_xta, s_xtd = sem("s_xg"), sem("s_xtp"), sem("s_xta"), sem("s_xtd")
    s_sil, s_hh, s_ht, s_hta, s_htd, s_yb, s_ya, s_yd, s_ys = [
        sem(n) for n in ("s_sil", "s_hh", "s_ht", "s_hta", "s_htd", "s_yb", "s_ya", "s_yd", "s_ys")]
    s_idx, s_xz = sem("s_idx"), sem("s_xz")
    A = Arena("moe")
    wg = A("wg", [P, 2, KD, DE])
    wu = A("wu", [P, 2, KD, DE])
    w2 = A("w2", [P, 2, DE // P, D])
    xg = A("xg", [P, D])
    xT = A("xT", [P, KD, P])
    sg = A("sg", [P, DE])
    hh = A("hh", [P, DE])
    hT2 = A("hT2", [P, DE // P, P])
    yo = A("yo", [P, D])
    gidx = A("gidx", [P, 1], I32)
    sidx = A("sidx", [P, 1], I32)

    counts = {}

    def blocks(eng, l):
        n = eng.value_load(blkcount[0:1, l:l + 1], min_val=NB_MIN[l], max_val=NB_MAX[l])
        n = eng.snap(n, min_val=NB_MIN[l], max_val=NB_MAX[l])
        before = counts.get((eng, 0), 0)
        counts[eng, l] = n
        return before, n

    def moe_loop(eng, l, body, chain=None):
        before, n = blocks(eng, l)
        with eng.Fori(0, n) as b:
            body(b, before + b)
        return before + n

    def sp_moe(sp, l):
        if l == 0:
            for s in (s_g, s_u, s_w2):
                sp.sem_inc(s, 16)
        w13v = e_w13[l].rearrange("e (k p) f -> p e k f", p=P)
        w2v = e_w2[l].rearrange("e (k p) f -> p e k f", p=P)

        def body(b, B):
            e = sp.value_load(exptab[0:1, ds(b, 1)], min_val=0, max_val=NE - 1)
            par = b % 2
            settled(sp, s_g, 16 * B + 16)
            settled(sp, s_gup, B + 1)
            sp.dma_start(wg[:, ds(par, 1)].rearrange("p o k f -> p (o k) f"), w13v[:, ds(e, 1), :, 0:DE].rearrange("p o k f -> p (o k) f")).then_inc(s_g, 16)
            settled(sp, s_u, 16 * B + 16)
            settled(sp, s_upp, B + 1)
            sp.dma_start(wu[:, ds(par, 1)].rearrange("p o k f -> p (o k) f"), w13v[:, ds(e, 1), :, DE:].rearrange("p o k f -> p (o k) f")).then_inc(s_u, 16)
            settled(sp, s_w2, 16 * B + 16)
            settled(sp, s_yb, B + 1)
            sp.dma_start(w2[:, ds(par, 1)].rearrange("p o k f -> p (o k) f"), w2v[:, ds(e, 1), :, :].rearrange("p o k f -> p (o k) f")).then_inc(s_w2, 16)
        moe_loop(sp, l, body)

    def pool_moe(pool, l):
        nc.gpsimd.memset(xg[:, :], 0.0).then_inc(s_xz, 1)
        settled(pool, s_xz, l + 1)
        if l == 0:
            pool.sem_inc(s_yfree, 1)

        before = counts.get((pool, 0), 0)
        if l == 0:
            pool.sem_inc(s_xtp, 1)
        settled(pool, s_xtp, before + l + 1)
        nc.gpsimd.tensor_copy(gidx[:, :], toktab[:, 0:1]).then_inc(s_idx, 1)
        settled(pool, s_idx, 2 * before + l + 1)
        pool.indirect_dma_start(xg[:, :], None, h2_d, bass.IndirectOffsetOnAxis(gidx[:, :], 0),
                                bounds_check=NTOK - 1, oob_is_err=False).then_inc(s_xg, 16)

        def body(b, B):
            settled(pool, s_xtp, B + l + 2)
            nc.gpsimd.tensor_copy(gidx[:, :], toktab[:, ds(b + 1, 1)]).then_inc(s_idx, 1)
            settled(pool, s_idx, 2 * B + l + 2)
            pool.indirect_dma_start(xg[:, :], None, h2_d, bass.IndirectOffsetOnAxis(gidx[:, :], 0),
                                    bounds_check=NTOK - 1, oob_is_err=False).then_inc(s_xg, 16)
            nc.gpsimd.tensor_copy(sidx[:, :], rowtab[:, ds(b, 1)]).then_inc(s_idx, 1)
            settled(pool, s_idx, 2 * B + l + 3)
            settled(pool, s_ya, B + 1)
            settled(pool, s_yd, B + 1)
            pool.indirect_dma_start(y_d, bass.IndirectOffsetOnAxis(sidx[:, :], 0), yo[:, :], None,
                                    bounds_check=2 * NTOK - 1, oob_is_err=False).then_inc(s_ys, 16)
            settled(pool, s_ys, 16 * B + 16)
            pool.sem_inc(s_yfree, 1)
        end = moe_loop(pool, l, body)
        settled(pool, s_xg, 16 * (end + l + 1))

    def pe_moe(pe, l):
        before = counts.get((pe, 0), 0)
        if l == 0:
            for s in (s_gup, s_upp, s_yb):
                pe.sem_inc(s, 2)

        def turn_x():
            for k in range(KD):
                ins = nc.tensor.transpose(psum[:, 3 + k // 4, (k % 4) * P:(k % 4 + 1) * P], xg[:, k * P:(k + 1) * P], ident)
            ins.then_inc(s_xtp, 1)
        pe.wait_ge(s_xg, 16 * (before + l + 1))
        turn_x()

        def body(b, B):
            par = b % 2
            pe.wait_ge(s_xta, B + l + 1)
            pe.wait_ge(s_xtd, B + l + 1)
            pe.wait_ge(s_g, 16 * B + 32)
            for k in range(KD):
                ins = nc.tensor.matmul(psum[:, 0, :], xT[:, k, :], wg[:, ds(par, 1), k, :].rearrange("p o n -> p (o n)"), start=(k == 0), stop=(k == KD - 1))
            ins.then_inc(s_gup, 1)
            pe.wait_ge(s_u, 16 * B + 32)
            for h in range(2):
                for k in range(KD):
                    ins = nc.tensor.matmul(psum[:, 1 + h, 0:256], xT[:, k, :], wu[:, ds(par, 1), k, h * 256:(h + 1) * 256].rearrange("p o n -> p (o n)"),
                                           start=(k == 0), stop=(k == KD - 1))
                if h == 0:
                    ins.then_inc(s_uph, 1)
            ins.then_inc(s_upp, 1)
            pe.wait_ge(s_xg, 16 * (B + l + 2))
            turn_x()
            for h in range(2):
                pe.wait_ge(s_hh, 2 * B + h + 1)
                for k in range(2):
                    ins = nc.tensor.transpose(psum[:, 5 if h == 0 else 1, k * P:(k + 1) * P], hh[:, (2 * h + k) * P:(2 * h + k + 1) * P], ident)
                ins.then_inc(s_ht, 1)
            pe.wait_ge(s_w2, 16 * B + 32)
            for h in range(2):
                pe.wait_ge(s_htd if h == 0 else s_hta, B + 1)
                for n in range(2):
                    for k in (2 * h, 2 * h + 1):
                        ins = nc.tensor.matmul(psum[:, 6 + n, :], hT2[:, k, :], w2[:, ds(par, 1), k, n * HALF:(n + 1) * HALF].rearrange("p o n -> p (o n)"),
                                               start=(k == 0), stop=(k == 3))
            ins.then_inc(s_yb, 1)
        moe_loop(pe, l, body)

    s_uph, s_yfree = sem("s_uph"), sem("s_yfree")

    def act_moe(act, l):
        before = counts.get((act, 0), 0)

        def take_x(B, n):
            act.wait_ge(s_xtp, n)
            nc.scalar.activation(xT[:, 0:4, :], psum[:, 3, :].rearrange("p (b n) -> p b n", b=4), ACT.Copy).then_inc(s_xta, 1)
        take_x(before, before + l + 2)

        def body(b, B):
            act.wait_ge(s_gup, B + 3)
            nc.scalar.activation(sg[:, :], psum[:, 0, :], ACT.Silu).then_inc(s_sil, 1)
            act.wait_ge(s_upp, B + 3)
            take_x(B, B + l + 3)
            act.wait_ge(s_ht, 2 * B + 2)
            nc.scalar.activation(hT2[:, 2:4, :], psum[:, 1, 0:256].rearrange("p (b n) -> p b n", b=2), ACT.Copy).then_inc(s_hta, 1)
            act.wait_ge(s_yb, B + 3)
            act.wait_ge(s_yfree, B + 1)
            nc.scalar.activation(yo[:, HALF:], psum[:, 7, :], ACT.Copy).then_inc(s_ya, 1)
        moe_loop(act, l, body)

    def dve_moe(dve, l):
        before = counts.get((dve, 0), 0)

        def take_x(n):
            dve.wait_ge(s_xtp, n)
            nc.vector.tensor_copy(xT[:, 4:8, :], psum[:, 4, :].rearrange("p (b n) -> p b n", b=4)).then_inc(s_xtd, 1)
        take_x(before + l + 2)

        def body(b, B):
            dve.wait_ge(s_sil, B + 1)
            for h in range(2):
                if h == 0:
                    dve.wait_ge(s_uph, B + 1)
                else:
                    dve.wait_ge(s_upp, B + 3)
                nc.vector.tensor_tensor(hh[:, h * 256:(h + 1) * 256], psum[:, 1 + h, 0:256], sg[:, h * 256:(h + 1) * 256], ALU.mult).then_inc(s_hh, 1)
            take_x(B + l + 3)
            dve.wait_ge(s_ht, 2 * B + 1)
            nc.vector.tensor_copy(hT2[:, 0:2, :], psum[:, 5, 0:256].rearrange("p (b n) -> p b n", b=2)).then_inc(s_htd, 1)
            dve.wait_ge(s_yb, B + 3)
            dve.wait_ge(s_yfree, B + 1)
            nc.vector.tensor_copy(yo[:, 0:HALF], psum[:, 6, :]).then_inc(s_yd, 1)
        moe_loop(dve, l, body)

    s_fin = [sem("s_fin0"), sem("s_fin1")]
    s_fx, s_fst, s_fg = sem("s_fx"), [sem("s_fst0"), sem("s_fst1")], sem("s_fg")
    A = Arena("last")
    fx = A("x", [P, 2, D])
    fy = A("y", [P, 2, 2, D])
    fu = A("u", [P, 2, D])
    fg = A("g", [P, D])
    fw = A("w", [P, 2, 2])

    def sp_last(sp):
        sp.dma_start(fg[:, :], mod_d[1, 0:1, 5 * D:].broadcast_to([P, D])).then_inc(s_fg, 16)
        sp.sem_inc(s_fst[0], 16)
        sp.sem_inc(s_fst[1], 16)

        def body(i):
            for par in range(2):
                t = 2 * i + par
                sp.wait_ge(s_fst[par], 16 * i + 16)
                sp.dma_start(fx[:, par], xs_d[ds(t * P, P), :]).then_inc(s_fin[par], 16)
                sp.dma_start(fy[:, par], y_d[ds(t * 2 * P, 2 * P), :].rearrange("(p c) n -> p c n", c=2)).then_inc(s_fin[par], 16)
        trips(sp, TX // 2, body)

    def dve_last(dve):
        dve.wait_ge(s_fg, 16)

        def body(i):
            for par in range(2):
                t = 2 * i + par
                dve.wait_ge(s_fin[par], 32 * (i + 1))
                dve_combine(dve, par, t, 0, fx[:, par], fy[:, par], fu[:, par], fw[:, par], fg[:, :]).then_inc(s_fx, 1)
        trips(dve, TX // 2, body, dvec, 8)

    def act_last(act):
        def body(i):
            for par in range(2):
                t = 2 * i + par
                act.wait_ge(s_fx, t + 1)
                act.dma_start(out[0, ds(t * P, P), :], fx[:, par]).then_inc(s_fst[par], 16)
        trips(act, TX // 2, body)
        for par in range(2):
            act.wait_ge(s_fst[par], 16 + 16 * (TX // 2))

    with nc.Block() as block:
        @block.sync
        def _(sp):
            sp_setup(sp)
            phase_end(sp)
            for l in range(2):
                for part in (sp_prep, sp_qkv, sp_att, sp_post):
                    part(sp, l)
                    phase_end(sp)
                phase_end(sp)
                sp_moe(sp, l)
                phase_end(sp)
            sp_last(sp)

        @block.gpsimd
        def _(pool):
            phase_end(pool)
            for l in range(2):
                for part in (pool_prep, pool_qkv, pool_att, pool_post):
                    part(pool, l)
                    phase_end(pool)
                phase_end(pool)
                pool_moe(pool, l)
                phase_end(pool)

        @block.tensor
        def _(pe):
            pe_setup(pe)
            phase_end(pe)
            for l in range(2):
                for part in (pe_prep, pe_qkv, pe_att, pe_post, pe_route, pe_moe):
                    part(pe, l)
                    phase_end(pe)

        @block.vector
        def _(dve):
            dve_setup(dve)
            phase_end(dve)
            for l in range(2):
                for part in (dve_prep, dve_qkv, dve_att, dve_post, dve_route, dve_moe):
                    part(dve, l)
                    phase_end(dve)
            dve_last(dve)

        @block.scalar
        def _(act):
            act_setup(act)
            phase_end(act)
            for l in range(2):
                for part in (act_prep, act_qkv, act_att, act_post, act_route, act_moe):
                    part(act, l)
                    phase_end(act)
            act_last(act)


_INS = ["x", "c", "ctx", "c_ctx", "ada_w", "ada_b", "norm1_g", "norm2_g", "a_wqkv", "a_wo", "a_q_norm", "a_k_norm",
        "a_lambda_q1", "a_lambda_k1", "a_lambda_q2", "a_lambda_k2", "a_subln_g", "b_wqkv", "b_wo", "b_q_norm",
        "b_k_norm", "b_sink", "r_w1", "r_b1", "r_w2", "r_b2", "e_w13", "e_w2"]


def constants():
    import numpy as np
    t = np.zeros((P, C_END), np.float32)
    i = np.arange(P)
    t[:, C_ID:C_ID + P] = np.eye(P)
    t[:, C_TRI:C_TRI + P] = i[:, None] < i[None, :]
    t[:, C_IOTA:C_IOTA + P] = i[None, :]
    t[:, C_PREV:C_PREV + P] = np.where(i[None, :] >= i[:, None], 0, -BIG)
    t[:, C_NEXT:C_NEXT + P] = np.where(i[None, :] <= i[:, None], 0, -BIG)
    grid_w, freqs = 64, HD // 4
    pos = np.arange(SEQ)
    inv = np.float32(10000.0) ** (-np.arange(freqs, dtype=np.float32) / np.float32(freqs))
    ang = np.stack([(pos // grid_w).astype(np.float32)[:, None] * inv, (pos % grid_w).astype(np.float32)[:, None] * inv], 1)
    cos, sin = np.cos(ang), np.sin(ang)
    full_c = np.ones((NTOK, 2, 2, freqs), np.float32)
    full_s = np.zeros((NTOK, 2, 2, freqs), np.float32)
    full_c[:SEQ] = cos[:, :, None, :]
    full_s[:SEQ, :, 0] = -sin
    full_s[:SEQ, :, 1] = sin
    t[:, C_COS:C_COS + TA * HD] = full_c.reshape(TA, P, HD).transpose(1, 0, 2).reshape(P, TA * HD)
    t[:, C_SIN:C_SIN + TA * HD] = full_s.reshape(TA, P, HD).transpose(1, 0, 2).reshape(P, TA * HD)
    t[:, C_TOK:C_TOK + TA] = 2 * (np.arange(TA)[None, :] * P + i[:, None]) + 1
    return t


def kernel(**inputs):
    import numpy as np
    import concourse.bacc as bacc
    from concourse.bass_utils import run_bass_kernel_spmd

    nc = bacc.Bacc("TRN2", target_bir_lowering=False, num_devices=1)
    arrays, args = {}, []
    for name in _INS:
        a = np.ascontiguousarray(inputs[name])
        arrays["in_" + name] = a
        args.append(nc.dram_tensor("in_" + name, a.shape, mybir.dt.from_np(a.dtype), kind="ExternalInput").ap())
    table = constants()
    arrays["in_consts"] = table
    args.append(nc.dram_tensor("in_consts", table.shape, F32, kind="ExternalInput").ap())
    args.append(nc.dram_tensor("out", (1, SEQ, D), F32, kind="ExternalOutput").ap())
    build(nc, *args)
    r = run_bass_kernel_spmd(nc, [arrays], core_ids=[0])
    return r.results[0]["out"]
```

```python
import math

import concourse.bass as bass
from concourse import mybir

F32 = mybir.dt.float32
BF16 = mybir.dt.bfloat16
F32R = mybir.dt.float32r
I32 = mybir.dt.int32
ALU = mybir.AluOpType
ACT = mybir.ActivationFunctionType
AX = mybir.AxisListType.X

P = 128
D = 1024
KD = D // P
SEQ, CTX = 1024, 256
TX, TC = SEQ // P, CTX // P
TA = TX + TC
NTOK = SEQ + CTX
HALF = 512
HD = 64
EPS = 1e-6
SCALE = HD ** -0.5
LAM_INIT = 0.8 - 0.6 * math.exp(-0.3 * 0)
NG, EPG = 4, 8
NE = NG * EPG
DE = 512
BIG = 1e30
NB_MAX = [2 * NTOK // P + NE, 2 * SEQ // P + NE]
NB_MIN = [2 * NTOK // P, 2 * SEQ // P]
NBT = NB_MAX[0] + 2
EMPTY = 1 << 20
TILES = [TA, TX]

C_ID, C_TRI, C_IOTA, C_PREV, C_NEXT = 0, 128, 256, 384, 512
C_COS, C_SIN = 640, 640 + TA * HD
C_TOK = C_SIN + TA * HD
C_END = C_TOK + TA


def build(nc, x, c, ctx, c_ctx, ada_w, ada_b, norm1_g, norm2_g, a_wqkv, a_wo, a_q_norm, a_k_norm,
          a_lambda_q1, a_lambda_k1, a_lambda_q2, a_lambda_k2, a_subln_g, b_wqkv, b_wo, b_q_norm,
          b_k_norm, b_sink, r_w1, r_b1, r_w2, r_b2, e_w13, e_w2, consts, out):
    ds = bass.ds
    nc.disable_value_cache = True

    def dram(name, shape):
        return nc.dram_tensor(name, shape, F32, kind="Internal").ap()

    mod_d = dram("mod_d", [2, 2, 6 * D])
    qk_d = dram("qk_d", [16, 2, P, NTOK])
    v_d = dram("v_d", [NTOK, 256])
    o_d = dram("o_d", [TA, P, D])
    xs_d = dram("xs_d", [NTOK, D])
    h2_d = dram("h2_d", [NTOK, D])
    y_d = dram("y_d", [2 * NTOK, D])

    def sb(name, shape, dt=F32):
        return nc.alloc_sbuf_tensor(name, shape, dt)

    cst = sb("cst", [P, C_END])
    ident = cst[:, C_ID:C_ID + P]
    tri = cst[:, C_TRI:C_TRI + P]
    iota = cst[:, C_IOTA:C_IOTA + P]
    tokrow = cst[:, C_TOK:C_TOK + TA]
    ones = sb("ones", [P, P])
    ident_h = sb("ident_h", [P, P], BF16)
    mask_h = sb("mask_h", [P, 2, 2, P], BF16)
    neghalf = sb("neghalf", [P, TA * 2])
    gains = sb("gains", [P, 4, HD])
    subg = sb("subg", [P, 1])
    lamv = sb("lamv", [P, 4, HD])
    lamw = sb("lamw", [P, 2, HD])
    lams = sb("lams", [P, 4])
    neglam = sb("neglam", [P, 1])
    sinks = sb("sinks", [P, 16])
    negsink = sb("negsink", [P, 16])
    wrt = sb("wrt", [P, 2, KD, NG + NE])
    brt = sb("brt", [P, 2, NG + NE])
    colw = sb("colw", [P, 40])
    mod_a = sb("mod_a", [P, 2, KD])
    mod_b = sb("mod_b", [P, 2, KD])
    logits = sb("logits", [P, TA, NG + NE])
    wsel = sb("wsel", [P, 2, TA])
    rowtab = sb("rowtab", [P, NBT], I32)
    toktab = sb("toktab", [P, NBT], I32)
    exptab = sb("exptab", [P, NBT], I32)
    blkcount = sb("blkcount", [P, 2], I32)
    arena0 = nc.sbuf_base
    arena0_at = (arena0 + 63) // 64 * 64
    limit = nc.sbuf_usable_end

    class Arena:

        def __init__(self, tag, at=None):
            self.tag, self.at = tag, at or arena0_at

        def __call__(self, name, shape, dt=F32):
            size = (4 if dt != BF16 else 2) * math.prod(shape[1:])
            t = nc.alloc_sbuf_tensor_at(f"{self.tag}_{name}", shape, dt, offset=self.at)
            self.at += (size + 63) // 64 * 64
            assert self.at <= limit, (self.tag, name, self.at, limit)
            return t

    psum = nc.alloc_psum_tensor("psum", [P, 8, HALF], F32)

    def sem(name):
        return nc.alloc_semaphore(name)

    s_phase = sem("s_phase")
    phases = {}

    def phase_end(eng):
        phases[eng] = phases.get(eng, 0) + 1
        eng.drain().then_inc(s_phase, 1)
        eng.wait_ge(s_phase, 5 * phases[eng])

    class Chain:

        def __init__(self, name):
            self.sem, self.base, self.n = sem(name), 0, 0

        def link(self, eng, ins):
            self.n += 1
            ins.then_inc(self.sem, 1)
            eng.wait_ge(self.sem, self.base + self.n)

        def trips(self, eng, n, body):
            if n == 1:
                return body(0)
            start, self.n = self.base + self.n, 0
            per = None
            with eng.Fori(0, n) as i:
                per = self.per_trip
                self.base, self.n = start + i * per, 0
                body(i)
                assert self.n == per, (self.n, per)
            self.base, self.n = start + n * per, 0

    dvec, actc, poolc = Chain("s_dve_chain"), Chain("s_act_chain"), Chain("s_pool_chain")

    def trips(eng, n, body, chain=None, links=0):
        if chain is None:
            if n == 1:
                return body(0)
            with eng.Fori(0, n) as i:
                body(i)
            return
        chain.per_trip = links
        chain.trips(eng, n, body)

    s_settled = sem("s_settled")

    def settled(eng, s, value):
        eng.wait_ge(s, value)
        if not isinstance(value, int):
            eng.sem_inc(s_settled, 1)

    s_const, s_small = sem("s_const"), sem("s_small")
    s_crow, s_ct, s_cs = sem("s_crow"), sem("s_ct"), sem("s_cs")
    s_adaw = [sem("s_adaw0"), sem("s_adaw1")]
    s_adaacc, s_adafree = sem("s_adaacc"), sem("s_adafree")
    s_adaput = [sem("s_adaput0"), sem("s_adaput1")]
    A = Arena("ada")
    crow = A("crow", [16, P])
    cs = A("cs", [P, 2, KD])
    adaw = A("w", [P, 2, KD, HALF])
    adab = A("b", [2, 2, HALF])
    adar = A("r", [2, 2, HALF])
    NCH = 6 * D // HALF
    SMALL = 0

    def sp_setup(sp):
        sp.dma_start(crow[0:8, :], c.rearrange("o (k p) -> (o k) p", p=P)).then_inc(s_crow, 16)
        sp.dma_start(crow[8:16, :], c_ctx.rearrange("(k p) -> k p", p=P)).then_inc(s_crow, 16)
        sp.dma_start(cst[:, :], consts).then_inc(s_const, 16)
        sp.sem_inc(s_adaw[0], 16)
        sp.sem_inc(s_adaw[1], 16)
        for l in range(2):
            wv = ada_w[l].rearrange("(k p) n -> p k n", p=P)

            def body(i):
                for par in range(2):
                    n = 2 * i + par
                    sp.wait_ge(s_adafree, l * NCH + n + 1)
                    sp.dma_start(adaw[:, par], wv[:, :, ds(n * HALF, HALF)]).then_inc(s_adaw[par], 16)
                    sp.dma_start(adab[:, par], ada_b[l:l + 1, ds(n * HALF, HALF)].broadcast_to([2, HALF])).then_inc(s_adaw[par], 16)

            trips(sp, NCH // 2, body)

    def act_small_loads(act):
        n = 0
        vecs = [(gains[:, 0], a_q_norm), (gains[:, 1], a_k_norm), (gains[:, 2], b_q_norm), (gains[:, 3], b_k_norm),
                (lamv[:, 0], a_lambda_q1), (lamv[:, 1], a_lambda_k1), (lamv[:, 2], a_lambda_q2),
                (lamv[:, 3], a_lambda_k2)]
        for dst, src in vecs:
            act.dma_start(dst, src.broadcast_to([P, HD])).then_inc(s_small, 16)
            n += 16
        act.dma_start(sinks[:, :], b_sink.broadcast_to([P, 16])).then_inc(s_small, 16)
        act.dma_start(subg[:, :], a_subln_g.rearrange("o e -> e o")).then_inc(s_small, 16)
        n += 32
        for l in range(2):
            act.dma_start(wrt[:, l, :, 0:NG], r_w1[l].rearrange("(k p) g -> p k g", p=P)).then_inc(s_small, 16)
            act.dma_start(brt[:, l, 0:NG], r_b1[l:l + 1, :].broadcast_to([P, NG])).then_inc(s_small, 16)
            act.dma_start(brt[:, l, NG:], r_b2[l:l + 1].rearrange("o g e -> o (g e)").broadcast_to([P, NE])).then_inc(s_small, 16)
            n += 48
            for g in range(NG):
                act.dma_start(wrt[:, l, :, NG + g * EPG:NG + (g + 1) * EPG],
                              r_w2[l, g].rearrange("(k p) e -> p k e", p=P)).then_inc(s_small, 16)
                n += 16
        return n

    n_small = 16 * (8 + 2 + 2 * (3 + NG))

    def act_setup(act):
        act.wait_ge(s_ct, 1)
        nc.scalar.activation(cs[:, :, :], psum[:, 0, 0:16].rearrange("p (s k) -> p s k", s=2), ACT.Silu).then_inc(s_cs, 1)
        assert act_small_loads(act) == n_small
        act.sem_inc(s_adaput[0], 16)
        act.sem_inc(s_adaput[1], 16)
        for l in range(2):
            def body(i):
                for par in range(2):
                    n = 2 * i + par
                    act.wait_ge(s_adafree, l * NCH + n + 3)
                    act.dma_start(mod_d[l, :, ds(n * HALF, HALF)], adar[:, par]).then_inc(s_adaput[par], 16)
            trips(act, NCH // 2, body)
        for par in range(2):
            act.wait_ge(s_adaput[par], 16 + 16 * NCH)
        act.wait_ge(s_lam, 1)
        nc.scalar.activation(lams[:, 2:4], lams[:, 0:2], ACT.Exp).then_inc(s_lam, 1)

    s_lam = sem("s_lam")

    def pe_setup(pe):
        pe.wait_ge(s_const, 16)
        pe.wait_ge(s_crow, 32)
        nc.tensor.transpose(psum[:, 0, 0:16], crow[:, :], ident[0:16, 0:16]).then_inc(s_ct, 1)
        pe.wait_ge(s_cs, 1)
        for l in range(2):
            def body(i):
                for par in range(2):
                    n = 2 * i + par
                    pe.wait_ge(s_adaw[par], 16 + 32 * (l * NCH // 2 + i + 1))
                    pe.wait_ge(s_adafree, l * NCH + n + 1)
                    for k in range(KD):
                        ins = nc.tensor.matmul(psum[0:2, 1 + par, :], cs[:, :, k], adaw[:, par, k], start=(k == 0), stop=(k == KD - 1))
                    ins.then_inc(s_adaacc, 1)
            trips(pe, NCH // 2, body)

    def dve_setup(dve):
        nc.vector.memset(ones[:, :], 1.0)
        dve.sem_inc(s_adafree, 2)
        nc.vector.memset(neghalf[:, :], -0.5)
        nc.vector.memset(blkcount[:, :], 0)
        for l in range(2):
            def body(i):
                for par in range(2):
                    n = 2 * i + par
                    dve.wait_ge(s_adaacc, l * NCH + n + 1)
                    dve.wait_ge(s_adaw[par], 16 + 32 * (l * NCH // 2 + i + 1))
                    dve.wait_ge(s_adaput[par], 16 + 16 * (l * NCH // 2 + i))
                    nc.vector.tensor_tensor(adar[:, par], psum[0:2, 1 + par, :], adab[:, par], ALU.add).then_inc(s_adafree, 1)
            trips(dve, NCH // 2, body)
        dve.wait_ge(s_const, 16)
        nc.vector.tensor_copy(ident_h[:, :], ident)
        dvec.link(dve, nc.vector.memset(mask_h[:, :, :, :], 0.0))
        nc.vector.tensor_copy(mask_h[:, 0, 0], cst[:, C_PREV:C_PREV + P])
        nc.vector.tensor_copy(mask_h[:, 1, 1], cst[:, C_NEXT:C_NEXT + P])
        dve.wait_ge(s_small, n_small)
        nc.vector.tensor_scalar(negsink[:, :], sinks[:, :], -1.0, None, ALU.mult)
        dvec.link(dve, nc.vector.tensor_scalar(subg[:, :], subg[:, :], 1.0 - LAM_INIT, None, ALU.mult))
        dvec.link(dve, nc.vector.tensor_tensor(lamw[:, :, :], lamv[:, 0:4:2], lamv[:, 1:4:2], ALU.mult))
        nc.vector.reduce_sum(lams[:, 0:2], lamw[:, :, :], AX).then_inc(s_lam, 1)
        dve.wait_ge(s_lam, 2)
        dvec.link(dve, nc.vector.tensor_tensor(neglam[:, :], lams[:, 3:4], lams[:, 2:3], ALU.subtract))
        dvec.link(dve, nc.vector.tensor_scalar(neglam[:, :], neglam[:, :], -LAM_INIT, None, ALU.add))

    s_cols, s_colt = sem("s_cols"), sem("s_colt")
    s_px = [sem("s_px0"), sem("s_px1")]
    s_pxfree, s_pss, s_prs = sem("s_pxfree"), sem("s_pss"), sem("s_prs")
    s_pxn, s_ptp, s_pta, s_ptd = sem("s_pxn"), sem("s_ptp"), sem("s_pta"), sem("s_ptd")
    s_pu = sem("s_pu")
    s_pst = [sem("s_pst0"), sem("s_pst1")]
    s_pg = sem("s_pg")
    Q = Arena("act")
    V = Q("V", [P, TA, D])
    after_V = Q.at
    hT = Q("hT", [P, KD, NTOK])
    after_hT = Q.at
    A = Arena("prep", after_hT)
    prow = A("row", [40, P])
    pxt = A("x", [P, 2, D])
    psq = A("sq", [P, 2, D])
    pxn = A("xn", [P, 2, D])
    pss = A("ss", [P, 2])
    prs = A("rs", [P, 2])
    py2 = A("y2", [P, 2, 2, D])
    pu = A("u", [P, 2, D])
    pg2 = A("g2", [P, D])
    pw = A("w", [P, 2, 2])

    def sources(l):
        if l == 0:
            return [(0, x[0], TX, 0, 0), (TX, ctx[0], TC, 1, 0)]
        return [(TA, xs_d[0:SEQ, :], TX, 0, 0), (TA + TX, xs_d[SEQ:, :], TC, 1, SEQ)]

    def sp_cols(sp, l):
        for s in range(2):
            sp.dma_start(prow[s * 16:s * 16 + 16, :], mod_d[l, s, 0:2 * D].rearrange("(r p) -> r p", p=P)).then_inc(s_cols, 16)
        sp.dma_start(prow[32:40, :], norm1_g[l].rearrange("(r p) -> r p", p=P)).then_inc(s_cols, 16)

    def pe_cols(pe, l):
        pe.wait_ge(s_cols, 48 * (l + 1))
        nc.tensor.transpose(psum[:, 0, 0:40], prow[:, :], ident[0:40, 0:40]).then_inc(s_colt, 1)

    def dve_cols(dve, l):
        dve.wait_ge(s_colt, 1 + 2 * l)
        dvec.link(dve, nc.vector.tensor_copy(colw[:, :], psum[:, 0, 0:40]))
        for s in range(2):
            nc.vector.tensor_copy(mod_b[:, s], colw[:, s * 16:s * 16 + 8])
            ins = nc.vector.scalar_tensor_tensor(mod_a[:, s], colw[:, s * 16 + 8:s * 16 + 16], 1.0, colw[:, 32:40], ALU.add, ALU.mult)
        ins.then_inc(s_colt, 1)
        dve.wait_ge(s_colt, 2 + 2 * l)

    def combine_part(T):
        return T >= TA

    def sp_prep(sp, l):
        sp_cols(sp, l)
        for T0, src, nt, s, r0 in sources(l):
            if l:
                sp.wait_ge(s_pxn, T0 + 2)
                sp.dma_start(pg2[:, :], mod_d[0, s:s + 1, 5 * D:].broadcast_to([P, D])).then_inc(s_pg, 16)

            def body(i):
                for par in range(2):
                    t = 2 * i + par
                    sp.wait_ge(s_pxfree, T0 + t + 1)
                    sp.dma_start(pxt[:, par], src[ds(t * P, P), :]).then_inc(s_px[par], 16)
                    if l:
                        sp.dma_start(py2[:, par], y_d[ds(2 * r0 + t * 2 * P, 2 * P), :].rearrange("(p c) n -> p c n", c=2)).then_inc(s_px[par], 16)
            trips(sp, nt // 2, body)

    def px_count(l, T0, i):
        return 16 * (T0 // 2 + i + 1) if l == 0 else 16 * (TA // 2) + 32 * (T0 // 2 - TA // 2 + i + 1)

    def act_prep(act, l):
        for T0, src, nt, s, r0 in sources(l):
            def body(i):
                for par in range(2):
                    t = 2 * i + par
                    T = T0 + t
                    if l == 0:
                        act.wait_ge(s_px[par], px_count(l, T0, i))
                    else:
                        act.wait_ge(s_pu, T - TA + 1)
                        act.dma_start(xs_d[ds(r0 + t * P, P), :], pxt[:, par]).then_inc(s_pst[par], 16)
                    act.wait_ge(s_pxn, T + 1)
                    nc.scalar.activation(psq[:, par], pxt[:, par], ACT.Square, scale=1 / 32, accum_out=pss[:, par:par + 1]).then_inc(s_pss, 1)
                for par in range(2):
                    t = 2 * i + par
                    act.wait_ge(s_ptp, T0 + t + 1)
                    for k in range(4):
                        ins = nc.scalar.activation(hT[:, k, ds(t * P + s * SEQ, P)], psum[:, 2 * par, k * P:(k + 1) * P], ACT.Identity,
                                                   bias=mod_b[:, s, k:k + 1], scale=mod_a[:, s, k:k + 1])
                    ins.then_inc(s_pta, 1)
            act.wait_ge(s_colt, 2 + 2 * l)
            trips(act, nt // 2, body)
        if l:
            for par in range(2):
                act.wait_ge(s_pst[par], 16 * (TA // 2))

    def pool_rstd(pool, dst, src, half, ready, request):
        settled(pool, *request)
        poolc.link(pool, nc.gpsimd.tensor_scalar(src, src, EPS, None, ALU.add))
        nc.gpsimd.tensor_tensor(dst, src, half, ALU.pow).then_inc(ready, 1)

    def pool_prep(pool, l):
        for T0, src, nt, s, r0 in sources(l):
            def body(i):
                for par in range(2):
                    T = T0 + 2 * i + par
                    pool_rstd(pool, prs[:, par:par + 1], pss[:, par:par + 1], neghalf[:, 0:1], s_prs, (s_pss, T + 1))
            trips(pool, nt // 2, body, poolc, 2)

    def dve_combine(dve, par, t, s, xt, yt, ut, wt, g2, done=None):
        dvec.link(dve, nc.vector.tensor_copy(wt, wsel[:, :, ds(t + s * TX, 1)].rearrange("p c o -> p (c o)")))
        dvec.link(dve, nc.vector.tensor_scalar(ut, yt[:, 0], wt[:, 0:1], None, ALU.mult))
        dvec.link(dve, nc.vector.scalar_tensor_tensor(ut, yt[:, 1], wt[:, 1:2], ut, ALU.mult, ALU.add))
        dvec.link(dve, nc.vector.tensor_tensor(ut, ut, g2, ALU.mult))
        return nc.vector.tensor_tensor(xt, xt, ut, ALU.add)

    def dve_prep(dve, l):
        if l == 0:
            dve.sem_inc(s_pxfree, 2)
            dve.sem_inc(s_ptd, 2)
        dve_cols(dve, l)
        for T0, src, nt, s, r0 in sources(l):
            if l:
                dve.wait_ge(s_pg, 16 * (s + 1))
            def body(i):
                for par in range(2):
                    t = 2 * i + par
                    T = T0 + t
                    dve.wait_ge(s_px[par], px_count(l, T0, i))
                    if l:
                        dve_combine(dve, par, t, s, pxt[:, par], py2[:, par], pu[:, par], pw[:, par], pg2[:, :]).then_inc(s_pu, 1)
                for par in range(2):
                    t = 2 * i + par
                    T = T0 + t
                    dve.wait_ge(s_prs, T + 1)
                    nc.vector.tensor_scalar(pxn[:, par], pxt[:, par], prs[:, par:par + 1], None, ALU.mult).then_inc(s_pxn, 1)
                    if l:
                        dve.wait_ge(s_pst[par], 16 * (T0 // 2 - TA // 2 + i + 1))
                    dve.wait_ge(s_pxn, T + 3)
                    dve.sem_inc(s_pxfree, 1)
                for par in range(2):
                    t = 2 * i + par
                    dve.wait_ge(s_ptp, T0 + t + 1)
                    for k in range(4, 8):
                        ins = nc.vector.tensor_scalar(hT[:, k, ds(t * P + s * SEQ, P)], psum[:, 2 * par + 1, (k - 4) * P:(k - 3) * P],
                                                      mod_a[:, s, k:k + 1], mod_b[:, s, k:k + 1], ALU.mult, ALU.add)
                    ins.then_inc(s_ptd, 1)
            if l == 0 and T0 == 0:
                dve.sem_inc(s_pxn, 2)
            trips(dve, nt // 2, body, dvec, 8 if l else 0)

    def pe_prep(pe, l):
        pe_cols(pe, l)
        pe.wait_ge(s_colt, 2 + 2 * l)
        if l == 0:
            pe.sem_inc(s_pta, 2)
        for T0, src, nt, s, r0 in sources(l):
            def body(i):
                for par in range(2):
                    T = T0 + 2 * i + par
                    pe.wait_ge(s_pxn, T + 3)
                    pe.wait_ge(s_pta, T + 1)
                    pe.wait_ge(s_ptd, T + 1)
                    for k in range(KD):
                        ins = nc.tensor.transpose(psum[:, 2 * par + k // 4, (k % 4) * P:(k % 4 + 1) * P], pxn[:, par, k * P:(k + 1) * P], ident)
                    ins.then_inc(s_ptp, 1)
            trips(pe, nt // 2, body)

    s_qw = [sem("s_qw0"), sem("s_qw1")]
    s_qwfree, s_qacc, s_qaccfree = sem("s_qwfree"), sem("s_qacc"), sem("s_qaccfree")
    s_qsq, s_qms, s_qrs, s_qxn, s_qt2 = sem("s_qsq"), sem("s_qms"), sem("s_qrs"), sem("s_qxn"), sem("s_qt2")
    s_qrot, s_qtr, s_qev = sem("s_qrot"), sem("s_qtr"), sem("s_qev")
    s_qst = [sem("s_qst0"), sem("s_qst1")]
    s_qhi = sem("s_qhi")
    s_vev, s_vst = sem("s_vev"), sem("s_vst")
    s_rope = sem("s_rope")
    A = Arena("qkv", Q.at)
    qw = A("w", [P, 2, KD, HALF])
    rope = A("rope", [P, 2, 2, TA, HD])
    qsq = A("sq", [P, 2, HALF])
    qms = A("ms", [P, 2, 8])
    qrs = A("rs", [P, 2, 8])
    qxn = A("xn", [P, 2, HALF])
    qt1 = A("t1", [P, 2, HALF])
    qt2 = A("t2", [P, 2, HALF])
    qrot = A("rot", [P, 2, HALF])
    qstg = A("stg", [P, 2, 2, 4, P], F32R)
    vstg = A("vstg", [P, TA, 256])

    SECTIONS = [
        [(2, 2, TA, "qk", 8, 0, 0, 0), (1, 2, TA, "v", 0, 40, 40, 4)],
        [(1, 2, TX, "qk", 8, 60, 40, 6), (1, 1, TA, "kv", 4, 76, 56, 8)],
    ]
    WQKV = [a_wqkv[0], b_wqkv[0]]

    def sp_qkv(sp, l):
        wv = WQKV[l].rearrange("(k p) n -> p k n", p=P)

        def load(C, par, col):
            sp.wait_ge(s_qwfree, C + 1)
            sp.dma_start(qw[:, par], wv[:, :, ds(col, HALF)]).then_inc(s_qw[par], 16)

        def pair(i):
            load(2 * i, 0, 2 * i * HALF)
            load(2 * i + 1, 1, (2 * i + 1) * HALF)
        if l == 0:
            trips(sp, 3, pair)
        else:
            for n in range(3):
                load(6 + n, n % 2, n * HALF)
            for t in range(TA):
                sp.wait_ge(s_vev, t + 1)
                sp.dma_start(v_d[t * P:(t + 1) * P, :], vstg[:, t, :]).then_inc(s_vst, 16)
            sp.wait_ge(s_vst, 16 * TA)

    def pe_qkv(pe, l):
        if l == 0:
            pe.sem_inc(s_qwfree, 2)
        for ntrip, nch, nt, kind, heads, U0, R0, C0 in SECTIONS[l]:
            def body(i):
                def transposes(j):
                    R = R0 + nch * nt * i + j
                    pe.wait_ge(s_qrot, R + 1)
                    pe.wait_ge(s_qev, R + 1)
                    for b in range(heads // 2):
                        ins = nc.tensor.transpose(psum[:, 2 + j % 2, b * P:(b + 1) * P], qrot[:, j % 2, b * P:(b + 1) * P], ident)
                    ins.then_inc(s_qtr, 1)
                for ci in range(nch):
                    C = C0 + nch * i + ci
                    pe.wait_ge(s_qw[ci % 2], 16 * (C0 // 2 + i + 1))
                    for t in range(nt):
                        j = ci * nt + t
                        U = U0 + nch * nt * i + j
                        pe.wait_ge(s_qaccfree, U + 1)
                        for k in range(KD):
                            ins = nc.tensor.matmul(psum[:, j % 2, :], hT[:, k, t * P:(t + 1) * P], qw[:, ci % 2, k], start=(k == 0), stop=(k == KD - 1))
                        ins.then_inc(s_qacc, 1)
                        if t == nt - 1:
                            pe.wait_ge(s_qacc, U + 1)
                            pe.sem_inc(s_qwfree, 1)
                        if heads and j:
                            transposes(j - 1)
                if heads:
                    transposes(nch * nt - 1)
            trips(pe, ntrip, body)

    def act_qkv(act, l):
        if l == 0:
            act.sem_inc(s_qaccfree, 2)
            act.sem_inc(s_qst[0], 16)
            act.sem_inc(s_qst[1], 16)
        for ntrip, nch, nt, kind, heads, U0, R0, C0 in SECTIONS[l]:
            def body(i):
                def evac(j):
                    R = R0 + nch * nt * i + j
                    nb = heads // 2
                    act.wait_ge(s_qtr, R + 3)
                    act.wait_ge(s_qst[j % 2], 32 * ((R0 + nch * nt * i) // 2 + j // 2) + 16)
                    nc.scalar.activation(qstg[:, j % 2, 0, 0:nb], psum[:, 2 + j % 2, 0:nb * P].rearrange("p (b n) -> p b n", b=nb), ACT.Copy).then_inc(s_qhi, 1)
                    act.wait_ge(s_qev, R + 3)
                    q0 = (C0 - 6 * l + nch * i + j // nt) * 4
                    for part in range(2):
                        act.dma_start(qk_d[ds(q0, nb), part, :, (j % nt) * P:(j % nt + 1) * P].rearrange("h p n -> p h n"), qstg[:, j % 2, part, 0:nb].bitcast(F32)).then_inc(s_qst[j % 2], 16)
                for j in range(nch * nt):
                    U = U0 + nch * nt * i + j
                    act.wait_ge(s_qacc, U + 1)
                    if kind == "v":
                        nc.scalar.activation(V[:, j % nt, (j // nt) * HALF:(j // nt + 1) * HALF], psum[:, j % 2, :], ACT.Copy).then_inc(s_qaccfree, 1)
                    if kind == "kv":
                        nc.scalar.activation(vstg[:, j, :], psum[:, j % 2, 256:512], ACT.Copy).then_inc(s_vev, 1)
                    if heads:
                        nc.scalar.activation(qsq[:, j % 2, 0:heads * HD], psum[:, j % 2, 0:heads * HD], ACT.Square, scale=1 / 8).then_inc(s_qsq, 1)
                        if j:
                            evac(j - 1)
                if heads:
                    evac(nch * nt - 1)
            trips(act, ntrip, body)
        for par in range(2):
            act.wait_ge(s_qst[par], 16 + 32 * [40, 66][l] // 2)

    def pool_qkv(pool, l):
        settled(pool, s_rope, l + 1)
        for ntrip, nch, nt, kind, heads, U0, R0, C0 in SECTIONS[l]:
            if not heads:
                continue

            def body(i):
                which = i if l == 0 else int(kind == "kv")
                for j in range(nch * nt):
                    R = R0 + nch * nt * i + j
                    t, par = j % nt, j % 2
                    pool_rstd(pool, qrs[:, par, 0:heads], qms[:, par, 0:heads], neghalf[:, 0:heads], s_qrs, (s_qms, R + 1))
                    settled(pool, s_qxn, R + 1)
                    src = qxn[:, par, 0:heads * HD].rearrange("p (h a b f) -> p h a b f", a=2, b=2, f=16)
                    dst = qt2[:, par, 0:heads * HD].rearrange("p (h a b f) -> p h a b f", a=2, b=2, f=16)
                    for b in range(2):
                        for a in range(2):
                            o = a * 32 + b * 16
                            if isinstance(which, int):
                                sn = rope[:, which, 1, t, o:o + 16].unsqueeze(1).broadcast_to([P, heads, 16])
                            else:
                                sn = rope[:, ds(which, 1), 1, t, o:o + 16].broadcast_to([P, heads, 16])
                            ins = nc.gpsimd.tensor_tensor(dst[:, :, a, b, :], src[:, :, a, 1 - b, :], sn, ALU.mult)
                    ins.then_inc(s_qt2, 1)
            trips(pool, ntrip, body, poolc, nch * nt)

    def dve_qkv(dve, l):
        dvec.link(dve, nc.vector.tensor_scalar(gains[:, 2 * l], gains[:, 2 * l], SCALE, None, ALU.mult))
        for w in range(2):
            g = gains[:, 2 * l + w]
            gs = g.rearrange("p (a b f) -> p a b f", a=2, b=2)
            nc.vector.tensor_tensor(rope[:, w, 0], cst[:, C_COS:C_COS + TA * HD].rearrange("p (t d) -> p t d", d=HD),
                                    g.unsqueeze(1).broadcast_to([P, TA, HD]), ALU.mult)
            sn = cst[:, C_SIN:C_SIN + TA * HD].rearrange("p (t a b f) -> p t a b f", a=2, b=2, f=16)
            dst = rope[:, w, 1].rearrange("p t (a b f) -> p t a b f", a=2, b=2)
            for a in range(2):
                for b in range(2):
                    ins = nc.vector.tensor_tensor(dst[:, :, a, b, :], sn[:, :, a, b, :],
                                                  gs[:, a, 1 - b, :].unsqueeze(1).broadcast_to([P, TA, 16]), ALU.mult)
        ins.then_inc(s_rope, 1)
        dve.wait_ge(s_rope, l + 1)
        for ntrip, nch, nt, kind, heads, U0, R0, C0 in SECTIONS[l]:
            if not heads:
                continue

            def body(i):
                which = i if l == 0 else int(kind == "kv")
                n = heads * HD

                def low(j):
                    R, m = R0 + nch * nt * i + j, heads // 2 * P
                    dve.wait_ge(s_qhi, R + 1)
                    nc.vector.tensor_tensor(qstg[:, j % 2, 1].rearrange("p b n -> p (b n)")[:, 0:m], psum[:, 2 + j % 2, 0:m],
                                            qstg[:, j % 2, 0].bitcast(F32).rearrange("p b n -> p (b n)")[:, 0:m], ALU.subtract).then_inc(s_qev, 1)
                for j in range(nch * nt):
                    R = R0 + nch * nt * i + j
                    t, par = j % nt, j % 2
                    dve.wait_ge(s_qsq, R + 1)
                    nc.vector.reduce_sum(qms[:, par, 0:heads], qsq[:, par, 0:n].rearrange("p (h d) -> p h d", d=HD), AX).then_inc(s_qms, 1)
                    if j:
                        low(j - 1)
                    dve.wait_ge(s_qrs, R + 1)
                    xn3 = qxn[:, par, 0:n].rearrange("p (h d) -> p h d", d=HD)
                    nc.vector.tensor_tensor(xn3, psum[:, par, 0:n].rearrange("p (h d) -> p h d", d=HD),
                                            qrs[:, par, 0:heads].unsqueeze(2).broadcast_to([P, heads, HD]), ALU.mult).then_inc(s_qxn, 1)
                    dve.wait_ge(s_qxn, R + 1)
                    dve.sem_inc(s_qaccfree, 1)
                    if isinstance(which, int):
                        cos = rope[:, which, 0, t].unsqueeze(1).broadcast_to([P, heads, HD])
                    else:
                        cos = rope[:, ds(which, 1), 0, t].broadcast_to([P, heads, HD])
                    t13 = qt1[:, par, 0:n].rearrange("p (h d) -> p h d", d=HD)
                    dvec.link(dve, nc.vector.tensor_tensor(t13, xn3, cos, ALU.mult))
                    dve.wait_ge(s_qt2, R + 1)
                    dve.wait_ge(s_qtr, R - 1 + 2)
                    nc.vector.tensor_tensor(qrot[:, par, 0:n], qt1[:, par, 0:n], qt2[:, par, 0:n], ALU.add).then_inc(s_qrot, 1)
                low(nch * nt - 1)
            if l == 0:
                dve.sem_inc(s_qtr, 2)
                dve.sem_inc(s_qev, 2)
            trips(dve, ntrip, body, dvec, nch * nt)


    s_kt = sem("s_kt")
    s_aq = [sem("s_aq0"), sem("s_aq1")]
    s_score, s_nmax, s_exp = sem("s_score"), sem("s_nmax"), sem("s_exp")
    s_mix, s_b6, s_b7, s_b6free, s_b7free = sem("s_mix"), sem("s_b6"), sem("s_b7"), sem("s_b6free"), sem("s_b7free")
    s_sumsq, s_fac, s_sinkexp = sem("s_sumsq"), sem("s_fac"), sem("s_sinkexp")
    s_ost = [sem("s_ost0"), sem("s_ost1")]
    s_turn, s_took = [sem(f"s_turn{n}") for n in range(3)], [sem(f"s_took{n}") for n in range(3)]
    s_av, s_raw, s_on, s_put = sem("s_av"), sem("s_raw"), sem("s_on"), sem("s_put")
    A = Arena("att0", after_V)
    kT = A("kT", [P, 2 * KD, NTOK], F32R)
    B = Arena("att1", arena0_at + 4 * KD * D)
    kc = B("kc", [P, 4, CTX], F32R)
    vc = B("vc", [P, TC, 256])
    kw = B("kw", [P, 2, 4, 3 * P], F32R)
    vw = B("vw", [P, 2, 3, 256])
    es = B("es", [P, 2, 2])
    A = Arena("att", max(A.at, B.at))
    aq = A("q", [P, 2, 2, 4, 2, P], F32R)
    prob = A("prob", [P, 4 * NTOK])
    aT = A("aT", [P, 2, 10, P])
    nmax = A("nmax", [P, 2, 2])
    mx = A("mx", [P, 2, 2])
    den = A("den", [P, 2, 2])
    rden = A("rden", [P, 2, 2])
    coef = A("coef", [P, 2, 1])
    epsum = A("epsum", [P, 2, 1])
    osq = A("osq", [P, 2, P])
    ssq = A("ssq", [P, 2, 1])
    fac = A("fac", [P, 2, 1])
    raw = A("raw", [P, 2, P])
    on = A("on", [P, 2, P])
    oTs = A("oTs", [P, 2, KD, P])
    KWID = CTX + 3 * P

    def probs(l, j, m, lo, hi):
        at = (2 * (j % 2) + m) * (KWID if l else NTOK)
        return prob[:, at + lo:at + hi]

    class Plan:

        def __init__(self, l, tiles, nblk, base):
            self.l, self.tiles, self.nblk, self.base = l, tiles, nblk, base
            self.use6, self.use7 = {}, {}
            n6 = n7 = 0
            for j in range(16):
                total = self.blocks(j)
                self.use6[j, "a"] = n6
                n6 += 1
                if total > 4:
                    self.use7[j, "b"] = n7
                    n7 += 1
                if total > 8:
                    self.use6[j, "c"] = n6
                    n6 += 1
                self.use7[j, "o"] = n7
                n7 += 1
            self.n6, self.n7 = n6, n7

        def blocks(self, j):
            return self.nblk[j // 8] * 2

    PARTS = []
    u6 = u7 = units = 0
    for l, ntrip, t0, kinds, nblk in [(0, TX // 2, 0, ("all", "all"), (10, 10)), (0, 1, TX, ("ctx", "ctx"), (2, 2)),
                                      (1, 1, 0, ("first", "last"), (4, 4)), (1, TX // 2 - 1, 1, ("mid", "mid"), (5, 5))]:
        plan = Plan(l, kinds, nblk, (u6, u7, units))
        PARTS.append((l, ntrip, t0, kinds, nblk, plan))
        units += 16 * ntrip
        if l:
            u6, u7 = u6 + ntrip * plan.n6, u7 + ntrip * plan.n7

    def tile_of(t0, kinds, i, par):
        return par * (TX - 1) if kinds[0] == "first" else t0 + 2 * i + par

    def at(plan, i):
        return plan.base[0] + i * plan.n6, plan.base[1] + i * plan.n7, plan.base[2] + i * 16

    def pair_no(plan, i):
        return plan.base[2] // 16 + i

    def win_no(plan, i):
        return pair_no(plan, i) - (PARTS[0][1] + PARTS[1][1])

    def sp_att(sp, l):
        def halves(dst, rows, cols, s, n_heads):
            for part in range(2):
                for m in range(2):
                    sp.dma_start(dst[64 * part:64 * part + 64, m:n_heads:2].bitcast(F32), qk_d[rows, part, 64 * m:64 * m + 64, cols].rearrange("h d n -> d h n")).then_inc(s, 16)
        if l == 0:
            halves(kT, slice(KD, 2 * KD), slice(0, NTOK), s_kt, 2 * KD)
        else:
            halves(kc, slice(8, 10), slice(SEQ, NTOK), s_kt, 4)
            sp.dma_start(vc[:, :, :], v_d[SEQ:, :].rearrange("(t p) n -> p t n", p=P)).then_inc(s_kt, 16)
        for pl, ntrip, t0, kinds, nblk, plan in PARTS:
            if pl != l:
                continue

            def body(i):
                for par in range(2):
                    t = tile_of(t0, kinds, i, par)
                    if l:
                        sp.wait_ge(s_winfree, 2 * win_no(plan, i) + par + 1)
                        lo = {"first": 0, "last": t - 1, "mid": t - 1}[kinds[par]]
                        w = {"first": 2, "last": 2, "mid": 3}[kinds[par]]
                        halves(kw[:, par, :, 0:w * P], slice(8, 10), ds(lo * P, w * P), s_win[par], 4)
                        sp.dma_start(vw[:, par, 0:w, :], v_d[ds(lo * P, w * P), :].rearrange("(b p) n -> p b n", p=P)).then_inc(s_win[par], 16)
                    for half in range(2):
                        sp.wait_ge(s_score, 8 * (4 * pair_no(plan, i) + 2 * par + half) + 8)
                        src = qk_d[4 * half:4 * half + 4, :, :, ds(t * P, P)]
                        for rows in range(2):
                            for m in range(2):
                                sp.dma_start(aq[64 * rows:64 * rows + 64, half, m].bitcast(F32).rearrange("d u x n -> d (u x) n"),
                                             src[:, :, 64 * m:64 * m + 64, :].rearrange("u x d n -> d (u x) n")).then_inc(s_aq[half], 16)
            trips(sp, ntrip, body)
        if l:
            load_wo(sp, l)

    def pool_att(pool, l):
        for pl, ntrip, t0, kinds, nblk, plan in PARTS:
            if pl != l or l:
                continue

            def body(i):
                u0 = at(plan, i)[2]
                for j in range(16):
                    settled(pool, s_fac, u0 + j + 1)
                    poolc.link(pool, nc.gpsimd.tensor_tensor(fac[:, j % 2], ssq[:, j % 2], neghalf[:, 0:1], ALU.pow))
                    settled(pool, s_turn[2], turn_no(plan, i) + j + 1)
                    nc.gpsimd.tensor_scalar(on[:, j % 2], raw[:, j % 2], fac[:, j % 2], None, ALU.mult).then_inc(s_on, 1)
            if t0 == 0:
                pool.sem_inc(s_on, 2)
            trips(pool, ntrip, body, poolc, 16)

    s_winfree, s_win = sem("s_winfree"), [sem("s_win0"), sem("s_win1")]

    def pe_att(pe, l):
        if l == 0:
            pe.sem_inc(s_winfree, 2)
            pe.sem_inc(s_score, 16)
        pe.wait_ge(s_kt, 64 if l == 0 else 144)
        for pl, ntrip, t0, kinds, nblk, plan in PARTS:
            if pl != l:
                continue

            def body(i):
                b6, b7, u0 = at(plan, i)

                def scores(j, m):
                    par, h, kind = j // 8, j % 8, kinds[j // 8]
                    if h % 4 == 0 and m == 0:
                        pe.wait_ge(s_aq[h // 4], 64 * (2 * pair_no(plan, i) + par + 1))
                    if l and h == 0 and m == 0:
                        pe.wait_ge(s_win[par], 80 * (win_no(plan, i) + 1))
                    pe.wait_ge(s_exp, 2 * (u0 + j) + m + 1)

                    def product(o, k, masked=None):
                        for x in range(2):
                            ins = nc.tensor.matmul(o, aq[:, h // 4, m, h % 4, x, :], k, start=x == 0, stop=x == 1 and masked is None)
                        if masked is not None:
                            ins = nc.tensor.matmul(o, ident_h[:, :], masked, start=False, stop=True)
                        return ins
                    if l == 0:
                        key = kT[:, 2 * h + m]
                        if kind == "all":
                            for b, (lo, hi) in enumerate(((0, 512), (512, 1024), (1024, 1280))):
                                ins = product(psum[:, 3 * m + b, 0:hi - lo], key[:, lo:hi])
                        else:
                            ins = product(psum[:, 3 * m, 0:CTX], key[:, SEQ:])
                    else:
                        g = h // 2
                        product(psum[:, 3 * m, 0:CTX], kc[:, g])
                        ins = product(psum[:, 3 * m, CTX:HALF], kw[:, par, g, 0:2 * P], mask_h[:, int(kind == "first")].rearrange("p b n -> p (b n)"))
                        if kind == "mid":
                            ins = product(psum[:, 3 * m + 1, 0:P], kw[:, par, g, 2 * P:3 * P], mask_h[:, 1, 1])
                    ins.then_inc(s_score, 1)

                scores(0, 0)
                scores(0, 1)
                if l == 0:
                    pe_units0(pe, plan, i, u0, kinds, nblk, scores)
                else:
                    pe_units1(pe, i, b6, b7, u0, nblk, plan, scores)
            trips(pe, ntrip, body)

    def turn_no(plan, i):
        return 17 * pair_no(plan, i)

    def pe_units0(pe, plan, i, u0, kinds, nblk, scores):
        t0 = turn_no(plan, i)

        def blocks(j, lo, hi, bank):
            for b in range(lo, hi):
                ins = nc.tensor.transpose(psum[:, bank, (b - lo) * P:(b - lo + 1) * P], probs(0, j, 0, b * P, (b + 1) * P), ident)
            return ins

        def turn_output(j, at):
            pe.wait_ge(s_on, u0 + j + 3)
            return nc.tensor.transpose(psum[:, 6, at * P:(at + 1) * P], on[:, j % 2], ident)

        def turn(j):
            nb = nblk[j // 8]
            pe.wait_ge(s_mix, u0 + j + 1)
            pe.wait_ge(s_took[2], t0 + j + 1)
            blocks(j, 0, min(4, nb), 6).then_inc(s_turn[0], 1)
            if nb > 4:
                pe.wait_ge(s_raw, u0 + j + 1)
                blocks(j, 4, 8, 7).then_inc(s_turn[1], 1)

        def turn_last(j):
            nb = nblk[j // 8]
            pe.wait_ge(s_took[0], u0 + j + 1)
            if nb > 8:
                ins = blocks(j, 8, nb, 6)
            if j >= 2:
                ins = turn_output(j - 2, 2)
            if nb > 8 or j >= 2:
                ins.then_inc(s_turn[2], 1)
            else:
                pe.sem_inc(s_turn[2], 1)

        def output(j):
            nb, h = nblk[j // 8], j % 8
            pe.wait_ge(s_took[0], u0 + j + 1)
            pe.wait_ge(s_raw, u0 + j + 1)
            if nb > 4:
                pe.wait_ge(s_took[1], u0 + j + 1)
            for b in range(nb):
                if b == 8:
                    pe.wait_ge(s_took[2], t0 + j + 2)
                v = V[:, b if kinds[j // 8] == "all" else TX + b, h * P:(h + 1) * P]
                ins = nc.tensor.matmul(psum[:, 7, 0:P], aT[:, j % 2, b, :], v, start=(b == 0), stop=(b == nb - 1))
            ins.then_inc(s_av, 1)

        scores(1, 0)
        scores(1, 1)
        for j in range(16):
            turn(j)
            if j < 14:
                scores(j + 2, 0)
            turn_last(j)
            output(j)
            if j < 14:
                scores(j + 2, 1)
        pe.wait_ge(s_took[2], t0 + 17)
        turn_output(14, 0)
        turn_output(15, 1).then_inc(s_turn[2], 1)

    def pe_units1(pe, i, b6, b7, u0, nblk, plan, scores):
        def turn(j, bank, lo, hi):
            for b in range(lo, hi):
                ins = nc.tensor.transpose(psum[:, bank, (b - lo) * P:(b - lo + 1) * P], probs(1, j, b % 2, b // 2 * P, (b // 2 + 1) * P), ident)
            ins.then_inc(s_b6 if bank == 6 else s_b7, 1)

        scores(1, 0)
        scores(1, 1)
        for j in range(16):
            par, g, nb = j // 8, j % 8 // 2, nblk[j // 8]
            total = plan.blocks(j)
            pe.wait_ge(s_mix, u0 + j + 1)
            pe.wait_ge(s_b6free, b6 + plan.use6[j, "a"] + 1)
            turn(j, 6, 0, 4)
            pe.wait_ge(s_b7free, b7 + plan.use7[j, "b"] + 1)
            turn(j, 7, 4, 8)
            if j < 14:
                scores(j + 2, 0)
            if total > 8:
                pe.wait_ge(s_b6free, b6 + plan.use6[j, "c"] + 1)
                turn(j, 6, 8, total)
            pe.wait_ge(s_b6free, b6 + plan.use6[j, "c" if total > 8 else "a"] + 2)
            pe.wait_ge(s_b7free, b7 + plan.use7[j, "o"] + 1)
            for b in range(nb):
                v = vc[:, b, g * HD:(g + 1) * HD] if b < TC else vw[:, par, b - TC, g * HD:(g + 1) * HD]
                ins = nc.tensor.matmul(psum[0:HD, 7, 0:2 * P], v, aT[:, j % 2, 2 * b:2 * b + 2, :].rearrange("p m n -> p (m n)"),
                                       start=(b == 0), stop=(b == nb - 1))
            ins.then_inc(s_b7, 1)
            if j < 14:
                scores(j + 2, 1)
            if j % 8 == 7:
                pe.wait_ge(s_b7, b7 + plan.use7[j, "o"] + 1)
                pe.sem_inc(s_winfree, 1)

    def act_att(act, l):
        for pl, ntrip, t0, kinds, nblk, plan in PARTS:
            if pl != l:
                continue

            def body(i):
                b6, b7, u0 = at(plan, i)

                def expo(j, m):
                    width = nblk[j // 8] * P
                    n = 2 * (u0 + j) + m
                    act.wait_ge(s_nmax, n + 1)
                    if l and j >= 2:
                        act.wait_ge(s_b7, b7 + plan.use7[j - 2, "b"] + 1)
                    nc.scalar.activation(probs(l, j, m, 0, width), psum[:, 3 * m:3 * m + 3, :].rearrange("p b n -> p (b n)")[:, 0:width], ACT.Exp,
                                         bias=nmax[:, j % 2, m:m + 1], accum_out=den[:, j % 2, m:m + 1]).then_inc(s_exp, 1)
                    if l:
                        h = 2 * (j % 8) + m
                        nc.scalar.activation(es[:, j % 2, m:m + 1], nmax[:, j % 2, m:m + 1], ACT.Exp, bias=sinks[:, h:h + 1]).then_inc(s_sinkexp, 1)

                def store(par):
                    act.dma_start(o_d[ds(tile_of(t0, kinds, i, par), 1)].rearrange("o p n -> p (o n)"),
                                  oTs[:, par].rearrange("p k n -> p (k n)")).then_inc(s_ost[par], 16)

                def take(j, bank, lo, hi, col=0):
                    return nc.scalar.activation(aT[:, j % 2, lo:hi, :], psum[:, bank, col:col + (hi - lo) * P].rearrange("p (b n) -> p b n", n=P), ACT.Copy)

                t2 = turn_no(plan, i)

                def square(j):
                    act.wait_ge(s_raw, u0 + j + 2)
                    nc.scalar.activation(osq[:, j % 2], raw[:, j % 2], ACT.Square, accum_out=ssq[:, j % 2]).then_inc(s_sumsq, 1)

                def put(j, at):
                    if j % 8 == 0:
                        act.wait_ge(s_ost[j // 8], 16 + 16 * pair_no(plan, i))
                    ins = nc.scalar.activation(oTs[:, j // 8, j % 8, :], psum[:, 6, at * P:(at + 1) * P], ACT.Copy, scale=subg[:, 0:1])
                    return ins

                def pieces0(j):
                    nb = nblk[j // 8]
                    act.wait_ge(s_turn[0], u0 + j + 1)
                    take(j, 6, 0, min(4, nb)).then_inc(s_took[0], 1)
                    if nb > 4:
                        act.wait_ge(s_turn[1], u0 + j + 1)
                        take(j, 7, 4, 8).then_inc(s_took[1], 1)

                def last_piece0(j):
                    nb = nblk[j // 8]
                    act.wait_ge(s_turn[2], t2 + j + 1)
                    if nb > 8:
                        ins = take(j, 6, 8, nb)
                    if j >= 2:
                        ins = put(j - 2, 2)
                    if nb > 8 or j >= 2:
                        ins.then_inc(s_took[2], 1)
                    else:
                        act.sem_inc(s_took[2], 1)
                    if j - 2 == 7:
                        act.wait_ge(s_took[2], t2 + j + 2)
                        store(0)

                def piece1(j):
                    act.wait_ge(s_b6, b6 + plan.use6[j, "a"] + 1)
                    take(j, 6, 0, 4).then_inc(s_b6free, 1)

                def last_piece1(j):
                    if (j, "c") in plan.use6:
                        act.wait_ge(s_b6, b6 + plan.use6[j, "c"] + 1)
                        take(j, 6, 8, plan.blocks(j)).then_inc(s_b6free, 1)

                expo(0, 0)
                expo(0, 1)
                if l:
                    expo(1, 0)
                for j in range(16):
                    if l == 0:
                        if j < 15:
                            expo(j + 1, 0)
                        if j:
                            square(j - 1)
                        pieces0(j)
                        if j < 15:
                            expo(j + 1, 1)
                        last_piece0(j)
                    else:
                        piece1(j)
                        if j < 15:
                            expo(j + 1, 1)
                        last_piece1(j)
                        if j < 14:
                            expo(j + 2, 0)
                        if j % 8 == 7:
                            act.wait_ge(s_b7free, b7 + plan.use7[j, "o"] + 2)
                            store(j // 8)
                if l == 0:
                    square(15)
                    act.wait_ge(s_turn[2], t2 + 17)
                    put(14, 0)
                    put(15, 1).then_inc(s_took[2], 1)
                    act.wait_ge(s_took[2], t2 + 18)
                    store(1)
            if l == 0 and t0 == 0:
                for s in s_ost:
                    act.sem_inc(s, 16)
                act.sem_inc(s_took[2], 1)
                act.sem_inc(s_b6free, 1)
                act.sem_inc(s_exp, 2)
            trips(act, ntrip, body)
        for par in range(2):
            act.wait_ge(s_ost[par], 16 + 16 * sum(p[1] for p in PARTS if p[0] <= l))

    def dve_att(dve, l):
        for pl, ntrip, t0, kinds, nblk, plan in PARTS:
            if pl != l:
                continue

            def body(i):
                b6, b7, u0 = at(plan, i)

                def peak(j, m):
                    width = nblk[j // 8] * P
                    score = psum[:, 3 * m:3 * m + 3, :].rearrange("p b n -> p (b n)")[:, 0:width]
                    dve.wait_ge(s_score, 2 * (u0 + j) + m + 1 + 16)
                    if l == 0:
                        nc.vector.reduce_max(nmax[:, j % 2, m:m + 1], score, AX, negate=True).then_inc(s_nmax, 1)
                    else:
                        h = 2 * (j % 8) + m
                        dvec.link(dve, nc.vector.reduce_max(mx[:, j % 2, m:m + 1], score, AX, negate=True))
                        nc.vector.tensor_tensor(nmax[:, j % 2, m:m + 1], mx[:, j % 2, m:m + 1], negsink[:, h:h + 1], ALU.min).then_inc(s_nmax, 1)

                def weigh(j):
                    width = nblk[j // 8] * P
                    q = j % 2
                    if l:
                        dve.wait_ge(s_sinkexp, 2 * (16 * win_no(plan, i) + j) + 2)
                        dvec.link(dve, nc.vector.tensor_tensor(rden[:, q], den[:, q], es[:, q], ALU.add))
                        dvec.link(dve, nc.vector.reciprocal(rden[:, q], rden[:, q]))
                        for m in range(2):
                            p = probs(l, j, m, 0, width)
                            ins = nc.vector.tensor_scalar(p, p, rden[:, q, m:m + 1], None, ALU.mult)
                        ins.then_inc(s_mix, 1)
                        return
                    dve.wait_ge(s_exp, 2 * (u0 + j) + 2 + 2)
                    dvec.link(dve, nc.vector.reciprocal(rden[:, q, 1:2], den[:, q, 1:2]))
                    nc.vector.scalar_tensor_tensor(epsum[:, q], den[:, q, 0:1], EPS, den[:, q, 0:1], ALU.mult, ALU.mult)
                    dvec.link(dve, nc.vector.scalar_tensor_tensor(coef[:, q], den[:, q, 0:1], neglam[:, 0:1], rden[:, q, 1:2], ALU.mult, ALU.mult))
                    nc.vector.scalar_tensor_tensor(probs(l, j, 0, 0, width), probs(l, j, 1, 0, width), coef[:, q], probs(l, j, 0, 0, width), ALU.mult, ALU.add).then_inc(s_mix, 1)

                def factor(j):
                    q = j % 2
                    dve.wait_ge(s_sumsq, u0 + j + 1)
                    nc.vector.scalar_tensor_tensor(ssq[:, q], ssq[:, q], 1 / P, epsum[:, q], ALU.mult, ALU.add).then_inc(s_fac, 1)

                def copy_output(j):
                    dve.wait_ge(s_av, u0 + j + 1)
                    dve.wait_ge(s_on, u0 + j + 1)
                    nc.vector.tensor_copy(raw[:, j % 2], psum[:, 7, 0:P]).then_inc(s_raw, 1)

                def piece1(j):
                    dve.wait_ge(s_b7, b7 + plan.use7[j, "b"] + 1)
                    nc.vector.tensor_copy(aT[:, j % 2, 4:8, :], psum[:, 7, :].rearrange("p (b n) -> p b n", n=P)).then_inc(s_b7free, 1)

                def finish1(j):
                    dve.wait_ge(s_b7, b7 + plan.use7[j, "o"] + 1)
                    if j % 8 == 0:
                        dve.wait_ge(s_ost[j // 8], 16 + 16 * pair_no(plan, i))
                    for m in range(2):
                        ins = nc.vector.tensor_copy(oTs[64 * m:64 * m + 64, j // 8, j % 8, :], psum[0:HD, 7, m * P:(m + 1) * P])
                    ins.then_inc(s_b7free, 1)

                peak(0, 0)
                peak(0, 1)
                if l:
                    peak(1, 0)
                    weigh(0)
                for j in range(16):
                    if l == 0:
                        if j < 15:
                            peak(j + 1, 0)
                        weigh(j)
                        if j:
                            copy_output(j - 1)
                        if j < 15:
                            peak(j + 1, 1)
                        if j:
                            factor(j - 1)
                    else:
                        if j < 15:
                            peak(j + 1, 1)
                        piece1(j)
                        if j < 14:
                            peak(j + 2, 0)
                        if j < 15:
                            weigh(j + 1)
                        finish1(j)
                if l == 0:
                    copy_output(15)
                    factor(15)
            if l == 0 and t0 == 0:
                dve.sem_inc(s_b7free, 1)
                dve.sem_inc(s_raw, 1)
            trips(dve, ntrip, body, dvec, 16 * (2 + 2 * l))

    s_pw = [sem("s_pw0"), sem("s_pw1")]
    s_pin = [sem("s_pin0"), sem("s_pin1")]
    s_pinfree, s_y, s_x1, s_x1ss, s_x1rs, s_h, s_h2 = [sem(n) for n in ("s_pinfree", "s_y", "s_x1", "s_x1ss", "s_x1rs", "s_h", "s_h2")]
    s_h2t, s_h2ta, s_h2td, s_rl, s_rld = [sem(n) for n in ("s_h2t", "s_h2ta", "s_h2td", "s_rl", "s_rld")]
    s_x1st = [sem("s_x1st0"), sem("s_x1st1")]
    s_h2st = [sem("s_h2st0"), sem("s_h2st1")]
    s_bc, s_bcd = [sem("s_bc0"), sem("s_bc1")], sem("s_bcd")
    A = Arena("post")
    wo = A("wo", [P, KD, D])
    bc = A("bc", [P, 2, 4, D])
    oT = A("oT", [P, 2, KD, P])
    xt = A("xt", [P, 2, D])
    x1 = A("x1", [P, 2, D])
    xsq = A("sq", [P, 2, D])
    xss = A("ss", [P, 2])
    xrs = A("rs", [P, 2])
    hm = A("hm", [P, 2, D])
    h2 = A("h2", [P, 2, D])
    h2T = A("h2T", [P, 2, KD, P])

    def post_steps(eng, l, step, chain=None, links=0):
        step(0, 0)
        step(1, 1)

        def body(i):
            for par in range(2):
                step(2 * i + 2 + par, par)
        trips(eng, TX // 2 - 1, body, chain, 2 * links)
        for t in range(TX, TILES[l]):
            step(t, t % 2)

    def load_wo(sp, l):
        for n in range(2):
            sp.dma_start(wo[:, :, n * HALF:(n + 1) * HALF], [a_wo, b_wo][l][0, :, n * HALF:(n + 1) * HALF].rearrange("(k p) n -> p k n", p=P)).then_inc(s_pw[n], 16)

    def sp_post(sp, l):
        def step(t, par):
            T = TA * l + t
            if l:
                src = xs_d[ds(t * P, P), :]
            else:
                src = ctx[0, (t - TX) * P:(t - TX + 1) * P, :] if isinstance(t, int) and t >= TX else x[0, ds(t * P, P), :]
            sp.wait_ge(s_pinfree, T + 1)
            sp.dma_start(oT[:, par].rearrange("p k n -> p (k n)"), o_d[ds(t, 1)].rearrange("o p n -> p (o n)")).then_inc(s_pin[par], 16)
            sp.dma_start(xt[:, par], src).then_inc(s_pin[par], 16)
            if l == 0 and isinstance(t, int) and t == 0:
                load_wo(sp, l)
        post_steps(sp, l, step)

    def pin_count(T, par):
        return 16 * (T - par + 2)

    def pe_post(pe, l):
        def turn(T, par):
            pe.wait_ge(s_h2, T + 1)
            pe.wait_ge(s_h2ta, T + 1)
            pe.wait_ge(s_h2td, T + 1)
            for k in range(KD):
                ins = nc.tensor.transpose(psum[:, 4 + k // 4, (k % 4) * P:(k % 4 + 1) * P], h2[:, par, k * P:(k + 1) * P], ident)
            ins.then_inc(s_h2t, 1)

        def route(T, par):
            pe.wait_ge(s_h2ta, T + 2)
            pe.wait_ge(s_h2td, T + 2)
            pe.wait_ge(s_rld, T + 1)
            for k in range(KD):
                ins = nc.tensor.matmul(psum[:, 6 + par, 0:NG + NE], h2T[:, par, k, :], wrt[:, l, k, :], start=(k == 0), stop=(k == KD - 1))
            ins.then_inc(s_rl, 1)

        def step(t, par):
            T = TA * l + t
            first = isinstance(t, int) and t < 2
            pe.wait_ge(s_pin[par], pin_count(T, par))
            pe.wait_ge(s_x1, T + 1)
            for n in range(2):
                if first:
                    pe.wait_ge(s_pw[n], 16 * (l + 1))
                for k in range(KD):
                    ins = nc.tensor.matmul(psum[:, 2 * par + n, :], oT[:, par, k, :], wo[:, k, n * HALF:(n + 1) * HALF], start=(k == 0), stop=(k == KD - 1))
                if n == 0 and not first:
                    route(T - 2, par)
            ins.then_inc(s_y, 1)
            if not (first and t == 0):
                turn(T - 1, 1 - par)
        if l == 0:
            pe.sem_inc(s_pinfree, 2)
        post_steps(pe, l, step)
        T = TA * l + TILES[l]
        route(T - 2, 0)
        turn(T - 1, 1)
        route(T - 1, 1)

    def dve_post(dve, l):
        if l == 0:
            dve.sem_inc(s_x1, 2)
            dve.sem_inc(s_rld, 2)
            dve.sem_inc(s_h2td, 1)

        def upper(T, par):
            dve.wait_ge(s_h2t, T + 1)
            nc.vector.tensor_copy(h2T[:, par, 4:8, :], psum[:, 5, :].rearrange("p (b n) -> p b n", b=4)).then_inc(s_h2td, 1)

        def logit(t, par):
            T = TA * l + t
            dve.wait_ge(s_rl, T + 1)
            nc.vector.tensor_tensor(logits[:, ds(t, 1), :].rearrange("p o n -> p (o n)"), psum[:, 6 + par, 0:NG + NE], brt[:, l, :], ALU.add).then_inc(s_rld, 1)

        def step(t, par):
            T = TA * l + t
            s = int(isinstance(t, int) and t >= TX)
            begin = isinstance(t, int) and t in (0, TX)
            if begin:
                dve.wait_ge(s_bc[s], 64 * (1 + l))
                nc.vector.scalar_tensor_tensor(bc[:, s, 2], bc[:, s, 2], 1.0, bc[:, s, 3], ALU.add, ALU.mult).then_inc(s_bcd, 1)
            dve.wait_ge(s_pin[par], pin_count(T, par))
            dve.wait_ge(s_y, T + 1)
            dve.wait_ge(s_x1st[par], 8 * (T - par + 2))
            y = psum[:, 2 * par:2 * par + 2, :].rearrange("p b n -> p (b n)")
            dvec.link(dve, nc.vector.tensor_tensor(x1[:, par], y, bc[:, s, 0], ALU.mult))
            dvec.link(dve, nc.vector.tensor_tensor(x1[:, par], x1[:, par], xt[:, par], ALU.add))
            dve.sem_inc(s_x1, 1)
            dve.sem_inc(s_pinfree, 1)
            later = not (isinstance(t, int) and t == 0)
            if later:
                upper(T - 1, 1 - par)
            if begin:
                dve.wait_ge(s_bcd, 1 + s + 2 * l)
            dve.wait_ge(s_x1rs, T + 1)
            nc.vector.scalar_tensor_tensor(hm[:, par], x1[:, par], xrs[:, par:par + 1], bc[:, s, 2], ALU.mult, ALU.mult).then_inc(s_h, 1)
            if later:
                logit(t - 1, 1 - par)
        post_steps(dve, l, step, dvec, 2)
        upper(TA * l + TILES[l] - 1, 1)
        logit(TILES[l] - 1, 1)

    def act_post(act, l):
        if l == 0:
            for s in s_x1st + s_h2st:
                act.sem_inc(s, 16)
            act.sem_inc(s_h2ta, 1)
        for s in range(2 - l):
            for n, src in enumerate([mod_d[l, s:s + 1, 2 * D:3 * D], mod_d[l, s:s + 1, 3 * D:4 * D],
                                     mod_d[l, s:s + 1, 4 * D:5 * D], norm2_g[l:l + 1, :]]):
                act.dma_start(bc[:, s, n], src.broadcast_to([P, D])).then_inc(s_bc[s], 16)

        def lower(t, par):
            T = TA * l + t
            act.wait_ge(s_h2t, T + 1)
            nc.scalar.activation(h2T[:, par, 0:4, :], psum[:, 4, :].rearrange("p (b n) -> p b n", b=4), ACT.Copy).then_inc(s_h2ta, 1)
            act.dma_start(h2_d[ds(t * P, P), :], h2[:, par]).then_inc(s_h2st[par], 16)

        def step(t, par):
            T = TA * l + t
            act.wait_ge(s_x1, T + 3)
            nc.scalar.activation(xsq[:, par], x1[:, par], ACT.Square, scale=1 / 32, accum_out=xss[:, par:par + 1]).then_inc(s_x1ss, 1)
            act.dma_start(xs_d[ds(t * P, P), :], x1[:, par]).then_inc(s_x1st[par], 16)
            if not (isinstance(t, int) and t == 0):
                lower(t - 1, 1 - par)
        post_steps(act, l, step)
        lower(TILES[l] - 1, 1)
        for s in s_x1st + s_h2st:
            act.wait_ge(s, 16 + 16 * (TA // 2 if l == 0 else (TA + TX) // 2))

    def pool_post(pool, l):
        def step(t, par):
            T = TA * l + t
            s = int(isinstance(t, int) and t >= TX)
            pool_rstd(pool, xrs[:, par:par + 1], xss[:, par:par + 1], neghalf[:, 0:1], s_x1rs, (s_x1ss, T + 1))
            settled(pool, s_h, T + 1)
            settled(pool, s_h2st[par], 8 * (T - par + 2))
            nc.gpsimd.tensor_tensor(h2[:, par], hm[:, par], bc[:, s, 1], ALU.add).then_inc(s_h2, 1)
        post_steps(pool, l, step, poolc, 1)

    s_rt, s_rta, s_rtp, s_rtm = sem("s_rt"), sem("s_rta"), sem("s_rtp"), sem("s_rtm")
    A = Arena("route")
    rg = A("rg", [P, TA, 8, NG])
    ru = A("ru", [P, TA, 16])
    re = A("re", [P, TA, 8, NE])
    pre = A("pre", [P, TA, NE])
    tot = A("tot", [P, NE])
    er = A("er", [P, 8, NE])
    eri = A("eri", [P, 2, NE], I32)
    sli = A("sli", [P, 2, TA], I32)
    slf = A("slf", [P, 6, TA])
    cmp_ = A("cmp", [P, NBT, NE])
    ebf = A("ebf", [P, NBT])
    lane1 = A("lane1", [P, 2, TA, P])
    blk1 = A("blk1", [P, 2, TA, NBT])
    tabf = A("tabf", [P, 2, NBT])

    def dve_route(dve, l):
        nt = TILES[l]
        V_ = nc.vector
        L = lambda ins: dvec.link(dve, ins)

        def pick(val, width, eq, code, top, code_top, one):
            L(V_.reduce_max(top, val, AX))
            L(V_.tensor_tensor(eq, val, top.unsqueeze(2).broadcast_to([P, nt, width]), ALU.is_equal))
            L(V_.tensor_tensor(code, eq, iota[:, P - width:P].unsqueeze(1).broadcast_to([P, nt, width]), ALU.mult))
            L(V_.tensor_scalar(eq, eq, float(P), None, ALU.mult))
            L(V_.tensor_tensor(code, eq, code, ALU.subtract))
            L(V_.reduce_max(code_top, code, AX))
            L(V_.tensor_tensor(one, code, code_top.unsqueeze(2).broadcast_to([P, nt, width]), ALU.is_equal))

        g = lambda n: rg[:, 0:nt, n, :]
        e = lambda n: re[:, 0:nt, n, :]
        u = lambda n: ru[:, 0:nt, n]
        G = logits[:, 0:nt, 0:NG]
        pick(G, NG, g(0), g(1), u(0), u(1), g(2))
        V_.tensor_tensor(g(3), G, u(0).unsqueeze(2).broadcast_to([P, nt, NG]), ALU.subtract).then_inc(s_rt, 1)
        L(V_.tensor_scalar(g(4), g(2), BIG, -BIG, ALU.mult, ALU.add))
        for n in range(NG):
            ins = V_.tensor_tensor(e(0)[:, :, n * EPG:(n + 1) * EPG], logits[:, 0:nt, NG + n * EPG:NG + (n + 1) * EPG],
                                   g(4)[:, :, n:n + 1].broadcast_to([P, nt, EPG]), ALU.add)
        L(ins)
        pick(e(0), NE, e(3), e(4), u(2), u(3), e(1))
        L(V_.scalar_tensor_tensor(e(5), e(1), -2 * BIG, e(0), ALU.mult, ALU.add))
        pick(e(5), NE, e(3), e(4), u(4), u(5), e(2))
        V_.tensor_tensor(u(6), u(4), u(2), ALU.subtract).then_inc(s_rt, 1)
        dve.wait_ge(s_rta, 2 * (l + 1))
        L(V_.reduce_sum(u(7), g(5), AX))
        L(V_.reciprocal(u(7), u(7)))
        L(V_.tensor_scalar(u(9), u(8), 1.0, None, ALU.add))
        L(V_.reciprocal(u(9), u(9)))
        L(V_.tensor_tensor(wsel[:, 0, 0:nt], u(7), u(9), ALU.mult))
        L(V_.tensor_tensor(wsel[:, 1, 0:nt], u(8), wsel[:, 0, 0:nt], ALU.mult))
        L(V_.tensor_tensor(e(6), e(1), e(2), ALU.add))
        L(V_.memset(pre[:, 0], 0.0))
        for t in range(1, nt):
            L(V_.tensor_tensor(pre[:, t], pre[:, t - 1], re[:, t - 1, 6], ALU.add))
        V_.tensor_tensor(tot[:, :], pre[:, nt - 1], re[:, nt - 1, 6], ALU.add).then_inc(s_rtp, 1)
        dve.wait_ge(s_rtm, 2 * l + 1)
        L(V_.tensor_scalar(er[:, 0], psum[:, 1, 0:NE], float(P - 1), None, ALU.add))
        L(V_.tensor_copy(eri[:, 0], er[:, 0]))
        L(V_.tensor_scalar(eri[:, 1], eri[:, 0], 7, None, ALU.arith_shift_right))
        L(V_.tensor_copy(er[:, 1], eri[:, 1]))
        L(V_.memset(er[:, 2], 1.0))
        L(V_.tensor_tensor_scan(er[:, 3], er[:, 2], er[:, 1], 0.0, ALU.mult, ALU.add))
        L(V_.tensor_copy(blkcount[:, l:l + 1], er[:, 3, NE - 1:NE]))
        L(V_.tensor_tensor(er[:, 4], er[:, 3], er[:, 1], ALU.subtract))
        L(V_.tensor_scalar(er[:, 4], er[:, 4], float(P), None, ALU.mult))
        L(V_.tensor_tensor(cmp_[:, :, :], er[:, 3].unsqueeze(1).broadcast_to([P, NBT, NE]),
                           iota[:, 0:NBT].unsqueeze(2).broadcast_to([P, NBT, NE]), ALU.is_le))
        L(V_.reduce_sum(ebf[:, :], cmp_[:, :, :], AX))
        L(V_.tensor_scalar(ebf[:, :], ebf[:, :], float(NE - 1), None, ALU.min))
        L(V_.tensor_copy(exptab[:, :], ebf[:, :]))
        L(V_.tensor_tensor(e(7), psum[:, 0, 0:nt * NE].rearrange("p (t e) -> p t e", e=NE),
                           er[:, 4].unsqueeze(1).broadcast_to([P, nt, NE]), ALU.add))
        for q in range(2):
            L(V_.tensor_tensor(e(3), e(7), e(1 + q), ALU.mult))
            L(V_.reduce_sum(slf[:, q, 0:nt], e(3), AX))
            L(V_.tensor_copy(sli[:, 0, 0:nt], slf[:, q, 0:nt]))
            L(V_.tensor_scalar(sli[:, 1, 0:nt], sli[:, 0, 0:nt], 7, None, ALU.arith_shift_right))
            L(V_.tensor_copy(slf[:, 2 + q, 0:nt], sli[:, 1, 0:nt]))
            L(V_.scalar_tensor_tensor(slf[:, 4 + q, 0:nt], slf[:, 2 + q, 0:nt], -float(P), slf[:, q, 0:nt], ALU.mult, ALU.add))
        for q in range(2):
            for t in range(nt):
                V_.tensor_scalar(lane1[:, q, t], iota, slf[:, 4 + q, t:t + 1], None, ALU.is_equal)
                ins = V_.tensor_scalar(blk1[:, q, t], iota[:, 0:NBT], slf[:, 2 + q, t:t + 1], tokrow[:, t:t + 1], ALU.is_equal, ALU.mult)
            L(ins)
            if q:
                for t in range(nt):
                    L(V_.tensor_scalar(cmp_[:, 0:NBT, 0], iota[:, 0:NBT], slf[:, 3, t:t + 1], None, ALU.is_equal))
                    ins = V_.tensor_tensor(blk1[:, 1, t], blk1[:, 1, t], cmp_[:, 0:NBT, 0], ALU.add)
                    L(ins)
        L(V_.memset(tabf[:, 1], 0.0))
        dve.sem_inc(s_rtp, 1)
        dve.wait_ge(s_rtm, 2 * l + 2)
        L(V_.tensor_scalar(tabf[:, 1], psum[:, 2, 0:NBT], 0.0, float(EMPTY), ALU.is_equal, ALU.mult))
        L(V_.scalar_tensor_tensor(tabf[:, 0], psum[:, 2, 0:NBT], -1.0, tabf[:, 1], ALU.add, ALU.add))
        L(V_.tensor_scalar(tabf[:, 0], tabf[:, 0], 0.0, None, ALU.max))
        L(V_.tensor_copy(rowtab[:, :], tabf[:, 0]))
        L(V_.tensor_scalar(toktab[:, :], rowtab[:, :], 1, None, ALU.arith_shift_right))

    def act_route(act, l):
        nt = TILES[l]
        act.wait_ge(s_rt, 2 * l + 1)
        nc.scalar.activation(rg[:, 0:nt, 5, :], rg[:, 0:nt, 3, :], ACT.Exp).then_inc(s_rta, 1)
        act.wait_ge(s_rt, 2 * l + 2)
        nc.scalar.activation(ru[:, 0:nt, 8], ru[:, 0:nt, 6], ACT.Exp).then_inc(s_rta, 1)

    def pe_route(pe, l):
        nt = TILES[l]
        pe.wait_ge(s_rtp, 2 * l + 1)
        nc.tensor.matmul(psum[:, 0, 0:nt * NE].rearrange("p (t e) -> p t e", e=NE), tri, re[:, 0:nt, 6, :], start=True, stop=False)
        nc.tensor.matmul(psum[:, 0, 0:nt * NE].rearrange("p (t e) -> p t e", e=NE), ones[:, :], pre[:, 0:nt, :], start=False, stop=True)
        nc.tensor.matmul(psum[:, 1, 0:NE], ones[:, :], tot[:, :], start=True, stop=True).then_inc(s_rtm, 1)
        pe.wait_ge(s_rtp, 2 * l + 2)
        for q in range(2):
            for t in range(nt):
                ins = nc.tensor.matmul(psum[:, 2, 0:NBT], lane1[:, q, t], blk1[:, q, t], start=(q + t == 0), stop=(q == 1 and t == nt - 1))
        ins.then_inc(s_rtm, 1)

    s_g, s_u, s_w2 = sem("s_g"), sem("s_u"), sem("s_w2")
    s_gup, s_upp = sem("s_gup"), sem("s_upp")
    s_xg, s_xtp, s_xta, s_xtd = sem("s_xg"), sem("s_xtp"), sem("s_xta"), sem("s_xtd")
    s_sil, s_hh, s_ht, s_hta, s_htd, s_yb, s_ya, s_yd, s_ys = [
        sem(n) for n in ("s_sil", "s_hh", "s_ht", "s_hta", "s_htd", "s_yb", "s_ya", "s_yd", "s_ys")]
    s_idx, s_xz = sem("s_idx"), sem("s_xz")
    A = Arena("moe")
    wg = A("wg", [P, 2, KD, DE])
    wu = A("wu", [P, 2, KD, DE])
    w2 = A("w2", [P, 2, DE // P, D])
    xl = A("xl", [P, D])
    xg = A("xg", [P, D])
    xT = A("xT", [P, KD, P])
    sg = A("sg", [P, DE])
    hh = A("hh", [P, DE])
    hT2 = A("hT2", [P, DE // P, P])
    yo = A("yo", [P, D])
    gidx = A("gidx", [P, 1], I32)
    sidx = A("sidx", [P, 1], I32)

    counts = {}

    def blocks(eng, l):
        n = eng.value_load(blkcount[0:1, l:l + 1], min_val=NB_MIN[l], max_val=NB_MAX[l])
        n = eng.snap(n, min_val=NB_MIN[l], max_val=NB_MAX[l])
        before = counts.get((eng, 0), 0)
        counts[eng, l] = n
        return before, n

    def moe_loop(eng, l, body, chain=None):
        before, n = blocks(eng, l)
        with eng.Fori(0, n) as b:
            body(b, before + b)
        return before + n

    def sp_moe(sp, l):
        if l == 0:
            for s in (s_g, s_u, s_w2):
                sp.sem_inc(s, 16)
        w13v = e_w13[l].rearrange("e (k p) f -> p e k f", p=P)
        w2v = e_w2[l].rearrange("e (k p) f -> p e k f", p=P)

        def body(b, B):
            e = sp.value_load(exptab[0:1, ds(b, 1)], min_val=0, max_val=NE - 1)
            par = b % 2
            settled(sp, s_g, 16 * B + 16)
            settled(sp, s_gup, B + 1)
            sp.dma_start(wg[:, ds(par, 1)].rearrange("p o k f -> p (o k) f"), w13v[:, ds(e, 1), :, 0:DE].rearrange("p o k f -> p (o k) f")).then_inc(s_g, 16)
            settled(sp, s_u, 16 * B + 16)
            settled(sp, s_upp, B + 1)
            sp.dma_start(wu[:, ds(par, 1)].rearrange("p o k f -> p (o k) f"), w13v[:, ds(e, 1), :, DE:].rearrange("p o k f -> p (o k) f")).then_inc(s_u, 16)
            settled(sp, s_w2, 16 * B + 16)
            settled(sp, s_yb, B + 1)
            sp.dma_start(w2[:, ds(par, 1)].rearrange("p o k f -> p (o k) f"), w2v[:, ds(e, 1), :, :].rearrange("p o k f -> p (o k) f")).then_inc(s_w2, 16)
        moe_loop(sp, l, body)

    def pool_moe(pool, l):
        nc.gpsimd.memset(xl[:, :], 0.0).then_inc(s_xz, 1)
        pool.wait_ge(s_xz, l + 1)
        if l == 0:
            pool.sem_inc(s_xtp, 1)
            pool.dma_start(xl[0:16, 0:P], consts[0:16, 0:P]).then_inc(s_ys, 16)
            pool.wait_ge(s_ys, 16)
        before = counts.get((pool, 0), 0)

        def gather(b, n_idx):
            nc.gpsimd.tensor_copy(gidx[:, :], toktab[:, ds(b, 1)]).then_inc(s_idx, 1)
            settled(pool, s_idx, n_idx + 1)
            pool.indirect_dma_start(xl[:, :], None, h2_d, bass.IndirectOffsetOnAxis(gidx[:, :], 0),
                                    bounds_check=NTOK - 1, oob_is_err=False).then_inc(s_xg, 16)

        def pass_on(n):
            settled(pool, s_xg, 16 * (n + l) + 16)
            settled(pool, s_xtp, n + 1)
            nc.gpsimd.tensor_copy(xg[:, :], xl[:, :]).then_inc(s_xcopy, 1)
            settled(pool, s_xcopy, n + 1)

        gather(0, 2 * (before + l))
        pass_on(before + l)
        gather(1, 2 * (before + l) + 1)

        def body(b, B):
            pass_on(B + l + 1)
            gather(b + 2, 2 * (B + l) + 2)
            settled(pool, s_ys, 16 * B + 16)
            pool.sem_inc(s_yfree, 1)
            nc.gpsimd.tensor_copy(sidx[:, :], rowtab[:, ds(b, 1)]).then_inc(s_idx, 1)
            settled(pool, s_idx, 2 * (B + l) + 4)
            settled(pool, s_ya, B + 1)
            settled(pool, s_yd, B + 1)
            pool.indirect_dma_start(y_d, bass.IndirectOffsetOnAxis(sidx[:, :], 0), yo[:, :], None,
                                    bounds_check=2 * NTOK - 1, oob_is_err=False).then_inc(s_ys, 16)
        end = moe_loop(pool, l, body)
        settled(pool, s_ys, 16 * end + 16)
        settled(pool, s_xg, 16 * (end + 2 * (l + 1)))

    def pe_moe(pe, l):
        before = counts.get((pe, 0), 0)
        if l == 0:
            for s in (s_gup, s_upp, s_yb):
                pe.sem_inc(s, 2)

        def turn_x(half):
            for k in range(4 * half, 4 * half + 4):
                ins = nc.tensor.transpose(psum[:, 3 + half, (k % 4) * P:(k % 4 + 1) * P], xg[:, k * P:(k + 1) * P], ident)
            if half:
                ins.then_inc(s_xtp, 1)
        pe.wait_ge(s_xcopy, before + l + 1)
        turn_x(0)
        turn_x(1)

        def body(b, B):
            par = b % 2
            pe.wait_ge(s_xta, B + l + 1)
            pe.wait_ge(s_xtd, B + l + 1)
            pe.wait_ge(s_g, 16 * B + 32)
            for k in range(KD):
                ins = nc.tensor.matmul(psum[:, 0, :], xT[:, k, :], wg[:, ds(par, 1), k, :].rearrange("p o n -> p (o n)"), start=(k == 0), stop=(k == KD - 1))
            ins.then_inc(s_gup, 1)
            pe.wait_ge(s_u, 16 * B + 32)
            for h in range(2):
                for k in range(KD):
                    ins = nc.tensor.matmul(psum[:, 1 + h, 0:256], xT[:, k, :], wu[:, ds(par, 1), k, h * 256:(h + 1) * 256].rearrange("p o n -> p (o n)"),
                                           start=(k == 0), stop=(k == KD - 1))
                if h == 0:
                    ins.then_inc(s_uph, 1)
            ins.then_inc(s_upp, 1)
            pe.wait_ge(s_xcopy, B + l + 2)
            turn_x(0)
            for h in range(2):
                pe.wait_ge(s_hh, 2 * B + h + 1)
                for k in range(2):
                    ins = nc.tensor.transpose(psum[:, 5 if h == 0 else 1, k * P:(k + 1) * P], hh[:, (2 * h + k) * P:(2 * h + k + 1) * P], ident)
                ins.then_inc(s_ht, 1)
            turn_x(1)
            pe.wait_ge(s_w2, 16 * B + 32)
            for h in range(2):
                pe.wait_ge(s_htd if h == 0 else s_hta, B + 1)
                for n in range(2):
                    for k in (2 * h, 2 * h + 1):
                        ins = nc.tensor.matmul(psum[:, 6 + n, :], hT2[:, k, :], w2[:, ds(par, 1), k, n * HALF:(n + 1) * HALF].rearrange("p o n -> p (o n)"),
                                               start=(k == 0), stop=(k == 3))
            ins.then_inc(s_yb, 1)
        moe_loop(pe, l, body)

    s_uph, s_yfree, s_xcopy = sem("s_uph"), sem("s_yfree"), sem("s_xcopy")

    def act_moe(act, l):
        before = counts.get((act, 0), 0)

        def take_x(B, n):
            act.wait_ge(s_xtp, n)
            nc.scalar.activation(xT[:, 0:4, :], psum[:, 3, :].rearrange("p (b n) -> p b n", b=4), ACT.Copy).then_inc(s_xta, 1)
        take_x(before, before + l + 2)

        def body(b, B):
            act.wait_ge(s_gup, B + 3)
            nc.scalar.activation(sg[:, :], psum[:, 0, :], ACT.Silu).then_inc(s_sil, 1)
            act.wait_ge(s_ht, 2 * B + 2)
            nc.scalar.activation(hT2[:, 2:4, :], psum[:, 1, 0:256].rearrange("p (b n) -> p b n", b=2), ACT.Copy).then_inc(s_hta, 1)
            take_x(B, B + l + 3)
            act.wait_ge(s_yb, B + 3)
            act.wait_ge(s_yfree, B + 1)
            nc.scalar.activation(yo[:, HALF:], psum[:, 7, :], ACT.Copy).then_inc(s_ya, 1)
        moe_loop(act, l, body)

    def dve_moe(dve, l):
        before = counts.get((dve, 0), 0)

        def take_x(n):
            dve.wait_ge(s_xtp, n)
            nc.vector.tensor_copy(xT[:, 4:8, :], psum[:, 4, :].rearrange("p (b n) -> p b n", b=4)).then_inc(s_xtd, 1)
        take_x(before + l + 2)

        def body(b, B):
            dve.wait_ge(s_sil, B + 1)
            for h in range(2):
                if h == 0:
                    dve.wait_ge(s_uph, B + 1)
                else:
                    dve.wait_ge(s_upp, B + 3)
                nc.vector.tensor_tensor(hh[:, h * 256:(h + 1) * 256], psum[:, 1 + h, 0:256], sg[:, h * 256:(h + 1) * 256], ALU.mult).then_inc(s_hh, 1)
            dve.wait_ge(s_ht, 2 * B + 1)
            nc.vector.tensor_copy(hT2[:, 0:2, :], psum[:, 5, 0:256].rearrange("p (b n) -> p b n", b=2)).then_inc(s_htd, 1)
            take_x(B + l + 3)
            dve.wait_ge(s_yb, B + 3)
            dve.wait_ge(s_yfree, B + 1)
            nc.vector.tensor_copy(yo[:, 0:HALF], psum[:, 6, :]).then_inc(s_yd, 1)
        moe_loop(dve, l, body)

    s_fin = [sem("s_fin0"), sem("s_fin1")]
    s_fx, s_fst, s_fg = sem("s_fx"), [sem("s_fst0"), sem("s_fst1")], sem("s_fg")
    A = Arena("last")
    fx = A("x", [P, 2, D])
    fy = A("y", [P, 2, 2, D])
    fu = A("u", [P, 2, D])
    fg = A("g", [P, D])
    fw = A("w", [P, 2, 2])

    def sp_last(sp):
        sp.dma_start(fg[:, :], mod_d[1, 0:1, 5 * D:].broadcast_to([P, D])).then_inc(s_fg, 16)
        sp.sem_inc(s_fst[0], 16)
        sp.sem_inc(s_fst[1], 16)

        def body(i):
            for par in range(2):
                t = 2 * i + par
                sp.wait_ge(s_fst[par], 16 * i + 16)
                sp.dma_start(fx[:, par], xs_d[ds(t * P, P), :]).then_inc(s_fin[par], 16)
                sp.dma_start(fy[:, par], y_d[ds(t * 2 * P, 2 * P), :].rearrange("(p c) n -> p c n", c=2)).then_inc(s_fin[par], 16)
        trips(sp, TX // 2, body)

    def dve_last(dve):
        dve.wait_ge(s_fg, 16)

        def body(i):
            for par in range(2):
                t = 2 * i + par
                dve.wait_ge(s_fin[par], 32 * (i + 1))
                dve_combine(dve, par, t, 0, fx[:, par], fy[:, par], fu[:, par], fw[:, par], fg[:, :]).then_inc(s_fx, 1)
        trips(dve, TX // 2, body, dvec, 8)

    def act_last(act):
        def body(i):
            for par in range(2):
                t = 2 * i + par
                act.wait_ge(s_fx, t + 1)
                act.dma_start(out[0, ds(t * P, P), :], fx[:, par]).then_inc(s_fst[par], 16)
        trips(act, TX // 2, body)
        for par in range(2):
            act.wait_ge(s_fst[par], 16 + 16 * (TX // 2))

    with nc.Block() as block:
        @block.sync
        def _(sp):
            sp_setup(sp)
            phase_end(sp)
            for l in range(2):
                for part in (sp_prep, sp_qkv, sp_att, sp_post):
                    part(sp, l)
                    phase_end(sp)
                phase_end(sp)
                sp_moe(sp, l)
                phase_end(sp)
            sp_last(sp)

        @block.gpsimd
        def _(pool):
            phase_end(pool)
            for l in range(2):
                for part in (pool_prep, pool_qkv, pool_att, pool_post):
                    part(pool, l)
                    phase_end(pool)
                phase_end(pool)
                pool_moe(pool, l)
                phase_end(pool)

        @block.tensor
        def _(pe):
            pe_setup(pe)
            phase_end(pe)
            for l in range(2):
                for part in (pe_prep, pe_qkv, pe_att, pe_post, pe_route, pe_moe):
                    part(pe, l)
                    phase_end(pe)

        @block.vector
        def _(dve):
            dve_setup(dve)
            phase_end(dve)
            for l in range(2):
                for part in (dve_prep, dve_qkv, dve_att, dve_post, dve_route, dve_moe):
                    part(dve, l)
                    phase_end(dve)
            dve_last(dve)

        @block.scalar
        def _(act):
            act_setup(act)
            phase_end(act)
            for l in range(2):
                for part in (act_prep, act_qkv, act_att, act_post, act_route, act_moe):
                    part(act, l)
                    phase_end(act)
            act_last(act)


_INS = ["x", "c", "ctx", "c_ctx", "ada_w", "ada_b", "norm1_g", "norm2_g", "a_wqkv", "a_wo", "a_q_norm", "a_k_norm",
        "a_lambda_q1", "a_lambda_k1", "a_lambda_q2", "a_lambda_k2", "a_subln_g", "b_wqkv", "b_wo", "b_q_norm",
        "b_k_norm", "b_sink", "r_w1", "r_b1", "r_w2", "r_b2", "e_w13", "e_w2"]


def constants():
    import numpy as np
    t = np.zeros((P, C_END), np.float32)
    i = np.arange(P)
    t[:, C_ID:C_ID + P] = np.eye(P)
    t[:, C_TRI:C_TRI + P] = i[:, None] < i[None, :]
    t[:, C_IOTA:C_IOTA + P] = i[None, :]
    t[:, C_PREV:C_PREV + P] = np.where(i[None, :] >= i[:, None], 0, -BIG)
    t[:, C_NEXT:C_NEXT + P] = np.where(i[None, :] <= i[:, None], 0, -BIG)
    grid_w, freqs = 64, HD // 4
    pos = np.arange(SEQ)
    inv = np.float32(10000.0) ** (-np.arange(freqs, dtype=np.float32) / np.float32(freqs))
    ang = np.stack([(pos // grid_w).astype(np.float32)[:, None] * inv, (pos % grid_w).astype(np.float32)[:, None] * inv], 1)
    cos, sin = np.cos(ang), np.sin(ang)
    full_c = np.ones((NTOK, 2, 2, freqs), np.float32)
    full_s = np.zeros((NTOK, 2, 2, freqs), np.float32)
    full_c[:SEQ] = cos[:, :, None, :]
    full_s[:SEQ, :, 0] = -sin
    full_s[:SEQ, :, 1] = sin
    t[:, C_COS:C_COS + TA * HD] = full_c.reshape(TA, P, HD).transpose(1, 0, 2).reshape(P, TA * HD)
    t[:, C_SIN:C_SIN + TA * HD] = full_s.reshape(TA, P, HD).transpose(1, 0, 2).reshape(P, TA * HD)
    t[:, C_TOK:C_TOK + TA] = 2 * (np.arange(TA)[None, :] * P + i[:, None]) + 1
    return t


def kernel(**inputs):
    import numpy as np
    import concourse.bacc as bacc
    from concourse.bass_utils import run_bass_kernel_spmd

    nc = bacc.Bacc("TRN2", target_bir_lowering=False, num_devices=1)
    arrays, args = {}, []
    for name in _INS:
        a = np.ascontiguousarray(inputs[name])
        arrays["in_" + name] = a
        args.append(nc.dram_tensor("in_" + name, a.shape, mybir.dt.from_np(a.dtype), kind="ExternalInput").ap())
    table = constants()
    arrays["in_consts"] = table
    args.append(nc.dram_tensor("in_consts", table.shape, F32, kind="ExternalInput").ap())
    args.append(nc.dram_tensor("out", (1, SEQ, D), F32, kind="ExternalOutput").ap())
    build(nc, *args)
    r = run_bass_kernel_spmd(nc, [arrays], core_ids=[0])
    return r.results[0]["out"]
```

```python
import math

import concourse.bass as bass
from concourse import mybir

F32 = mybir.dt.float32
BF16 = mybir.dt.bfloat16
F32R = mybir.dt.float32r
I32 = mybir.dt.int32
ALU = mybir.AluOpType
ACT = mybir.ActivationFunctionType
AX = mybir.AxisListType.X

P = 128
D = 1024
KD = D // P
SEQ, CTX = 1024, 256
TX, TC = SEQ // P, CTX // P
TA = TX + TC
NTOK = SEQ + CTX
HALF = 512
HD = 64
EPS = 1e-6
SCALE = HD ** -0.5
LAM_INIT = 0.8 - 0.6 * math.exp(-0.3 * 0)
NG, EPG = 4, 8
NE = NG * EPG
DE = 512
BIG = 1e30
NB_MAX = [2 * NTOK // P + NE, 2 * SEQ // P + NE]
NB_MIN = [2 * NTOK // P, 2 * SEQ // P]
NBT = NB_MAX[0] + 2
EMPTY = 1 << 20
TILES = [TA, TX]

C_ID, C_TRI, C_IOTA, C_PREV, C_NEXT = 0, 128, 256, 384, 512
C_COS, C_SIN = 640, 640 + TA * HD
C_TOK = C_SIN + TA * HD
C_END = C_TOK + TA


def build(nc, x, c, ctx, c_ctx, ada_w, ada_b, norm1_g, norm2_g, a_wqkv, a_wo, a_q_norm, a_k_norm,
          a_lambda_q1, a_lambda_k1, a_lambda_q2, a_lambda_k2, a_subln_g, b_wqkv, b_wo, b_q_norm,
          b_k_norm, b_sink, r_w1, r_b1, r_w2, r_b2, e_w13, e_w2, consts, out):
    ds = bass.ds
    nc.disable_value_cache = True

    def dram(name, shape):
        return nc.dram_tensor(name, shape, F32, kind="Internal").ap()

    mod_d = dram("mod_d", [2, 2, 6 * D])
    qk_d = dram("qk_d", [16, 2, P, NTOK])
    v_d = dram("v_d", [NTOK, 256])
    o_d = dram("o_d", [TA, P, D])
    xs_d = dram("xs_d", [NTOK, D])
    h2_d = dram("h2_d", [NTOK, D])
    y_d = dram("y_d", [2 * NTOK, D])

    def sb(name, shape, dt=F32):
        return nc.alloc_sbuf_tensor(name, shape, dt)

    cst = sb("cst", [P, C_END])
    ident = cst[:, C_ID:C_ID + P]
    tri = cst[:, C_TRI:C_TRI + P]
    iota = cst[:, C_IOTA:C_IOTA + P]
    tokrow = cst[:, C_TOK:C_TOK + TA]
    ones = sb("ones", [P, P])
    ident_h = sb("ident_h", [P, P], BF16)
    mask_h = sb("mask_h", [P, 2, 2, P], BF16)
    neghalf = sb("neghalf", [P, TA * 2])
    gains = sb("gains", [P, 4, HD])
    subg = sb("subg", [P, 1])
    lamv = sb("lamv", [P, 4, HD])
    lamw = sb("lamw", [P, 2, HD])
    lams = sb("lams", [P, 4])
    neglam = sb("neglam", [P, 1])
    sinks = sb("sinks", [P, 16])
    negsink = sb("negsink", [P, 16])
    wrt = sb("wrt", [P, 2, KD, NG + NE])
    brt = sb("brt", [P, 2, NG + NE])
    colw = sb("colw", [P, 40])
    mod_a = sb("mod_a", [P, 2, KD])
    mod_b = sb("mod_b", [P, 2, KD])
    logits = sb("logits", [P, TA, NG + NE])
    wsel = sb("wsel", [P, 2, TA])
    rowtab = sb("rowtab", [P, NBT], I32)
    toktab = sb("toktab", [P, NBT], I32)
    exptab = sb("exptab", [P, NBT], I32)
    blkcount = sb("blkcount", [P, 2], I32)
    arena0 = nc.sbuf_base
    arena0_at = (arena0 + 63) // 64 * 64
    limit = nc.sbuf_usable_end

    class Arena:

        def __init__(self, tag, at=None):
            self.tag, self.at = tag, at or arena0_at

        def __call__(self, name, shape, dt=F32):
            size = (4 if dt != BF16 else 2) * math.prod(shape[1:])
            t = nc.alloc_sbuf_tensor_at(f"{self.tag}_{name}", shape, dt, offset=self.at)
            self.at += (size + 63) // 64 * 64
            assert self.at <= limit, (self.tag, name, self.at, limit)
            return t

    psum = nc.alloc_psum_tensor("psum", [P, 8, HALF], F32)

    def sem(name):
        return nc.alloc_semaphore(name)

    s_phase = sem("s_phase")
    phases = {}

    def phase_end(eng):
        phases[eng] = phases.get(eng, 0) + 1
        eng.drain().then_inc(s_phase, 1)
        eng.wait_ge(s_phase, 5 * phases[eng])

    class Chain:

        def __init__(self, name):
            self.sem, self.base, self.n = sem(name), 0, 0

        def link(self, eng, ins):
            self.n += 1
            ins.then_inc(self.sem, 1)
            eng.wait_ge(self.sem, self.base + self.n)

        def trips(self, eng, n, body):
            if n == 1:
                return body(0)
            start, self.n = self.base + self.n, 0
            with eng.Fori(0, n) as i:
                per = self.per_trip
                self.base, self.n = start + i * per, 0
                body(i)
                assert self.n == per, (self.n, per)
            self.base, self.n = start + n * per, 0

    dvec, poolc = Chain("s_dve_chain"), Chain("s_pool_chain")

    def trips(eng, n, body, chain=None, links=0):
        if chain is None:
            if n == 1:
                return body(0)
            with eng.Fori(0, n) as i:
                body(i)
            return
        chain.per_trip = links
        chain.trips(eng, n, body)

    def tile_steps(eng, tiles, step, chain=None, links=0):
        step(0, 0)
        step(1, 1)

        def body(i):
            for par in range(2):
                step(2 * i + 2 + par, par)
        trips(eng, TX // 2 - 1, body, chain, 2 * links)
        for t in range(TX, tiles):
            step(t, t % 2)

    s_settled = sem("s_settled")

    def settled(eng, s, value):
        eng.wait_ge(s, value)
        if not isinstance(value, int):
            eng.sem_inc(s_settled, 1)

    s_const, s_small = sem("s_const"), sem("s_small")
    s_crow, s_ct, s_cs = sem("s_crow"), sem("s_ct"), sem("s_cs")
    s_adaw = [sem(f"s_adaw{n}") for n in range(4)]
    s_adaacc, s_adafree = sem("s_adaacc"), sem("s_adafree")
    s_adaput = [sem(f"s_adaput{n}") for n in range(4)]
    A = Arena("ada")
    crow = A("crow", [16, P])
    cs = A("cs", [P, 2, KD])
    adaw = A("w", [P, 4, KD, HALF])
    adab = A("b", [2, 4, HALF])
    adar = A("r", [2, 4, HALF])
    NCH = 6 * D // HALF

    def sp_setup(sp):
        sp.dma_start(crow[0:8, :], c.rearrange("o (k p) -> (o k) p", p=P)).then_inc(s_crow, 16)
        sp.dma_start(crow[8:16, :], c_ctx.rearrange("(k p) -> k p", p=P)).then_inc(s_crow, 16)
        sp.dma_start(cst[:, :], consts).then_inc(s_const, 16)
        for l in range(2):
            wv = ada_w[l].rearrange("(k p) n -> p k n", p=P)

            def body(i):
                for par in range(4):
                    n = 4 * i + par
                    sp.wait_ge(s_adafree, l * NCH + n + 1)
                    sp.dma_start(adaw[:, par], wv[:, :, ds(n * HALF, HALF)]).then_inc(s_adaw[par], 16)
                    sp.dma_start(adab[:, par], ada_b[l:l + 1, ds(n * HALF, HALF)].broadcast_to([2, HALF])).then_inc(s_adaw[par], 16)

            trips(sp, NCH // 4, body)

    def act_small_loads(act):
        n = 0
        vecs = [(gains[:, 0], a_q_norm), (gains[:, 1], a_k_norm), (gains[:, 2], b_q_norm), (gains[:, 3], b_k_norm),
                (lamv[:, 0], a_lambda_q1), (lamv[:, 1], a_lambda_k1), (lamv[:, 2], a_lambda_q2),
                (lamv[:, 3], a_lambda_k2)]
        for dst, src in vecs:
            act.dma_start(dst, src.broadcast_to([P, HD])).then_inc(s_small, 16)
            n += 16
        act.dma_start(sinks[:, :], b_sink.broadcast_to([P, 16])).then_inc(s_small, 16)
        act.dma_start(subg[:, :], a_subln_g.rearrange("o e -> e o")).then_inc(s_small, 16)
        n += 32
        for l in range(2):
            act.dma_start(wrt[:, l, :, 0:NG], r_w1[l].rearrange("(k p) g -> p k g", p=P)).then_inc(s_small, 16)
            act.dma_start(brt[:, l, 0:NG], r_b1[l:l + 1, :].broadcast_to([P, NG])).then_inc(s_small, 16)
            act.dma_start(brt[:, l, NG:], r_b2[l:l + 1].rearrange("o g e -> o (g e)").broadcast_to([P, NE])).then_inc(s_small, 16)
            n += 48
            for g in range(NG):
                act.dma_start(wrt[:, l, :, NG + g * EPG:NG + (g + 1) * EPG],
                              r_w2[l, g].rearrange("(k p) e -> p k e", p=P)).then_inc(s_small, 16)
                n += 16
        return n

    n_small = 16 * (8 + 2 + 2 * (3 + NG))

    def act_setup(act):
        act.wait_ge(s_ct, 1)
        nc.scalar.activation(cs[:, :, :], psum[:, 0, 0:16].rearrange("p (s k) -> p s k", s=2), ACT.Silu).then_inc(s_cs, 1)
        assert act_small_loads(act) == n_small
        for s in s_adaput:
            act.sem_inc(s, 16)
        for l in range(2):
            def body(i):
                for par in range(4):
                    n = 4 * i + par
                    act.wait_ge(s_adafree, l * NCH + n + 5)
                    act.dma_start(mod_d[l, :, ds(n * HALF, HALF)], adar[:, par]).then_inc(s_adaput[par], 16)
            trips(act, NCH // 4, body)
        for s in s_adaput:
            act.wait_ge(s, 16 + 16 * (2 * NCH // 4))
        act.wait_ge(s_lam, 1)
        nc.scalar.activation(lams[:, 2:4], lams[:, 0:2], ACT.Exp).then_inc(s_lam, 1)

    s_lam = sem("s_lam")

    def pe_setup(pe):
        pe.wait_ge(s_const, 16)
        pe.wait_ge(s_crow, 32)
        nc.tensor.transpose(psum[:, 0, 0:16], crow[:, :], ident[0:16, 0:16]).then_inc(s_ct, 1)
        pe.wait_ge(s_cs, 1)
        for l in range(2):
            def body(i):
                for par in range(4):
                    n = 4 * i + par
                    pe.wait_ge(s_adaw[par], 32 * (l * NCH // 4 + i + 1))
                    pe.wait_ge(s_adafree, l * NCH + n + 1)
                    for k in range(KD):
                        ins = nc.tensor.matmul(psum[0:2, 1 + par, :], cs[:, :, k], adaw[:, par, k], start=(k == 0), stop=(k == KD - 1))
                    ins.then_inc(s_adaacc, 1)
            trips(pe, NCH // 4, body)

    def dve_setup(dve):
        nc.vector.memset(ones[:, :], 1.0)
        dve.sem_inc(s_adafree, 4)
        nc.vector.memset(neghalf[:, :], -0.5)
        nc.vector.memset(blkcount[:, :], 0)
        for l in range(2):
            def body(i):
                for par in range(4):
                    n = 4 * i + par
                    dve.wait_ge(s_adaacc, l * NCH + n + 1)
                    dve.wait_ge(s_adaw[par], 32 * (l * NCH // 4 + i + 1))
                    dve.wait_ge(s_adaput[par], 16 + 16 * (l * NCH // 4 + i))
                    nc.vector.tensor_tensor(adar[:, par], psum[0:2, 1 + par, :], adab[:, par], ALU.add).then_inc(s_adafree, 1)
            trips(dve, NCH // 4, body)
        dve.wait_ge(s_const, 16)
        nc.vector.tensor_copy(ident_h[:, :], ident)
        dvec.link(dve, nc.vector.memset(mask_h[:, :, :, :], 0.0))
        nc.vector.tensor_copy(mask_h[:, 0, 0], cst[:, C_PREV:C_PREV + P])
        nc.vector.tensor_copy(mask_h[:, 1, 1], cst[:, C_NEXT:C_NEXT + P])
        dve.wait_ge(s_small, n_small)
        nc.vector.tensor_scalar(negsink[:, :], sinks[:, :], -1.0, None, ALU.mult)
        dvec.link(dve, nc.vector.tensor_scalar(subg[:, :], subg[:, :], 1.0 - LAM_INIT, None, ALU.mult))
        dvec.link(dve, nc.vector.tensor_tensor(lamw[:, :, :], lamv[:, 0:4:2], lamv[:, 1:4:2], ALU.mult))
        nc.vector.reduce_sum(lams[:, 0:2], lamw[:, :, :], AX).then_inc(s_lam, 1)
        dve.wait_ge(s_lam, 2)
        dvec.link(dve, nc.vector.tensor_tensor(neglam[:, :], lams[:, 3:4], lams[:, 2:3], ALU.subtract))
        dvec.link(dve, nc.vector.tensor_scalar(neglam[:, :], neglam[:, :], -LAM_INIT, None, ALU.add))

    s_cols, s_colt = sem("s_cols"), sem("s_colt")
    s_px = [sem("s_px0"), sem("s_px1")]
    s_pxfree, s_pss, s_prs = sem("s_pxfree"), sem("s_pss"), sem("s_prs")
    s_pxn, s_ptp, s_pta = sem("s_pxn"), sem("s_ptp"), sem("s_pta")
    s_pu = sem("s_pu")
    s_pst = [sem("s_pst0"), sem("s_pst1")]
    s_pg = sem("s_pg")
    Q = Arena("act")
    V = Q("V", [P, TA, D])
    after_V = Q.at
    hT = Q("hT", [P, KD, NTOK])
    after_hT = Q.at
    A = Arena("prep", after_hT + 2 * 4 * KD * HALF)
    prow = A("row", [40, P])
    pxt = A("x", [P, 2, D])
    psq = A("sq", [P, 2, D])
    pxn = A("xn", [P, 2, D])
    pss = A("ss", [P, 2])
    prs = A("rs", [P, 2])
    py2 = A("y2", [P, 2, 2, D])
    pu = A("u", [P, 2, D])
    pg2 = A("g2", [P, 2, D])
    pw = A("w", [P, 2, 2])

    def sp_cols(sp, l):
        for s in range(2):
            sp.dma_start(prow[s * 16:s * 16 + 16, :], mod_d[l, s, 0:2 * D].rearrange("(r p) -> r p", p=P)).then_inc(s_cols, 16)
        sp.dma_start(prow[32:40, :], norm1_g[l].rearrange("(r p) -> r p", p=P)).then_inc(s_cols, 16)

    def pe_cols(pe, l):
        pe.wait_ge(s_cols, 48 * (l + 1))
        nc.tensor.transpose(psum[:, 0, 0:40], prow[:, :], ident[0:40, 0:40]).then_inc(s_colt, 1)

    def dve_cols(dve, l):
        dve.wait_ge(s_colt, 1 + 2 * l)
        dvec.link(dve, nc.vector.tensor_copy(colw[:, :], psum[:, 0, 0:40]))
        for s in range(2):
            nc.vector.tensor_copy(mod_b[:, s], colw[:, s * 16:s * 16 + 8])
            ins = nc.vector.scalar_tensor_tensor(mod_a[:, s], colw[:, s * 16 + 8:s * 16 + 16], 1.0, colw[:, 32:40], ALU.add, ALU.mult)
        ins.then_inc(s_colt, 1)
        dve.wait_ge(s_colt, 2 + 2 * l)

    def sp_prep(sp, l):
        def step(t, par):
            T = TA * l + t
            if l:
                src = xs_d[ds(t * P, P), :]
            else:
                src = ctx[0, (t - TX) * P:(t - TX + 1) * P, :] if isinstance(t, int) and t >= TX else x[0, ds(t * P, P), :]
            if l == 0:
                sp.wait_ge(s_pxfree, T + 1)
            else:
                sp.wait_ge(s_pu, t + 1)
                sp.dma_start(py2[:, par], y_d[ds(t * 2 * P, 2 * P), :].rearrange("(p c) n -> p c n", c=2)).then_inc(s_px[par], 16)
            sp.dma_start(pxt[:, par], src).then_inc(s_px[par], 16)
        sp_cols(sp, l)
        if l:
            for s in range(2):
                sp.dma_start(pg2[:, s], mod_d[0, s:s + 1, 5 * D:].broadcast_to([P, D])).then_inc(s_pg, 16)
        tile_steps(sp, TA, step)
        sp_first_weights(sp, l)

    def px_count(l, t, par):
        return 8 * (t - par + 2) if l == 0 else 8 * TA + 16 * (t - par + 2)

    def act_prep(act, l):
        def put(t, par):
            s = int(isinstance(t, int) and t >= TX)
            act.wait_ge(s_ptp, TA * l + t + 3)
            for k in range(KD):
                ins = nc.scalar.activation(hT[:, k, ds(t * P, P)], psum[:, 2 * par + k // 4, (k % 4) * P:(k % 4 + 1) * P], ACT.Identity,
                                           bias=mod_b[:, s, k:k + 1], scale=mod_a[:, s, k:k + 1])
            ins.then_inc(s_pta, 1)

        def step(t, par):
            T = TA * l + t
            if l == 0:
                act.wait_ge(s_px[par], px_count(l, t, par))
            else:
                act.wait_ge(s_pu, t + 3)
                act.dma_start(xs_d[ds(t * P, P), :], pu[:, par]).then_inc(s_pst[par], 16)
            act.wait_ge(s_pxn, T + 1)
            nc.scalar.activation(psq[:, par], (pu if l else pxt)[:, par], ACT.Square, scale=1 / 32, accum_out=pss[:, par:par + 1]).then_inc(s_pss, 1)
            if not (isinstance(t, int) and t < 2):
                put(t - 2, par)
        act.wait_ge(s_colt, 2 + 2 * l)
        tile_steps(act, TA, step)
        put(TA - 2, 0)
        put(TA - 1, 1)
        if l:
            for par in range(2):
                act.wait_ge(s_pst[par], 16 * (TA // 2))

    def pool_rstd(pool, dst, src, half, ready, request):
        settled(pool, *request)
        poolc.link(pool, nc.gpsimd.tensor_scalar(src, src, EPS, None, ALU.add))
        nc.gpsimd.tensor_tensor(dst, src, half, ALU.pow).then_inc(ready, 1)

    def pool_prep(pool, l):
        def step(t, par):
            pool_rstd(pool, prs[:, par:par + 1], pss[:, par:par + 1], neghalf[:, 0:1], s_prs, (s_pss, TA * l + t + 1))
        tile_steps(pool, TA, step, poolc, 1)

    def dve_combine(dve, t, xt, yt, ut, wt, g2):
        dvec.link(dve, nc.vector.tensor_copy(wt, wsel[:, :, ds(t, 1)].rearrange("p c o -> p (c o)")))
        dvec.link(dve, nc.vector.tensor_scalar(ut, yt[:, 0], wt[:, 0:1], None, ALU.mult))
        dvec.link(dve, nc.vector.scalar_tensor_tensor(ut, yt[:, 1], wt[:, 1:2], ut, ALU.mult, ALU.add))
        dvec.link(dve, nc.vector.tensor_tensor(ut, ut, g2, ALU.mult))
        return nc.vector.tensor_tensor(ut, xt, ut, ALU.add)

    def dve_prep(dve, l):
        def norm(t, par):
            T = TA * l + t
            dve.wait_ge(s_prs, T + 1)
            dve.wait_ge(s_ptp, T + 1)
            nc.vector.tensor_scalar(pxn[:, par], (pu if l else pxt)[:, par], prs[:, par:par + 1], None, ALU.mult).then_inc(s_pxn, 1)
            dve.wait_ge(s_pxn, T + 3)
            if l:
                dve.wait_ge(s_pst[par], 8 * (t - par + 2))
            else:
                dve.sem_inc(s_pxfree, 1)

        def step(t, par):
            s = int(isinstance(t, int) and t >= TX)
            dve.wait_ge(s_px[par], px_count(l, t, par))
            if l:
                dve_combine(dve, t, pxt[:, par], py2[:, par], pu[:, par], pw[:, par], pg2[:, s]).then_inc(s_pu, 1)
            if l == 0:
                norm(t, par)
            elif not (isinstance(t, int) and t == 0):
                norm(t - 1, 1 - par)
        if l == 0:
            dve.sem_inc(s_pxfree, 2)
            dve.sem_inc(s_pxn, 2)
        else:
            dve.sem_inc(s_pu, 2)
        dve_cols(dve, l)
        if l:
            dve.wait_ge(s_pg, 32)
        tile_steps(dve, TA, step, dvec, 4 * l)
        if l:
            norm(TA - 1, 1)

    def pe_prep(pe, l):
        pe_cols(pe, l)
        pe.wait_ge(s_colt, 2 + 2 * l)
        if l == 0:
            pe.sem_inc(s_qwfree, 2)
            pe.sem_inc(s_pta, 2)
            pe.sem_inc(s_ptp, 2)

        def step(t, par):
            T = TA * l + t
            pe.wait_ge(s_pxn, T + 3)
            pe.wait_ge(s_pta, T + 1)
            for k in range(KD):
                ins = nc.tensor.transpose(psum[:, 2 * par + k // 4, (k % 4) * P:(k % 4 + 1) * P], pxn[:, par, k * P:(k + 1) * P], ident)
            ins.then_inc(s_ptp, 1)
        tile_steps(pe, TA, step)

    s_qw = [sem("s_qw0"), sem("s_qw1")]
    s_qwfree, s_qacc, s_qaccfree = sem("s_qwfree"), sem("s_qacc"), sem("s_qaccfree")
    s_qsq, s_qms, s_qrs, s_qxn, s_qt2 = sem("s_qsq"), sem("s_qms"), sem("s_qrs"), sem("s_qxn"), sem("s_qt2")
    s_qrot, s_qtr, s_qev = sem("s_qrot"), sem("s_qtr"), sem("s_qev")
    s_qst = [sem("s_qst0"), sem("s_qst1")]
    s_qhi = sem("s_qhi")
    s_vev, s_vst = sem("s_vev"), sem("s_vst")
    s_rope = sem("s_rope")
    A = Arena("qkv", Q.at)
    qw = A("w", [P, 2, KD, HALF])
    rope = A("rope", [P, 2, 2, TA, HD])
    qsq = A("sq", [P, 2, HALF])
    qms = A("ms", [P, 2, 8])
    qrs = A("rs", [P, 2, 8])
    qxn = A("xn", [P, 2, HALF])
    qt1 = A("t1", [P, 2, HALF])
    qt2 = A("t2", [P, 2, HALF])
    qrot = A("rot", [P, 2, HALF])
    qstg = A("stg", [P, 2, 2, 4, P], F32R)
    vstg = A("vstg", [P, TA, 256])

    SECTIONS = [
        [(2, 2, TA, "qk", 8, 0, 0, 0), (1, 2, TA, "v", 0, 40, 40, 4)],
        [(1, 2, TX, "qk", 8, 60, 40, 6), (1, 1, TA, "kv", 4, 76, 56, 8)],
    ]
    WQKV = [a_wqkv[0], b_wqkv[0]]

    def load_qkv(sp, l, C, par, col):
        sp.wait_ge(s_qwfree, C + 1)
        sp.dma_start(qw[:, par], WQKV[l].rearrange("(k p) n -> p k n", p=P)[:, :, ds(col, HALF)]).then_inc(s_qw[par], 16)

    def sp_first_weights(sp, l):
        for n in range(2):
            load_qkv(sp, l, 6 * l + n, n, n * HALF)

    def sp_qkv(sp, l):
        def pair(i):
            for par in range(2):
                load_qkv(sp, l, 2 * i + 2 + par, par, (2 * i + 2 + par) * HALF)
        if l == 0:
            trips(sp, 2, pair)
        else:
            load_qkv(sp, l, 8, 0, 2 * HALF)
            for t in range(TA):
                sp.wait_ge(s_vev, t + 1)
                sp.dma_start(v_d[t * P:(t + 1) * P, :], vstg[:, t, :]).then_inc(s_vst, 16)
            sp.wait_ge(s_vst, 16 * TA)

    def pe_qkv(pe, l):
        for ntrip, nch, nt, kind, heads, U0, R0, C0 in SECTIONS[l]:
            def body(i):
                def transposes(j):
                    R = R0 + nch * nt * i + j
                    pe.wait_ge(s_qrot, R + 1)
                    pe.wait_ge(s_qev, R + 1)
                    for b in range(heads // 2):
                        ins = nc.tensor.transpose(psum[:, 2 + j % 2, b * P:(b + 1) * P], qrot[:, j % 2, b * P:(b + 1) * P], ident)
                    ins.then_inc(s_qtr, 1)
                for ci in range(nch):
                    C = C0 + nch * i + ci
                    pe.wait_ge(s_qw[ci % 2], 16 * (C0 // 2 + i + 1))
                    for t in range(nt):
                        j = ci * nt + t
                        U = U0 + nch * nt * i + j
                        pe.wait_ge(s_qaccfree, U + 1)
                        for k in range(KD):
                            ins = nc.tensor.matmul(psum[:, j % 2, :], hT[:, k, t * P:(t + 1) * P], qw[:, ci % 2, k], start=(k == 0), stop=(k == KD - 1))
                        ins.then_inc(s_qacc, 1)
                        if t == nt - 1:
                            pe.wait_ge(s_qacc, U + 1)
                            pe.sem_inc(s_qwfree, 1)
                        if heads and j:
                            transposes(j - 1)
                if heads:
                    transposes(nch * nt - 1)
            trips(pe, ntrip, body)

    def act_qkv(act, l):
        if l == 0:
            act.sem_inc(s_qaccfree, 2)
            act.sem_inc(s_qst[0], 16)
            act.sem_inc(s_qst[1], 16)
        for ntrip, nch, nt, kind, heads, U0, R0, C0 in SECTIONS[l]:
            def body(i):
                def evac(j):
                    R = R0 + nch * nt * i + j
                    nb = heads // 2
                    act.wait_ge(s_qtr, R + 3)
                    act.wait_ge(s_qst[j % 2], 32 * ((R0 + nch * nt * i) // 2 + j // 2) + 16)
                    nc.scalar.activation(qstg[:, j % 2, 0, 0:nb], psum[:, 2 + j % 2, 0:nb * P].rearrange("p (b n) -> p b n", b=nb), ACT.Copy).then_inc(s_qhi, 1)
                    act.wait_ge(s_qev, R + 3)
                    q0 = (C0 - 6 * l + nch * i + j // nt) * 4
                    for part in range(2):
                        act.dma_start(qk_d[ds(q0, nb), part, :, (j % nt) * P:(j % nt + 1) * P].rearrange("h p n -> p h n"), qstg[:, j % 2, part, 0:nb].bitcast(F32)).then_inc(s_qst[j % 2], 16)
                for j in range(nch * nt):
                    U = U0 + nch * nt * i + j
                    act.wait_ge(s_qacc, U + 1)
                    if kind == "v":
                        nc.scalar.activation(V[:, j % nt, (j // nt) * HALF:(j // nt + 1) * HALF], psum[:, j % 2, :], ACT.Copy).then_inc(s_qaccfree, 1)
                    if kind == "kv":
                        nc.scalar.activation(vstg[:, j, :], psum[:, j % 2, 256:512], ACT.Copy).then_inc(s_vev, 1)
                    if heads:
                        nc.scalar.activation(qsq[:, j % 2, 0:heads * HD], psum[:, j % 2, 0:heads * HD], ACT.Square, scale=1 / 8).then_inc(s_qsq, 1)
                        if j:
                            evac(j - 1)
                if heads:
                    evac(nch * nt - 1)
            trips(act, ntrip, body)
        for par in range(2):
            act.wait_ge(s_qst[par], 16 + 32 * [40, 66][l] // 2)

    def pool_qkv(pool, l):
        settled(pool, s_rope, l + 1)
        for ntrip, nch, nt, kind, heads, U0, R0, C0 in SECTIONS[l]:
            if not heads:
                continue

            def body(i):
                which = i if l == 0 else int(kind == "kv")
                for j in range(nch * nt):
                    R = R0 + nch * nt * i + j
                    t, par = j % nt, j % 2
                    pool_rstd(pool, qrs[:, par, 0:heads], qms[:, par, 0:heads], neghalf[:, 0:heads], s_qrs, (s_qms, R + 1))
                    settled(pool, s_qxn, R + 1)
                    src = qxn[:, par, 0:heads * HD].rearrange("p (h a b f) -> p h a b f", a=2, b=2, f=16)
                    dst = qt2[:, par, 0:heads * HD].rearrange("p (h a b f) -> p h a b f", a=2, b=2, f=16)
                    for b in range(2):
                        for a in range(2):
                            o = a * 32 + b * 16
                            if isinstance(which, int):
                                sn = rope[:, which, 1, t, o:o + 16].unsqueeze(1).broadcast_to([P, heads, 16])
                            else:
                                sn = rope[:, ds(which, 1), 1, t, o:o + 16].broadcast_to([P, heads, 16])
                            ins = nc.gpsimd.tensor_tensor(dst[:, :, a, b, :], src[:, :, a, 1 - b, :], sn, ALU.mult)
                    ins.then_inc(s_qt2, 1)
            trips(pool, ntrip, body, poolc, nch * nt)

    def dve_qkv(dve, l):
        dvec.link(dve, nc.vector.tensor_scalar(gains[:, 2 * l], gains[:, 2 * l], SCALE, None, ALU.mult))
        for w in range(2):
            g = gains[:, 2 * l + w]
            gs = g.rearrange("p (a b f) -> p a b f", a=2, b=2)
            nc.vector.tensor_tensor(rope[:, w, 0], cst[:, C_COS:C_COS + TA * HD].rearrange("p (t d) -> p t d", d=HD),
                                    g.unsqueeze(1).broadcast_to([P, TA, HD]), ALU.mult)
            sn = cst[:, C_SIN:C_SIN + TA * HD].rearrange("p (t a b f) -> p t a b f", a=2, b=2, f=16)
            dst = rope[:, w, 1].rearrange("p t (a b f) -> p t a b f", a=2, b=2)
            for a in range(2):
                for b in range(2):
                    ins = nc.vector.tensor_tensor(dst[:, :, a, b, :], sn[:, :, a, b, :],
                                                  gs[:, a, 1 - b, :].unsqueeze(1).broadcast_to([P, TA, 16]), ALU.mult)
        ins.then_inc(s_rope, 1)
        dve.wait_ge(s_rope, l + 1)
        for ntrip, nch, nt, kind, heads, U0, R0, C0 in SECTIONS[l]:
            if not heads:
                continue

            def body(i):
                which = i if l == 0 else int(kind == "kv")
                n = heads * HD

                def low(j):
                    R, m = R0 + nch * nt * i + j, heads // 2 * P
                    dve.wait_ge(s_qhi, R + 1)
                    nc.vector.tensor_tensor(qstg[:, j % 2, 1].rearrange("p b n -> p (b n)")[:, 0:m], psum[:, 2 + j % 2, 0:m],
                                            qstg[:, j % 2, 0].bitcast(F32).rearrange("p b n -> p (b n)")[:, 0:m], ALU.subtract).then_inc(s_qev, 1)
                for j in range(nch * nt):
                    R = R0 + nch * nt * i + j
                    t, par = j % nt, j % 2
                    dve.wait_ge(s_qsq, R + 1)
                    nc.vector.reduce_sum(qms[:, par, 0:heads], qsq[:, par, 0:n].rearrange("p (h d) -> p h d", d=HD), AX).then_inc(s_qms, 1)
                    if j:
                        low(j - 1)
                    dve.wait_ge(s_qrs, R + 1)
                    xn3 = qxn[:, par, 0:n].rearrange("p (h d) -> p h d", d=HD)
                    nc.vector.tensor_tensor(xn3, psum[:, par, 0:n].rearrange("p (h d) -> p h d", d=HD),
                                            qrs[:, par, 0:heads].unsqueeze(2).broadcast_to([P, heads, HD]), ALU.mult).then_inc(s_qxn, 1)
                    dve.wait_ge(s_qxn, R + 1)
                    dve.sem_inc(s_qaccfree, 1)
                    if isinstance(which, int):
                        cos = rope[:, which, 0, t].unsqueeze(1).broadcast_to([P, heads, HD])
                    else:
                        cos = rope[:, ds(which, 1), 0, t].broadcast_to([P, heads, HD])
                    t13 = qt1[:, par, 0:n].rearrange("p (h d) -> p h d", d=HD)
                    dvec.link(dve, nc.vector.tensor_tensor(t13, xn3, cos, ALU.mult))
                    dve.wait_ge(s_qt2, R + 1)
                    dve.wait_ge(s_qtr, R - 1 + 2)
                    nc.vector.tensor_tensor(qrot[:, par, 0:n], qt1[:, par, 0:n], qt2[:, par, 0:n], ALU.add).then_inc(s_qrot, 1)
                low(nch * nt - 1)
            if l == 0:
                dve.sem_inc(s_qtr, 2)
                dve.sem_inc(s_qev, 2)
            trips(dve, ntrip, body, dvec, nch * nt)


    s_kt, s_kc = [sem(f"s_kt{n}") for n in range(3)], sem("s_kc")
    s_aq = [sem("s_aq0"), sem("s_aq1")]
    s_score, s_nmax, s_exp = sem("s_score"), sem("s_nmax"), sem("s_exp")
    s_mix, s_b6, s_b7, s_b6free, s_b7free = sem("s_mix"), sem("s_b6"), sem("s_b7"), sem("s_b6free"), sem("s_b7free")
    s_sumsq, s_fac, s_sinkexp = sem("s_sumsq"), sem("s_fac"), sem("s_sinkexp")
    s_ost = [sem("s_ost0"), sem("s_ost1")]
    s_turn, s_took = [sem(f"s_turn{n}") for n in range(3)], [sem(f"s_took{n}") for n in range(3)]
    s_av, s_raw, s_on = sem("s_av"), sem("s_raw"), sem("s_on")
    A = Arena("att0", after_V)
    kT = A("kT", [P, 2 * KD, NTOK], F32R)
    B = Arena("att1", arena0_at + 4 * KD * D)
    kc = B("kc", [P, 4, CTX], F32R)
    vc = B("vc", [P, TC, 256])
    kw = B("kw", [P, 2, 4, 3 * P], F32R)
    vw = B("vw", [P, 2, 3, 256])
    es = B("es", [P, 2, 2])
    A = Arena("att", max(A.at, B.at))
    aq = A("q", [P, 2, 2, 4, 2, P], F32R)
    prob = A("prob", [P, 4 * NTOK])
    aT = A("aT", [P, 2, 10, P])
    nmax = A("nmax", [P, 2, 2])
    mx = A("mx", [P, 2, 2])
    den = A("den", [P, 2, 2])
    rden = A("rden", [P, 2, 2])
    coef = A("coef", [P, 2, 1])
    epsum = A("epsum", [P, 2, 1])
    osq = A("osq", [P, 2, P])
    ssq = A("ssq", [P, 2, 1])
    fac = A("fac", [P, 2, 1])
    raw = A("raw", [P, 2, P])
    on = A("on", [P, 2, P])
    oTs = A("oTs", [P, 2, KD, P])
    KWID = CTX + 3 * P

    def probs(l, j, m, lo, hi):
        at = (2 * (j % 2) + m) * (KWID if l else NTOK)
        return prob[:, at + lo:at + hi]

    class Plan:

        def __init__(self, nblk, base):
            self.nblk, self.base = nblk, base
            self.use6, self.use7 = {}, {}
            n6 = n7 = 0
            for j in range(16):
                total = self.blocks(j)
                self.use6[j, "a"] = n6
                n6 += 1
                if total > 4:
                    self.use7[j, "b"] = n7
                    n7 += 1
                if total > 8:
                    self.use6[j, "c"] = n6
                    n6 += 1
                self.use7[j, "o"] = n7
                n7 += 1
            self.n6, self.n7 = n6, n7

        def blocks(self, j):
            return self.nblk[j // 8] * 2

    PARTS = []
    u6 = u7 = units = 0
    for l, ntrip, t0, kinds, nblk in [(0, TX // 2, 0, ("all", "all"), (10, 10)), (0, 1, TX, ("ctx", "ctx"), (2, 2)),
                                      (1, 1, 0, ("first", "last"), (4, 4)), (1, TX // 2 - 1, 1, ("mid", "mid"), (5, 5))]:
        plan = Plan(nblk, (u6, u7, units))
        PARTS.append((l, ntrip, t0, kinds, nblk, plan))
        units += 16 * ntrip
        if l:
            u6, u7 = u6 + ntrip * plan.n6, u7 + ntrip * plan.n7

    def tile_of(t0, kinds, i, par):
        return par * (TX - 1) if kinds[0] == "first" else t0 + 2 * i + par

    def at(plan, i):
        return plan.base[0] + i * plan.n6, plan.base[1] + i * plan.n7, plan.base[2] + i * 16

    def pair_no(plan, i):
        return plan.base[2] // 16 + i

    def win_no(plan, i):
        return pair_no(plan, i) - (PARTS[0][1] + PARTS[1][1])

    def halves(eng, dst, lo, hi, cols, s):
        for part in range(2):
            for m in range(2):
                eng.dma_start(dst[64 * part:64 * part + 64, m:2 * (hi - lo):2].bitcast(F32), qk_d[lo:hi, part, 64 * m:64 * m + 64, cols].rearrange("h d n -> d h n")).then_inc(s, 16)

    KEY_GROUPS = [(0, 2), (2, 4), (4, 8)]

    def load_keys(eng, n):
        lo, hi = KEY_GROUPS[n]
        halves(eng, kT[:, 2 * lo:2 * hi], KD + lo, KD + hi, slice(0, NTOK), s_kt[n])

    def sp_att(sp, l):
        if l == 0:
            load_keys(sp, 0)
        else:
            halves(sp, kc, 8, 10, slice(SEQ, NTOK), s_kc)
            sp.dma_start(vc[:, :, :], v_d[SEQ:, :].rearrange("(t p) n -> p t n", p=P)).then_inc(s_kc, 16)
        for pl, ntrip, t0, kinds, nblk, plan in PARTS:
            if pl != l:
                continue

            def body(i):
                for par in range(2):
                    t = tile_of(t0, kinds, i, par)
                    if l:
                        sp.wait_ge(s_winfree, 2 * win_no(plan, i) + par + 1)
                        lo = {"first": 0, "last": t - 1, "mid": t - 1}[kinds[par]]
                        w = {"first": 2, "last": 2, "mid": 3}[kinds[par]]
                        halves(sp, kw[:, par, :, 0:w * P], 8, 10, ds(lo * P, w * P), s_win[par])
                        sp.dma_start(vw[:, par, 0:w, :], v_d[ds(lo * P, w * P), :].rearrange("(b p) n -> p b n", p=P)).then_inc(s_win[par], 16)
                    for half in range(2):
                        sp.wait_ge(s_score, 8 * (4 * pair_no(plan, i) + 2 * par + half) + 8)
                        src = qk_d[4 * half:4 * half + 4, :, :, ds(t * P, P)]
                        for rows in range(2):
                            for m in range(2):
                                sp.dma_start(aq[64 * rows:64 * rows + 64, half, m].bitcast(F32).rearrange("d u x n -> d (u x) n"),
                                             src[:, :, 64 * m:64 * m + 64, :].rearrange("u x d n -> d (u x) n")).then_inc(s_aq[half], 16)
            trips(sp, ntrip, body)
        if l:
            load_wo(sp, l)

    def pool_att(pool, l):
        for pl, ntrip, t0, kinds, nblk, plan in PARTS:
            if pl != l or l:
                continue

            def body(i):
                u0 = at(plan, i)[2]
                for j in range(16):
                    settled(pool, s_fac, u0 + j + 1)
                    poolc.link(pool, nc.gpsimd.tensor_tensor(fac[:, j % 2], ssq[:, j % 2], neghalf[:, 0:1], ALU.pow))
                    settled(pool, s_turn[2], turn_no(plan, i) + j + 1)
                    nc.gpsimd.tensor_scalar(on[:, j % 2], raw[:, j % 2], fac[:, j % 2], None, ALU.mult).then_inc(s_on, 1)
            if t0 == 0:
                pool.sem_inc(s_on, 2)
            trips(pool, ntrip, body, poolc, 16)

    s_winfree, s_win = sem("s_winfree"), [sem("s_win0"), sem("s_win1")]

    def pe_att(pe, l):
        if l == 0:
            pe.sem_inc(s_winfree, 2)
            pe.sem_inc(s_score, 16)
        if l:
            pe.wait_ge(s_kc, 80)
        for pl, ntrip, t0, kinds, nblk, plan in PARTS:
            if pl != l:
                continue

            def body(i):
                b6, b7, u0 = at(plan, i)

                def scores(j, m):
                    par, h, kind = j // 8, j % 8, kinds[j // 8]
                    if h % 4 == 0 and m == 0:
                        pe.wait_ge(s_aq[h // 4], 64 * (2 * pair_no(plan, i) + par + 1))
                    if l == 0 and m == 0:
                        for n, (lo, hi) in enumerate(KEY_GROUPS):
                            if h == lo:
                                pe.wait_ge(s_kt[n], 64)
                    if l and h == 0 and m == 0:
                        pe.wait_ge(s_win[par], 80 * (win_no(plan, i) + 1))
                    pe.wait_ge(s_exp, 2 * (u0 + j) + m + 1)

                    def product(o, k, masked=None):
                        for x in range(2):
                            ins = nc.tensor.matmul(o, aq[:, h // 4, m, h % 4, x, :], k, start=x == 0, stop=x == 1 and masked is None)
                        if masked is not None:
                            ins = nc.tensor.matmul(o, ident_h[:, :], masked, start=False, stop=True)
                        return ins
                    if l == 0:
                        key = kT[:, 2 * h + m]
                        if kind == "all":
                            for b, (lo, hi) in enumerate(((0, 512), (512, 1024), (1024, 1280))):
                                ins = product(psum[:, 3 * m + b, 0:hi - lo], key[:, lo:hi])
                        else:
                            ins = product(psum[:, 3 * m, 0:CTX], key[:, SEQ:])
                    else:
                        g = h // 2
                        product(psum[:, 3 * m, 0:CTX], kc[:, g])
                        ins = product(psum[:, 3 * m, CTX:HALF], kw[:, par, g, 0:2 * P], mask_h[:, int(kind == "first")].rearrange("p b n -> p (b n)"))
                        if kind == "mid":
                            ins = product(psum[:, 3 * m + 1, 0:P], kw[:, par, g, 2 * P:3 * P], mask_h[:, 1, 1])
                    ins.then_inc(s_score, 1)

                scores(0, 0)
                scores(0, 1)
                if l == 0:
                    pe_units0(pe, plan, i, u0, kinds, nblk, scores)
                else:
                    pe_units1(pe, i, b6, b7, u0, nblk, plan, scores)
            trips(pe, ntrip, body)

    def turn_no(plan, i):
        return 17 * pair_no(plan, i)

    def pe_units0(pe, plan, i, u0, kinds, nblk, scores):
        t0 = turn_no(plan, i)

        def blocks(j, lo, hi, bank):
            for b in range(lo, hi):
                ins = nc.tensor.transpose(psum[:, bank, (b - lo) * P:(b - lo + 1) * P], probs(0, j, 0, b * P, (b + 1) * P), ident)
            return ins

        def turn_output(j, at):
            pe.wait_ge(s_on, u0 + j + 3)
            return nc.tensor.transpose(psum[:, 6, at * P:(at + 1) * P], on[:, j % 2], ident)

        def turn(j):
            nb = nblk[j // 8]
            pe.wait_ge(s_mix, u0 + j + 1)
            pe.wait_ge(s_took[2], t0 + j + 1)
            blocks(j, 0, min(4, nb), 6).then_inc(s_turn[0], 1)
            if nb > 4:
                pe.wait_ge(s_raw, u0 + j + 1)
                blocks(j, 4, 8, 7).then_inc(s_turn[1], 1)

        def turn_last(j):
            nb = nblk[j // 8]
            pe.wait_ge(s_took[0], u0 + j + 1)
            if nb > 8:
                ins = blocks(j, 8, nb, 6)
            if j >= 2:
                ins = turn_output(j - 2, 2)
            if nb > 8 or j >= 2:
                ins.then_inc(s_turn[2], 1)
            else:
                pe.sem_inc(s_turn[2], 1)

        def output(j):
            nb, h = nblk[j // 8], j % 8
            pe.wait_ge(s_took[0], u0 + j + 1)
            pe.wait_ge(s_raw, u0 + j + 1)
            if nb > 4:
                pe.wait_ge(s_took[1], u0 + j + 1)
            for b in range(nb):
                if b == 8:
                    pe.wait_ge(s_took[2], t0 + j + 2)
                v = V[:, b if kinds[j // 8] == "all" else TX + b, h * P:(h + 1) * P]
                ins = nc.tensor.matmul(psum[:, 7, 0:P], aT[:, j % 2, b, :], v, start=(b == 0), stop=(b == nb - 1))
            ins.then_inc(s_av, 1)

        scores(1, 0)
        scores(1, 1)
        for j in range(16):
            turn(j)
            if j < 14:
                scores(j + 2, 0)
            turn_last(j)
            output(j)
            if j < 14:
                scores(j + 2, 1)
        pe.wait_ge(s_took[2], t0 + 17)
        turn_output(14, 0)
        turn_output(15, 1).then_inc(s_turn[2], 1)

    def pe_units1(pe, i, b6, b7, u0, nblk, plan, scores):
        def turn(j, bank, lo, hi):
            for b in range(lo, hi):
                ins = nc.tensor.transpose(psum[:, bank, (b - lo) * P:(b - lo + 1) * P], probs(1, j, b % 2, b // 2 * P, (b // 2 + 1) * P), ident)
            ins.then_inc(s_b6 if bank == 6 else s_b7, 1)

        scores(1, 0)
        scores(1, 1)
        for j in range(16):
            par, g, nb = j // 8, j % 8 // 2, nblk[j // 8]
            total = plan.blocks(j)
            pe.wait_ge(s_mix, u0 + j + 1)
            pe.wait_ge(s_b6free, b6 + plan.use6[j, "a"] + 1)
            turn(j, 6, 0, 4)
            pe.wait_ge(s_b7free, b7 + plan.use7[j, "b"] + 1)
            turn(j, 7, 4, 8)
            if j < 14:
                scores(j + 2, 0)
            if total > 8:
                pe.wait_ge(s_b6free, b6 + plan.use6[j, "c"] + 1)
                turn(j, 6, 8, total)
            pe.wait_ge(s_b6free, b6 + plan.use6[j, "c" if total > 8 else "a"] + 2)
            pe.wait_ge(s_b7free, b7 + plan.use7[j, "o"] + 1)
            for b in range(nb):
                v = vc[:, b, g * HD:(g + 1) * HD] if b < TC else vw[:, par, b - TC, g * HD:(g + 1) * HD]
                ins = nc.tensor.matmul(psum[0:HD, 7, 0:2 * P], v, aT[:, j % 2, 2 * b:2 * b + 2, :].rearrange("p m n -> p (m n)"),
                                       start=(b == 0), stop=(b == nb - 1))
            ins.then_inc(s_b7, 1)
            if j < 14:
                scores(j + 2, 1)
            if j % 8 == 7:
                pe.wait_ge(s_b7, b7 + plan.use7[j, "o"] + 1)
                pe.sem_inc(s_winfree, 1)

    def act_att(act, l):
        if l == 0:
            act.wait_ge(s_kt[0], 64)
            load_keys(act, 1)
            load_keys(act, 2)
        for pl, ntrip, t0, kinds, nblk, plan in PARTS:
            if pl != l:
                continue

            def body(i):
                b6, b7, u0 = at(plan, i)

                def expo(j, m):
                    width = nblk[j // 8] * P
                    n = 2 * (u0 + j) + m
                    act.wait_ge(s_nmax, n + 1)
                    if l and j >= 2:
                        act.wait_ge(s_b7, b7 + plan.use7[j - 2, "b"] + 1)
                    nc.scalar.activation(probs(l, j, m, 0, width), psum[:, 3 * m:3 * m + 3, :].rearrange("p b n -> p (b n)")[:, 0:width], ACT.Exp,
                                         bias=nmax[:, j % 2, m:m + 1], accum_out=den[:, j % 2, m:m + 1]).then_inc(s_exp, 1)
                    if l:
                        h = 2 * (j % 8) + m
                        nc.scalar.activation(es[:, j % 2, m:m + 1], nmax[:, j % 2, m:m + 1], ACT.Exp, bias=sinks[:, h:h + 1]).then_inc(s_sinkexp, 1)

                def store(par):
                    act.dma_start(o_d[ds(tile_of(t0, kinds, i, par), 1)].rearrange("o p n -> p (o n)"),
                                  oTs[:, par].rearrange("p k n -> p (k n)")).then_inc(s_ost[par], 16)

                def take(j, bank, lo, hi, col=0):
                    return nc.scalar.activation(aT[:, j % 2, lo:hi, :], psum[:, bank, col:col + (hi - lo) * P].rearrange("p (b n) -> p b n", n=P), ACT.Copy)

                t2 = turn_no(plan, i)

                def square(j):
                    act.wait_ge(s_raw, u0 + j + 2)
                    nc.scalar.activation(osq[:, j % 2], raw[:, j % 2], ACT.Square, accum_out=ssq[:, j % 2]).then_inc(s_sumsq, 1)

                def put(j, at):
                    if j % 8 == 0:
                        act.wait_ge(s_ost[j // 8], 16 + 16 * pair_no(plan, i))
                    ins = nc.scalar.activation(oTs[:, j // 8, j % 8, :], psum[:, 6, at * P:(at + 1) * P], ACT.Copy, scale=subg[:, 0:1])
                    return ins

                def pieces0(j):
                    nb = nblk[j // 8]
                    act.wait_ge(s_turn[0], u0 + j + 1)
                    take(j, 6, 0, min(4, nb)).then_inc(s_took[0], 1)
                    if nb > 4:
                        act.wait_ge(s_turn[1], u0 + j + 1)
                        take(j, 7, 4, 8).then_inc(s_took[1], 1)

                def last_piece0(j):
                    nb = nblk[j // 8]
                    act.wait_ge(s_turn[2], t2 + j + 1)
                    if nb > 8:
                        ins = take(j, 6, 8, nb)
                    if j >= 2:
                        ins = put(j - 2, 2)
                    if nb > 8 or j >= 2:
                        ins.then_inc(s_took[2], 1)
                    else:
                        act.sem_inc(s_took[2], 1)
                    if j - 2 == 7:
                        act.wait_ge(s_took[2], t2 + j + 2)
                        store(0)

                def piece1(j):
                    act.wait_ge(s_b6, b6 + plan.use6[j, "a"] + 1)
                    take(j, 6, 0, 4).then_inc(s_b6free, 1)

                def last_piece1(j):
                    if (j, "c") in plan.use6:
                        act.wait_ge(s_b6, b6 + plan.use6[j, "c"] + 1)
                        take(j, 6, 8, plan.blocks(j)).then_inc(s_b6free, 1)

                expo(0, 0)
                expo(0, 1)
                if l:
                    expo(1, 0)
                for j in range(16):
                    if l == 0:
                        if j < 15:
                            expo(j + 1, 0)
                        if j:
                            square(j - 1)
                        pieces0(j)
                        if j < 15:
                            expo(j + 1, 1)
                        last_piece0(j)
                    else:
                        piece1(j)
                        if j < 15:
                            expo(j + 1, 1)
                        last_piece1(j)
                        if j < 14:
                            expo(j + 2, 0)
                        if j % 8 == 7:
                            act.wait_ge(s_b7free, b7 + plan.use7[j, "o"] + 2)
                            store(j // 8)
                if l == 0:
                    square(15)
                    act.wait_ge(s_turn[2], t2 + 17)
                    put(14, 0)
                    put(15, 1).then_inc(s_took[2], 1)
                    act.wait_ge(s_took[2], t2 + 18)
                    store(1)
            if l == 0 and t0 == 0:
                for s in s_ost:
                    act.sem_inc(s, 16)
                act.sem_inc(s_took[2], 1)
                act.sem_inc(s_b6free, 1)
                act.sem_inc(s_exp, 2)
            trips(act, ntrip, body)
        for par in range(2):
            act.wait_ge(s_ost[par], 16 + 16 * sum(p[1] for p in PARTS if p[0] <= l))

    def dve_att(dve, l):
        for pl, ntrip, t0, kinds, nblk, plan in PARTS:
            if pl != l:
                continue

            def body(i):
                b6, b7, u0 = at(plan, i)

                def peak(j, m):
                    width = nblk[j // 8] * P
                    score = psum[:, 3 * m:3 * m + 3, :].rearrange("p b n -> p (b n)")[:, 0:width]
                    dve.wait_ge(s_score, 2 * (u0 + j) + m + 1 + 16)
                    if l == 0:
                        nc.vector.reduce_max(nmax[:, j % 2, m:m + 1], score, AX, negate=True).then_inc(s_nmax, 1)
                    else:
                        h = 2 * (j % 8) + m
                        dvec.link(dve, nc.vector.reduce_max(mx[:, j % 2, m:m + 1], score, AX, negate=True))
                        nc.vector.tensor_tensor(nmax[:, j % 2, m:m + 1], mx[:, j % 2, m:m + 1], negsink[:, h:h + 1], ALU.min).then_inc(s_nmax, 1)

                def weigh(j):
                    width = nblk[j // 8] * P
                    q = j % 2
                    if l:
                        dve.wait_ge(s_sinkexp, 2 * (16 * win_no(plan, i) + j) + 2)
                        dvec.link(dve, nc.vector.tensor_tensor(rden[:, q], den[:, q], es[:, q], ALU.add))
                        dvec.link(dve, nc.vector.reciprocal(rden[:, q], rden[:, q]))
                        for m in range(2):
                            p = probs(l, j, m, 0, width)
                            ins = nc.vector.tensor_scalar(p, p, rden[:, q, m:m + 1], None, ALU.mult)
                        ins.then_inc(s_mix, 1)
                        return
                    dve.wait_ge(s_exp, 2 * (u0 + j) + 2 + 2)
                    dvec.link(dve, nc.vector.reciprocal(rden[:, q, 1:2], den[:, q, 1:2]))
                    nc.vector.scalar_tensor_tensor(epsum[:, q], den[:, q, 0:1], EPS, den[:, q, 0:1], ALU.mult, ALU.mult)
                    dvec.link(dve, nc.vector.scalar_tensor_tensor(coef[:, q], den[:, q, 0:1], neglam[:, 0:1], rden[:, q, 1:2], ALU.mult, ALU.mult))
                    nc.vector.scalar_tensor_tensor(probs(l, j, 0, 0, width), probs(l, j, 1, 0, width), coef[:, q], probs(l, j, 0, 0, width), ALU.mult, ALU.add).then_inc(s_mix, 1)

                def factor(j):
                    q = j % 2
                    dve.wait_ge(s_sumsq, u0 + j + 1)
                    nc.vector.scalar_tensor_tensor(ssq[:, q], ssq[:, q], 1 / P, epsum[:, q], ALU.mult, ALU.add).then_inc(s_fac, 1)

                def copy_output(j):
                    dve.wait_ge(s_av, u0 + j + 1)
                    dve.wait_ge(s_on, u0 + j + 1)
                    nc.vector.tensor_copy(raw[:, j % 2], psum[:, 7, 0:P]).then_inc(s_raw, 1)

                def piece1(j):
                    dve.wait_ge(s_b7, b7 + plan.use7[j, "b"] + 1)
                    nc.vector.tensor_copy(aT[:, j % 2, 4:8, :], psum[:, 7, :].rearrange("p (b n) -> p b n", n=P)).then_inc(s_b7free, 1)

                def finish1(j):
                    dve.wait_ge(s_b7, b7 + plan.use7[j, "o"] + 1)
                    if j % 8 == 0:
                        dve.wait_ge(s_ost[j // 8], 16 + 16 * pair_no(plan, i))
                    for m in range(2):
                        ins = nc.vector.tensor_copy(oTs[64 * m:64 * m + 64, j // 8, j % 8, :], psum[0:HD, 7, m * P:(m + 1) * P])
                    ins.then_inc(s_b7free, 1)

                peak(0, 0)
                peak(0, 1)
                if l:
                    peak(1, 0)
                    weigh(0)
                for j in range(16):
                    if l == 0:
                        if j < 15:
                            peak(j + 1, 0)
                        weigh(j)
                        if j:
                            copy_output(j - 1)
                        if j < 15:
                            peak(j + 1, 1)
                        if j:
                            factor(j - 1)
                    else:
                        if j < 15:
                            peak(j + 1, 1)
                        piece1(j)
                        if j < 14:
                            peak(j + 2, 0)
                        if j < 15:
                            weigh(j + 1)
                        finish1(j)
                if l == 0:
                    copy_output(15)
                    factor(15)
            if l == 0 and t0 == 0:
                dve.sem_inc(s_b7free, 1)
                dve.sem_inc(s_raw, 1)
            trips(dve, ntrip, body, dvec, 16 * (2 + 2 * l))

    s_pw = [sem("s_pw0"), sem("s_pw1")]
    s_pin = [sem("s_pin0"), sem("s_pin1")]
    s_pinfree, s_y, s_x1, s_x1ss, s_x1rs, s_h, s_h2 = [sem(n) for n in ("s_pinfree", "s_y", "s_x1", "s_x1ss", "s_x1rs", "s_h", "s_h2")]
    s_h2t, s_h2ta, s_h2td, s_rl, s_rld = [sem(n) for n in ("s_h2t", "s_h2ta", "s_h2td", "s_rl", "s_rld")]
    s_x1st = [sem("s_x1st0"), sem("s_x1st1")]
    s_h2st = [sem("s_h2st0"), sem("s_h2st1")]
    s_bc, s_bcd = [sem("s_bc0"), sem("s_bc1")], sem("s_bcd")
    A = Arena("post")
    wo = A("wo", [P, KD, D])
    bc = A("bc", [P, 2, 4, D])
    oT = A("oT", [P, 2, KD, P])
    xt = A("xt", [P, 2, D])
    x1 = A("x1", [P, 2, D])
    xsq = A("sq", [P, 2, D])
    xss = A("ss", [P, 2])
    xrs = A("rs", [P, 2])
    hm = A("hm", [P, 2, D])
    h2 = A("h2", [P, 2, D])
    h2T = A("h2T", [P, 2, KD, P])

    def load_wo(sp, l):
        for n in range(2):
            sp.dma_start(wo[:, :, n * HALF:(n + 1) * HALF], [a_wo, b_wo][l][0, :, n * HALF:(n + 1) * HALF].rearrange("(k p) n -> p k n", p=P)).then_inc(s_pw[n], 16)

    def sp_post(sp, l):
        def step(t, par):
            T = TA * l + t
            if l:
                src = xs_d[ds(t * P, P), :]
            else:
                src = ctx[0, (t - TX) * P:(t - TX + 1) * P, :] if isinstance(t, int) and t >= TX else x[0, ds(t * P, P), :]
            sp.wait_ge(s_pinfree, T + 1)
            sp.dma_start(oT[:, par].rearrange("p k n -> p (k n)"), o_d[ds(t, 1)].rearrange("o p n -> p (o n)")).then_inc(s_pin[par], 16)
            sp.dma_start(xt[:, par], src).then_inc(s_pin[par], 16)
            if isinstance(t, int) and t == 0 and l == 0:
                load_wo(sp, l)
            if isinstance(t, int) and t < 2 - l:
                for n, src in enumerate([mod_d[l, t:t + 1, 2 * D:3 * D], mod_d[l, t:t + 1, 3 * D:4 * D],
                                         mod_d[l, t:t + 1, 4 * D:5 * D], norm2_g[l:l + 1, :]]):
                    sp.dma_start(bc[:, t, n], src.broadcast_to([P, D])).then_inc(s_bc[t], 16)
        tile_steps(sp, TILES[l], step)

    def pin_count(T, par):
        return 16 * (T - par + 2)

    def pe_post(pe, l):
        def turn(T, par):
            pe.wait_ge(s_h2, T + 1)
            pe.wait_ge(s_h2ta, T + 1)
            pe.wait_ge(s_h2td, T + 1)
            for k in range(KD):
                ins = nc.tensor.transpose(psum[:, 4 + k // 4, (k % 4) * P:(k % 4 + 1) * P], h2[:, par, k * P:(k + 1) * P], ident)
            ins.then_inc(s_h2t, 1)

        def route(T, par):
            pe.wait_ge(s_h2ta, T + 2)
            pe.wait_ge(s_h2td, T + 2)
            pe.wait_ge(s_rld, T + 1)
            for k in range(KD):
                ins = nc.tensor.matmul(psum[:, 6 + par, 0:NG + NE], h2T[:, par, k, :], wrt[:, l, k, :], start=(k == 0), stop=(k == KD - 1))
            ins.then_inc(s_rl, 1)

        def step(t, par):
            T = TA * l + t
            first = isinstance(t, int) and t < 2
            pe.wait_ge(s_pin[par], pin_count(T, par))
            pe.wait_ge(s_x1, T + 1)
            for n in range(2):
                if first:
                    pe.wait_ge(s_pw[n], 16 * (l + 1))
                for k in range(KD):
                    ins = nc.tensor.matmul(psum[:, 2 * par + n, :], oT[:, par, k, :], wo[:, k, n * HALF:(n + 1) * HALF], start=(k == 0), stop=(k == KD - 1))
                if n == 0 and not first:
                    route(T - 2, par)
            ins.then_inc(s_y, 1)
            if not (first and t == 0):
                turn(T - 1, 1 - par)
        if l == 0:
            pe.sem_inc(s_pinfree, 2)
        tile_steps(pe, TILES[l], step)
        T = TA * l + TILES[l]
        route(T - 2, 0)
        turn(T - 1, 1)
        route(T - 1, 1)

    def dve_post(dve, l):
        if l == 0:
            dve.sem_inc(s_x1, 2)
            dve.sem_inc(s_rld, 2)
            dve.sem_inc(s_h2td, 1)

        def upper(T, par):
            dve.wait_ge(s_h2t, T + 1)
            nc.vector.tensor_copy(h2T[:, par, 4:8, :], psum[:, 5, :].rearrange("p (b n) -> p b n", b=4)).then_inc(s_h2td, 1)

        def logit(t, par):
            T = TA * l + t
            dve.wait_ge(s_rl, T + 1)
            nc.vector.tensor_tensor(logits[:, ds(t, 1), :].rearrange("p o n -> p (o n)"), psum[:, 6 + par, 0:NG + NE], brt[:, l, :], ALU.add).then_inc(s_rld, 1)

        def step(t, par):
            T = TA * l + t
            s = int(isinstance(t, int) and t >= TX)
            begin = isinstance(t, int) and t in (0, TX)
            if begin:
                dve.wait_ge(s_bc[s], 64 * (1 + l))
                nc.vector.scalar_tensor_tensor(bc[:, s, 2], bc[:, s, 2], 1.0, bc[:, s, 3], ALU.add, ALU.mult).then_inc(s_bcd, 1)
            dve.wait_ge(s_pin[par], pin_count(T, par))
            dve.wait_ge(s_y, T + 1)
            dve.wait_ge(s_x1st[par], 8 * (T - par + 2))
            y = psum[:, 2 * par:2 * par + 2, :].rearrange("p b n -> p (b n)")
            dvec.link(dve, nc.vector.tensor_tensor(x1[:, par], y, bc[:, s, 0], ALU.mult))
            dvec.link(dve, nc.vector.tensor_tensor(x1[:, par], x1[:, par], xt[:, par], ALU.add))
            dve.sem_inc(s_x1, 1)
            dve.sem_inc(s_pinfree, 1)
            later = not (isinstance(t, int) and t == 0)
            if later:
                upper(T - 1, 1 - par)
            if begin:
                dve.wait_ge(s_bcd, 1 + s + 2 * l)
            dve.wait_ge(s_x1rs, T + 1)
            nc.vector.scalar_tensor_tensor(hm[:, par], x1[:, par], xrs[:, par:par + 1], bc[:, s, 2], ALU.mult, ALU.mult).then_inc(s_h, 1)
            if later:
                logit(t - 1, 1 - par)
        tile_steps(dve, TILES[l], step, dvec, 2)
        upper(TA * l + TILES[l] - 1, 1)
        logit(TILES[l] - 1, 1)

    def act_post(act, l):
        if l == 0:
            for s in s_x1st + s_h2st:
                act.sem_inc(s, 16)
            act.sem_inc(s_h2ta, 1)

        def lower(t, par):
            T = TA * l + t
            act.wait_ge(s_h2t, T + 1)
            nc.scalar.activation(h2T[:, par, 0:4, :], psum[:, 4, :].rearrange("p (b n) -> p b n", b=4), ACT.Copy).then_inc(s_h2ta, 1)
            act.dma_start(h2_d[ds(t * P, P), :], h2[:, par]).then_inc(s_h2st[par], 16)

        def step(t, par):
            T = TA * l + t
            act.wait_ge(s_x1, T + 3)
            nc.scalar.activation(xsq[:, par], x1[:, par], ACT.Square, scale=1 / 32, accum_out=xss[:, par:par + 1]).then_inc(s_x1ss, 1)
            act.dma_start(xs_d[ds(t * P, P), :], x1[:, par]).then_inc(s_x1st[par], 16)
            if not (isinstance(t, int) and t == 0):
                lower(t - 1, 1 - par)
        tile_steps(act, TILES[l], step)
        lower(TILES[l] - 1, 1)
        for s in s_x1st + s_h2st:
            act.wait_ge(s, 16 + 16 * (TA // 2 if l == 0 else (TA + TX) // 2))

    def pool_post(pool, l):
        def step(t, par):
            T = TA * l + t
            s = int(isinstance(t, int) and t >= TX)
            pool_rstd(pool, xrs[:, par:par + 1], xss[:, par:par + 1], neghalf[:, 0:1], s_x1rs, (s_x1ss, T + 1))
            settled(pool, s_h, T + 1)
            settled(pool, s_h2st[par], 8 * (T - par + 2))
            nc.gpsimd.tensor_tensor(h2[:, par], hm[:, par], bc[:, s, 1], ALU.add).then_inc(s_h2, 1)
        tile_steps(pool, TILES[l], step, poolc, 1)

    s_rt, s_rta, s_rtp, s_rtm = sem("s_rt"), sem("s_rta"), sem("s_rtp"), sem("s_rtm")
    A = Arena("route")
    rg = A("rg", [P, TA, 8, NG])
    ru = A("ru", [P, TA, 16])
    re = A("re", [P, TA, 8, NE])
    pre = A("pre", [P, TA, NE])
    tot = A("tot", [P, NE])
    er = A("er", [P, 8, NE])
    eri = A("eri", [P, 2, NE], I32)
    sli = A("sli", [P, 2, TA], I32)
    slf = A("slf", [P, 6, TA])
    cmp_ = A("cmp", [P, NBT, NE])
    ebf = A("ebf", [P, NBT])
    lane1 = A("lane1", [P, 2, TA, P])
    blk1 = A("blk1", [P, 2, TA, NBT])
    tabf = A("tabf", [P, 2, NBT])
    tok2 = A("tok2", [P, TA])

    def dve_route(dve, l):
        nt = TILES[l]
        V_ = nc.vector
        L = lambda ins: dvec.link(dve, ins)

        def pick(val, width, eq, code, top, code_top, one):
            L(V_.reduce_max(top, val, AX))
            L(V_.tensor_tensor(eq, val, top.unsqueeze(2).broadcast_to([P, nt, width]), ALU.is_equal))
            L(V_.tensor_tensor(code, eq, iota[:, P - width:P].unsqueeze(1).broadcast_to([P, nt, width]), ALU.mult))
            L(V_.tensor_scalar(eq, eq, float(P), None, ALU.mult))
            L(V_.tensor_tensor(code, eq, code, ALU.subtract))
            L(V_.reduce_max(code_top, code, AX))
            L(V_.tensor_tensor(one, code, code_top.unsqueeze(2).broadcast_to([P, nt, width]), ALU.is_equal))

        g = lambda n: rg[:, 0:nt, n, :]
        e = lambda n: re[:, 0:nt, n, :]
        u = lambda n: ru[:, 0:nt, n]
        G = logits[:, 0:nt, 0:NG]
        pick(G, NG, g(0), g(1), u(0), u(1), g(2))
        V_.tensor_tensor(g(3), G, u(0).unsqueeze(2).broadcast_to([P, nt, NG]), ALU.subtract).then_inc(s_rt, 1)
        L(V_.tensor_scalar(g(4), g(2), BIG, -BIG, ALU.mult, ALU.add))
        for n in range(NG):
            ins = V_.tensor_tensor(e(0)[:, :, n * EPG:(n + 1) * EPG], logits[:, 0:nt, NG + n * EPG:NG + (n + 1) * EPG],
                                   g(4)[:, :, n:n + 1].broadcast_to([P, nt, EPG]), ALU.add)
        L(ins)
        pick(e(0), NE, e(3), e(4), u(2), u(3), e(1))
        L(V_.scalar_tensor_tensor(e(5), e(1), -2 * BIG, e(0), ALU.mult, ALU.add))
        pick(e(5), NE, e(3), e(4), u(4), u(5), e(2))
        V_.tensor_tensor(u(6), u(4), u(2), ALU.subtract).then_inc(s_rt, 1)
        dve.wait_ge(s_rta, 2 * (l + 1))
        L(V_.reduce_sum(u(7), g(5), AX))
        L(V_.reciprocal(u(7), u(7)))
        L(V_.tensor_scalar(u(9), u(8), 1.0, None, ALU.add))
        L(V_.reciprocal(u(9), u(9)))
        L(V_.tensor_tensor(wsel[:, 0, 0:nt], u(7), u(9), ALU.mult))
        L(V_.tensor_tensor(wsel[:, 1, 0:nt], u(8), wsel[:, 0, 0:nt], ALU.mult))
        L(V_.tensor_tensor(e(6), e(1), e(2), ALU.add))
        L(V_.memset(pre[:, 0], 0.0))
        for t in range(1, nt):
            L(V_.tensor_tensor(pre[:, t], pre[:, t - 1], re[:, t - 1, 6], ALU.add))
        V_.tensor_tensor(tot[:, :], pre[:, nt - 1], re[:, nt - 1, 6], ALU.add).then_inc(s_rtp, 1)
        dve.wait_ge(s_rtm, 2 * l + 1)
        L(V_.tensor_scalar(er[:, 0], psum[:, 1, 0:NE], float(P - 1), None, ALU.add))
        L(V_.tensor_copy(eri[:, 0], er[:, 0]))
        L(V_.tensor_scalar(eri[:, 1], eri[:, 0], 7, None, ALU.arith_shift_right))
        L(V_.tensor_copy(er[:, 1], eri[:, 1]))
        L(V_.memset(er[:, 2], 1.0))
        L(V_.tensor_tensor_scan(er[:, 3], er[:, 2], er[:, 1], 0.0, ALU.mult, ALU.add))
        L(V_.tensor_copy(blkcount[:, l:l + 1], er[:, 3, NE - 1:NE]))
        L(V_.tensor_tensor(er[:, 4], er[:, 3], er[:, 1], ALU.subtract))
        L(V_.tensor_scalar(er[:, 4], er[:, 4], float(P), None, ALU.mult))
        L(V_.tensor_tensor(cmp_[:, :, :], er[:, 3].unsqueeze(1).broadcast_to([P, NBT, NE]),
                           iota[:, 0:NBT].unsqueeze(2).broadcast_to([P, NBT, NE]), ALU.is_le))
        L(V_.reduce_sum(ebf[:, :], cmp_[:, :, :], AX))
        L(V_.tensor_scalar(ebf[:, :], ebf[:, :], float(NE - 1), None, ALU.min))
        L(V_.tensor_copy(exptab[:, :], ebf[:, :]))
        L(V_.tensor_tensor(e(7), psum[:, 0, 0:nt * NE].rearrange("p (t e) -> p t e", e=NE),
                           er[:, 4].unsqueeze(1).broadcast_to([P, nt, NE]), ALU.add))
        for q in range(2):
            L(V_.tensor_tensor(e(3), e(7), e(1 + q), ALU.mult))
            L(V_.reduce_sum(slf[:, q, 0:nt], e(3), AX))
            L(V_.tensor_copy(sli[:, 0, 0:nt], slf[:, q, 0:nt]))
            L(V_.tensor_scalar(sli[:, 1, 0:nt], sli[:, 0, 0:nt], 7, None, ALU.arith_shift_right))
            L(V_.tensor_copy(slf[:, 2 + q, 0:nt], sli[:, 1, 0:nt]))
            L(V_.scalar_tensor_tensor(slf[:, 4 + q, 0:nt], slf[:, 2 + q, 0:nt], -float(P), slf[:, q, 0:nt], ALU.mult, ALU.add))
        L(V_.tensor_scalar(tok2[:, :], tokrow, 1.0, None, ALU.add))
        for q in range(2):
            for t in range(nt):
                V_.tensor_scalar(lane1[:, q, t], iota, slf[:, 4 + q, t:t + 1], None, ALU.is_equal)
                ins = V_.tensor_scalar(blk1[:, q, t], iota[:, 0:NBT], slf[:, 2 + q, t:t + 1], (tok2 if q else tokrow)[:, t:t + 1], ALU.is_equal, ALU.mult)
            L(ins)
        L(V_.memset(tabf[:, 1], 0.0))
        dve.sem_inc(s_rtp, 1)
        dve.wait_ge(s_rtm, 2 * l + 2)
        L(V_.tensor_scalar(tabf[:, 1], psum[:, 2, 0:NBT], 0.0, float(EMPTY), ALU.is_equal, ALU.mult))
        L(V_.scalar_tensor_tensor(tabf[:, 0], psum[:, 2, 0:NBT], -1.0, tabf[:, 1], ALU.add, ALU.add))
        L(V_.tensor_scalar(tabf[:, 0], tabf[:, 0], 0.0, None, ALU.max))
        L(V_.tensor_copy(rowtab[:, :], tabf[:, 0]))
        L(V_.tensor_scalar(toktab[:, :], rowtab[:, :], 1, None, ALU.arith_shift_right))

    def act_route(act, l):
        nt = TILES[l]
        act.wait_ge(s_rt, 2 * l + 1)
        nc.scalar.activation(rg[:, 0:nt, 5, :], rg[:, 0:nt, 3, :], ACT.Exp).then_inc(s_rta, 1)
        act.wait_ge(s_rt, 2 * l + 2)
        nc.scalar.activation(ru[:, 0:nt, 8], ru[:, 0:nt, 6], ACT.Exp).then_inc(s_rta, 1)

    def pe_route(pe, l):
        nt = TILES[l]
        pe.wait_ge(s_rtp, 2 * l + 1)
        nc.tensor.matmul(psum[:, 0, 0:nt * NE].rearrange("p (t e) -> p t e", e=NE), tri, re[:, 0:nt, 6, :], start=True, stop=False)
        nc.tensor.matmul(psum[:, 0, 0:nt * NE].rearrange("p (t e) -> p t e", e=NE), ones[:, :], pre[:, 0:nt, :], start=False, stop=True)
        nc.tensor.matmul(psum[:, 1, 0:NE], ones[:, :], tot[:, :], start=True, stop=True).then_inc(s_rtm, 1)
        pe.wait_ge(s_rtp, 2 * l + 2)
        for q in range(2):
            for t in range(nt):
                ins = nc.tensor.matmul(psum[:, 2, 0:NBT], lane1[:, q, t], blk1[:, q, t], start=(q + t == 0), stop=(q == 1 and t == nt - 1))
        ins.then_inc(s_rtm, 1)

    s_g, s_u, s_w2 = sem("s_g"), sem("s_u"), sem("s_w2")
    s_gup, s_upp = sem("s_gup"), sem("s_upp")
    s_xg, s_xtp, s_xta, s_xtd = sem("s_xg"), sem("s_xtp"), sem("s_xta"), sem("s_xtd")
    s_sil, s_hh, s_ht, s_hta, s_htd, s_yb, s_ya, s_yd, s_ys = [
        sem(n) for n in ("s_sil", "s_hh", "s_ht", "s_hta", "s_htd", "s_yb", "s_ya", "s_yd", "s_ys")]
    s_idx, s_xz, s_first = sem("s_idx"), sem("s_xz"), sem("s_first")
    A = Arena("moe")
    wg = A("wg", [P, 2, KD, DE])
    wu = A("wu", [P, 2, KD, DE])
    w2 = A("w2", [P, 2, DE // P, D])
    xl = A("xl", [P, D])
    xg = A("xg", [P, D])
    xT = A("xT", [P, KD, P])
    sg = A("sg", [P, DE])
    hh = A("hh", [P, DE])
    hT2 = A("hT2", [P, DE // P, P])
    yo = A("yo", [P, D])
    gidx = A("gidx", [P, 1], I32)
    sidx = A("sidx", [P, 1], I32)

    counts = {}

    def blocks(eng, l):
        n = eng.value_load(blkcount[0:1, l:l + 1], min_val=NB_MIN[l], max_val=NB_MAX[l])
        n = eng.snap(n, min_val=NB_MIN[l], max_val=NB_MAX[l])
        before = counts.get((eng, 0), 0)
        counts[eng, l] = n
        return before, n

    def moe_loop(eng, l, body, chain=None):
        before, n = blocks(eng, l)
        with eng.Fori(0, n) as b:
            body(b, before + b)
        return before + n

    def sp_moe(sp, l):
        if l == 0:
            for s in (s_g, s_u, s_w2):
                sp.sem_inc(s, 16)
        sp.wait_ge(s_first, l + 1)
        w13v = e_w13[l].rearrange("e (k p) f -> p e k f", p=P)
        w2v = e_w2[l].rearrange("e (k p) f -> p e k f", p=P)

        def body(b, B):
            e = sp.value_load(exptab[0:1, ds(b, 1)], min_val=0, max_val=NE - 1)
            par = b % 2
            settled(sp, s_g, 16 * B + 16)
            settled(sp, s_gup, B + 1)
            sp.dma_start(wg[:, ds(par, 1)].rearrange("p o k f -> p (o k) f"), w13v[:, ds(e, 1), :, 0:DE].rearrange("p o k f -> p (o k) f")).then_inc(s_g, 16)
            settled(sp, s_u, 16 * B + 16)
            settled(sp, s_upp, B + 1)
            sp.dma_start(wu[:, ds(par, 1)].rearrange("p o k f -> p (o k) f"), w13v[:, ds(e, 1), :, DE:].rearrange("p o k f -> p (o k) f")).then_inc(s_u, 16)
            settled(sp, s_w2, 16 * B + 16)
            settled(sp, s_yb, B + 1)
            sp.dma_start(w2[:, ds(par, 1)].rearrange("p o k f -> p (o k) f"), w2v[:, ds(e, 1), :, :].rearrange("p o k f -> p (o k) f")).then_inc(s_w2, 16)
        moe_loop(sp, l, body)

    def pool_moe(pool, l):
        nc.gpsimd.memset(xl[:, :], 0.0).then_inc(s_xz, 1)
        pool.wait_ge(s_xz, l + 1)
        if l == 0:
            pool.sem_inc(s_xtp, 1)
            pool.dma_start(xl[0:16, 0:P], consts[0:16, 0:P]).then_inc(s_ys, 16)
            pool.wait_ge(s_ys, 16)
        before = counts.get((pool, 0), 0)

        def gather(b, n_idx):
            nc.gpsimd.tensor_copy(gidx[:, :], toktab[:, ds(b, 1)]).then_inc(s_idx, 1)
            settled(pool, s_idx, n_idx + 1)
            pool.indirect_dma_start(xl[:, :], None, h2_d, bass.IndirectOffsetOnAxis(gidx[:, :], 0),
                                    bounds_check=NTOK - 1, oob_is_err=False).then_inc(s_xg, 16)

        def pass_on(n, first=False):
            settled(pool, s_xg, 16 * (n + l) + 16)
            if first:
                pool.sem_inc(s_first, 1)
            settled(pool, s_xtp, n + 1)
            nc.gpsimd.tensor_copy(xg[:, :], xl[:, :]).then_inc(s_xcopy, 1)
            settled(pool, s_xcopy, n + 1)

        gather(0, 2 * (before + l))
        pass_on(before + l, True)
        gather(1, 2 * (before + l) + 1)

        def body(b, B):
            pass_on(B + l + 1)
            gather(b + 2, 2 * (B + l) + 2)
            settled(pool, s_ys, 16 * B + 16)
            pool.sem_inc(s_yfree, 1)
            nc.gpsimd.tensor_copy(sidx[:, :], rowtab[:, ds(b, 1)]).then_inc(s_idx, 1)
            settled(pool, s_idx, 2 * (B + l) + 4)
            settled(pool, s_ya, B + 1)
            settled(pool, s_yd, B + 1)
            pool.indirect_dma_start(y_d, bass.IndirectOffsetOnAxis(sidx[:, :], 0), yo[:, :], None,
                                    bounds_check=2 * NTOK - 1, oob_is_err=False).then_inc(s_ys, 16)
        end = moe_loop(pool, l, body)
        settled(pool, s_ys, 16 * end + 16)
        settled(pool, s_xg, 16 * (end + 2 * (l + 1)))

    def pe_moe(pe, l):
        before = counts.get((pe, 0), 0)
        if l == 0:
            for s in (s_gup, s_upp, s_yb):
                pe.sem_inc(s, 2)

        def turn_x(half):
            for k in range(4 * half, 4 * half + 4):
                ins = nc.tensor.transpose(psum[:, 3 + half, (k % 4) * P:(k % 4 + 1) * P], xg[:, k * P:(k + 1) * P], ident)
            if half:
                ins.then_inc(s_xtp, 1)
        pe.wait_ge(s_xcopy, before + l + 1)
        turn_x(0)
        turn_x(1)

        def body(b, B):
            par = b % 2
            pe.wait_ge(s_xta, B + l + 1)
            pe.wait_ge(s_xtd, B + l + 1)
            pe.wait_ge(s_g, 16 * B + 32)
            for k in range(KD):
                ins = nc.tensor.matmul(psum[:, 0, :], xT[:, k, :], wg[:, ds(par, 1), k, :].rearrange("p o n -> p (o n)"), start=(k == 0), stop=(k == KD - 1))
            ins.then_inc(s_gup, 1)
            pe.wait_ge(s_u, 16 * B + 32)
            for h in range(2):
                for k in range(KD):
                    ins = nc.tensor.matmul(psum[:, 1 + h, 0:256], xT[:, k, :], wu[:, ds(par, 1), k, h * 256:(h + 1) * 256].rearrange("p o n -> p (o n)"),
                                           start=(k == 0), stop=(k == KD - 1))
                if h == 0:
                    ins.then_inc(s_uph, 1)
            ins.then_inc(s_upp, 1)
            pe.wait_ge(s_xcopy, B + l + 2)
            turn_x(0)
            for h in range(2):
                pe.wait_ge(s_hh, 2 * B + h + 1)
                for k in range(2):
                    ins = nc.tensor.transpose(psum[:, 5 if h == 0 else 1, k * P:(k + 1) * P], hh[:, (2 * h + k) * P:(2 * h + k + 1) * P], ident)
                ins.then_inc(s_ht, 1)
            turn_x(1)
            pe.wait_ge(s_w2, 16 * B + 32)
            for h in range(2):
                pe.wait_ge(s_htd if h == 0 else s_hta, B + 1)
                for n in range(2):
                    for k in (2 * h, 2 * h + 1):
                        ins = nc.tensor.matmul(psum[:, 6 + n, :], hT2[:, k, :], w2[:, ds(par, 1), k, n * HALF:(n + 1) * HALF].rearrange("p o n -> p (o n)"),
                                               start=(k == 0), stop=(k == 3))
            ins.then_inc(s_yb, 1)
        moe_loop(pe, l, body)

    s_uph, s_yfree, s_xcopy = sem("s_uph"), sem("s_yfree"), sem("s_xcopy")

    def act_moe(act, l):
        before = counts.get((act, 0), 0)

        def take_x(n):
            act.wait_ge(s_xtp, n)
            nc.scalar.activation(xT[:, 0:4, :], psum[:, 3, :].rearrange("p (b n) -> p b n", b=4), ACT.Copy).then_inc(s_xta, 1)
        take_x(before + l + 2)

        def body(b, B):
            act.wait_ge(s_gup, B + 3)
            nc.scalar.activation(sg[:, :], psum[:, 0, :], ACT.Silu).then_inc(s_sil, 1)
            act.wait_ge(s_ht, 2 * B + 2)
            nc.scalar.activation(hT2[:, 2:4, :], psum[:, 1, 0:256].rearrange("p (b n) -> p b n", b=2), ACT.Copy).then_inc(s_hta, 1)
            take_x(B + l + 3)
            act.wait_ge(s_yb, B + 3)
            act.wait_ge(s_yfree, B + 1)
            nc.scalar.activation(yo[:, HALF:], psum[:, 7, :], ACT.Copy).then_inc(s_ya, 1)
        moe_loop(act, l, body)

    def dve_moe(dve, l):
        before = counts.get((dve, 0), 0)

        def take_x(n):
            dve.wait_ge(s_xtp, n)
            nc.vector.tensor_copy(xT[:, 4:8, :], psum[:, 4, :].rearrange("p (b n) -> p b n", b=4)).then_inc(s_xtd, 1)
        take_x(before + l + 2)

        def body(b, B):
            dve.wait_ge(s_sil, B + 1)
            for h in range(2):
                if h == 0:
                    dve.wait_ge(s_uph, B + 1)
                else:
                    dve.wait_ge(s_upp, B + 3)
                nc.vector.tensor_tensor(hh[:, h * 256:(h + 1) * 256], psum[:, 1 + h, 0:256], sg[:, h * 256:(h + 1) * 256], ALU.mult).then_inc(s_hh, 1)
            dve.wait_ge(s_ht, 2 * B + 1)
            nc.vector.tensor_copy(hT2[:, 0:2, :], psum[:, 5, 0:256].rearrange("p (b n) -> p b n", b=2)).then_inc(s_htd, 1)
            take_x(B + l + 3)
            dve.wait_ge(s_yb, B + 3)
            dve.wait_ge(s_yfree, B + 1)
            nc.vector.tensor_copy(yo[:, 0:HALF], psum[:, 6, :]).then_inc(s_yd, 1)
        moe_loop(dve, l, body)

    s_fin = [sem(f"s_fin{n}") for n in range(4)]
    s_fx, s_fst, s_fg = sem("s_fx"), [sem(f"s_fst{n}") for n in range(4)], sem("s_fg")
    A = Arena("last")
    fx = A("x", [P, 4, D])
    fy = A("y", [P, 4, 2, D])
    fu = A("u", [P, 4, D])
    fg = A("g", [P, D])
    fw = A("w", [P, 2, 2])

    def sp_last(sp):
        for s in s_fst:
            sp.sem_inc(s, 16)

        def body(i):
            for n in range(4):
                t = 4 * i + n
                sp.wait_ge(s_fst[n], 16 * i + 16)
                sp.dma_start(fx[:, n], xs_d[ds(t * P, P), :]).then_inc(s_fin[n], 16)
                sp.dma_start(fy[:, n], y_d[ds(t * 2 * P, 2 * P), :].rearrange("(p c) n -> p c n", c=2)).then_inc(s_fin[n], 16)
        trips(sp, TX // 4, body)

    def dve_last(dve):
        dve.wait_ge(s_fg, 16)

        def body(i):
            for n in range(4):
                dve.wait_ge(s_fin[n], 32 * (i + 1))
                dve_combine(dve, 4 * i + n, fx[:, n], fy[:, n], fu[:, n], fw[:, n % 2], fg[:, :]).then_inc(s_fx, 1)
        trips(dve, TX // 4, body, dvec, 16)

    def act_last(act):
        act.dma_start(fg[:, :], mod_d[1, 0:1, 5 * D:].broadcast_to([P, D])).then_inc(s_fg, 16)

        def body(i):
            for n in range(4):
                t = 4 * i + n
                act.wait_ge(s_fx, t + 1)
                act.dma_start(out[0, ds(t * P, P), :], fu[:, n]).then_inc(s_fst[n], 16)
        trips(act, TX // 4, body)
        for n in range(4):
            act.wait_ge(s_fst[n], 16 + 16 * (TX // 4))

    with nc.Block() as block:
        @block.sync
        def _(sp):
            sp_setup(sp)
            phase_end(sp)
            for l in range(2):
                for part in (sp_prep, sp_qkv, sp_att, sp_post):
                    part(sp, l)
                    phase_end(sp)
                phase_end(sp)
                sp_moe(sp, l)
                phase_end(sp)
            sp_last(sp)

        @block.gpsimd
        def _(pool):
            phase_end(pool)
            for l in range(2):
                for part in (pool_prep, pool_qkv, pool_att, pool_post):
                    part(pool, l)
                    phase_end(pool)
                phase_end(pool)
                pool_moe(pool, l)
                phase_end(pool)

        @block.tensor
        def _(pe):
            pe_setup(pe)
            phase_end(pe)
            for l in range(2):
                for part in (pe_prep, pe_qkv, pe_att, pe_post, pe_route, pe_moe):
                    part(pe, l)
                    phase_end(pe)

        @block.vector
        def _(dve):
            dve_setup(dve)
            phase_end(dve)
            for l in range(2):
                for part in (dve_prep, dve_qkv, dve_att, dve_post, dve_route, dve_moe):
                    part(dve, l)
                    phase_end(dve)
            dve_last(dve)

        @block.scalar
        def _(act):
            act_setup(act)
            phase_end(act)
            for l in range(2):
                for part in (act_prep, act_qkv, act_att, act_post, act_route, act_moe):
                    part(act, l)
                    phase_end(act)
            act_last(act)


_INS = ["x", "c", "ctx", "c_ctx", "ada_w", "ada_b", "norm1_g", "norm2_g", "a_wqkv", "a_wo", "a_q_norm", "a_k_norm",
        "a_lambda_q1", "a_lambda_k1", "a_lambda_q2", "a_lambda_k2", "a_subln_g", "b_wqkv", "b_wo", "b_q_norm",
        "b_k_norm", "b_sink", "r_w1", "r_b1", "r_w2", "r_b2", "e_w13", "e_w2"]


def constants():
    import numpy as np
    t = np.zeros((P, C_END), np.float32)
    i = np.arange(P)
    t[:, C_ID:C_ID + P] = np.eye(P)
    t[:, C_TRI:C_TRI + P] = i[:, None] < i[None, :]
    t[:, C_IOTA:C_IOTA + P] = i[None, :]
    t[:, C_PREV:C_PREV + P] = np.where(i[None, :] >= i[:, None], 0, -BIG)
    t[:, C_NEXT:C_NEXT + P] = np.where(i[None, :] <= i[:, None], 0, -BIG)
    grid_w, freqs = 64, HD // 4
    pos = np.arange(SEQ)
    inv = np.float32(10000.0) ** (-np.arange(freqs, dtype=np.float32) / np.float32(freqs))
    ang = np.stack([(pos // grid_w).astype(np.float32)[:, None] * inv, (pos % grid_w).astype(np.float32)[:, None] * inv], 1)
    cos, sin = np.cos(ang), np.sin(ang)
    full_c = np.ones((NTOK, 2, 2, freqs), np.float32)
    full_s = np.zeros((NTOK, 2, 2, freqs), np.float32)
    full_c[:SEQ] = cos[:, :, None, :]
    full_s[:SEQ, :, 0] = -sin
    full_s[:SEQ, :, 1] = sin
    t[:, C_COS:C_COS + TA * HD] = full_c.reshape(TA, P, HD).transpose(1, 0, 2).reshape(P, TA * HD)
    t[:, C_SIN:C_SIN + TA * HD] = full_s.reshape(TA, P, HD).transpose(1, 0, 2).reshape(P, TA * HD)
    t[:, C_TOK:C_TOK + TA] = 2 * (np.arange(TA)[None, :] * P + i[:, None]) + 1
    return t


def kernel(**inputs):
    import numpy as np
    import concourse.bacc as bacc
    from concourse.bass_utils import run_bass_kernel_spmd

    nc = bacc.Bacc("TRN2", target_bir_lowering=False, num_devices=1)
    arrays, args = {}, []
    for name in _INS:
        a = np.ascontiguousarray(inputs[name])
        arrays["in_" + name] = a
        args.append(nc.dram_tensor("in_" + name, a.shape, mybir.dt.from_np(a.dtype), kind="ExternalInput").ap())
    table = constants()
    arrays["in_consts"] = table
    args.append(nc.dram_tensor("in_consts", table.shape, F32, kind="ExternalInput").ap())
    args.append(nc.dram_tensor("out", (1, SEQ, D), F32, kind="ExternalOutput").ap())
    build(nc, *args)
    r = run_bass_kernel_spmd(nc, [arrays], core_ids=[0])
    return r.results[0]["out"]
```
